# Optimizing a Trainium2 kernel written in Bass

```python
import math
import jax, jax.numpy as jnp
from jax import lax
import numpy as np

'''Hybrid decoder trunk: DEPTH layers of [RMSNorm -> one combined input projection split into four parallel
head groups (HGRN2 | RG-LRU | S5 | RWKV-7) -> concat -> one output projection] + [RMSNorm -> 4-head
cross-attention into 256 memory tokens] + [RMSNorm -> gated MLP with causal depthwise conv], final RMSNorm.
Inputs: x (BATCH, SEQ, D_MODEL), mem (BATCH, 256, D_MODEL), per-layer parameters stacked on a leading DEPTH axis.
Output: (BATCH, SEQ, D_MODEL).'''

D_MODEL = 1024
BATCH = 1
SEQ = 2048
DEPTH = 1

F32 = jnp.float32
EPS = 1e-6
N_MEM = 256
D_MIX = D_MODEL
D_A = D_MIX // 4
D_B = D_MIX // 4
D_C = D_MIX // 4
D_D = D_MIX - D_A - D_B - D_C
HG_HEADS = 4
HG_DK = D_A // HG_HEADS
HG_DV = D_A // HG_HEADS
HG_CHUNK = 64
LRU_BLOCKS = 4
LRU_BW = D_B // LRU_BLOCKS
LRU_CONV = 4
LRU_C = 8.0
S5_GROUP = 16
S5_GROUPS = D_C // S5_GROUP
S5_STATE = 64
RW_HEADS = 4
RW_HD = D_D // RW_HEADS
RW_DECAY_LORA = 32
RW_A_LORA = 32
RW_G_LORA = 64
RW_LN_EPS = 64e-5
P_D = 3 * D_D + RW_DECAY_LORA + RW_A_LORA + RW_G_LORA
XA_HEADS = 4
XA_HD = D_MODEL // XA_HEADS
D_FF = 2816
FFN_CONV = 3
IN_SIZES = (D_A, D_A, D_A, D_A, D_B, D_B, D_C, P_D)
P_IN = sum(IN_SIZES)
IN_SPLITS = tuple(int(v) for v in np.cumsum(IN_SIZES)[:-1])
RW_SPLITS = tuple(int(v) for v in np.cumsum((D_D, D_D, D_D, RW_DECAY_LORA, RW_A_LORA, RW_G_LORA))[:-1])

kernel_name = 'hymba_style_hgrn2_rglru_s5_rwkv7_hybrid'

def rmsnorm(x, g):
    xf = x.astype(F32)
    y = xf * lax.rsqrt(jnp.mean(xf * xf, axis=-1, keepdims=True) + EPS)
    return (y * g.astype(F32)).astype(x.dtype)

def causal_dwconv(x, w, b):
    k = w.shape[0]
    y = lax.conv_general_dilated(x, w[:, None, :].astype(x.dtype), (1,), [(k - 1, 0)],
                                 dimension_numbers=('NWC', 'WIO', 'NWC'),
                                 feature_group_count=x.shape[-1])
    return y + b.astype(x.dtype)

def token_shift(t):
    return jnp.pad(t, ((0, 0), (1, 0), (0, 0)))[:, :-1, :]

def linear_combine(left, right):
    return left[0] * right[0], right[0] * left[1] + right[1]

def hgrn2_mixer(q_in, f_in, i_in, g_in, lb, norm_g):
    bsz, s, _ = q_in.shape
    n = s // HG_CHUNK
    lbf = lb.astype(F32)
    zf = f_in.astype(F32)
    q = jax.nn.silu(q_in.astype(F32))
    log_f = jnp.logaddexp(jnp.log(lbf), jnp.log1p(-lbf) + jax.nn.log_sigmoid(zf))
    k = (1.0 - lbf) * jax.nn.sigmoid(-zf)
    v = i_in.astype(F32)

    def chunks(t):
        return t.reshape(bsz, n, HG_CHUNK, HG_HEADS, -1).transpose(1, 0, 3, 2, 4)

    causal = jnp.tril(jnp.ones((HG_CHUNK, HG_CHUNK), dtype=bool))[:, :, None]

    def step(state, inp):
        qc, kc, vc, gc = inp
        cum = jnp.cumsum(gc, axis=2)
        pair = jnp.exp(jnp.where(causal, cum[:, :, :, None, :] - cum[:, :, None, :, :], -jnp.inf))
        scores = jnp.einsum('bhtd,bhsd,bhtsd->bhts', qc, kc, pair)
        last = cum[:, :, -1:, :]
        out = (jnp.einsum('bhts,bhse->bhte', scores, vc)
               + jnp.einsum('bhtd,bhde->bhte', qc * jnp.exp(cum), state))
        state = (jnp.exp(last[:, :, 0, :, None]) * state
                 + jnp.einsum('bhsd,bhse->bhde', kc * jnp.exp(last - cum), vc))
        return state, out

    s0 = jnp.zeros((bsz, HG_HEADS, HG_DK, HG_DV), F32)
    _, o = lax.scan(step, s0, (chunks(q), chunks(k), chunks(v), chunks(log_f)))
    o = o.transpose(1, 0, 3, 2, 4).reshape(bsz, s, HG_HEADS, HG_DV)
    o = o * lax.rsqrt(jnp.mean(o * o, axis=-1, keepdims=True) + EPS)
    o = o.reshape(bsz, s, D_A) * norm_g.astype(F32) * jax.nn.silu(g_in.astype(F32))
    return o.astype(q_in.dtype)

def rglru_mixer(y_in, x_in, conv_w, conv_b, w_a, b_a, w_x, b_x, lam, norm_g):
    bsz, s, _ = x_in.shape
    xc = causal_dwconv(x_in, conv_w, conv_b).astype(F32).reshape(bsz, s, LRU_BLOCKS, LRU_BW)
    gate_r = jax.nn.sigmoid(jnp.einsum('bsgi,gij->bsgj', xc, w_a.astype(F32)) + b_a.astype(F32))
    gate_i = jax.nn.sigmoid(jnp.einsum('bsgi,gij->bsgj', xc, w_x.astype(F32)) + b_x.astype(F32))
    log_a = -LRU_C * gate_r * jax.nn.softplus(-lam.astype(F32))
    a = jnp.exp(log_a)
    u = jnp.sqrt(-jnp.expm1(2.0 * log_a)) * (gate_i * xc)
    _, hs = lax.associative_scan(linear_combine, (a, u), axis=1)
    out = hs.reshape(bsz, s, D_B) * jax.nn.gelu(y_in.astype(F32))
    return rmsnorm(out, norm_g).astype(y_in.dtype)

def s5_mixer(u, a_re, a_im, log_dt, b_re, b_im, c_re, c_im, d_skip, w_glu, b_glu, norm_g):
    bsz, s, _ = u.shape
    uf = u.astype(F32).reshape(bsz, s, S5_GROUPS, S5_GROUP)
    lam = lax.complex(a_re.astype(F32), a_im.astype(F32))
    dt = jnp.exp(log_dt.astype(F32))[:, None]
    a_bar = jnp.exp(lam * dt)
    b_bar = ((a_bar - 1.0) / lam)[:, :, None] * lax.complex(b_re.astype(F32), b_im.astype(F32))
    bu = jnp.einsum('gpc,bsgc->bsgp', b_bar, uf.astype(jnp.complex64))
    _, hs = lax.associative_scan(linear_combine, (jnp.broadcast_to(a_bar, bu.shape), bu), axis=1)
    c = lax.complex(c_re.astype(F32), c_im.astype(F32))
    y = jnp.einsum('gcp,bsgp->bsgc', c, hs).real + d_skip.astype(F32).reshape(S5_GROUPS, S5_GROUP) * uf
    y = jax.nn.gelu(y.reshape(bsz, s, D_C))
    out = y * jax.nn.sigmoid(y @ w_glu.astype(F32) + b_glu.astype(F32))
    return rmsnorm(out, norm_g).astype(u.dtype)

def rwkv7_mixer(zd, mu, w0, w_up, a0, a_up, g_up, k_k, k_a, r_k, ln_g, ln_b):
    bsz, s, _ = zd.shape
    zf = zd.astype(F32)
    zf = zf + mu.astype(F32) * (token_shift(zf) - zf)
    r, k, v, w_lat, a_lat, g_lat = jnp.split(zf, RW_SPLITS, axis=-1)
    w = w0.astype(F32) + jnp.tanh(w_lat) @ w_up.astype(F32)
    decay = jnp.exp(-jnp.exp(-jax.nn.softplus(-w) - 0.5))
    a = jax.nn.sigmoid(a0.astype(F32) + a_lat @ a_up.astype(F32))
    g = jax.nn.sigmoid(g_lat) @ g_up.astype(F32)

    def heads(t):
        return t.reshape(bsz, s, RW_HEADS, RW_HD)

    kk = heads(k * k_k.astype(F32))
    kk = kk / jnp.maximum(jnp.sqrt(jnp.sum(kk * kk, axis=-1, keepdims=True)), 1e-12)
    k = k * (1.0 + (a - 1.0) * k_a.astype(F32))
    r4, k4, v4, w4, a4 = heads(r), heads(k), heads(v), heads(decay), heads(a)

    def step(state, inp):
        rt, wt, kt, vt, kkt, at = inp
        sa = jnp.einsum('bhij,bhj->bhi', state, -kkt)
        state = (state * wt[:, :, None, :] + sa[..., None] * (kkt * at)[:, :, None, :]
                 + vt[..., None] * kt[:, :, None, :])
        return state, jnp.einsum('bhij,bhj->bhi', state, rt)

    def tm(t):
        return jnp.moveaxis(t, 1, 0)

    s0 = jnp.zeros((bsz, RW_HEADS, RW_HD, RW_HD), F32)
    _, y = lax.scan(step, s0, (tm(r4), tm(w4), tm(k4), tm(v4), tm(kk), tm(a4)))
    y = jnp.moveaxis(y, 0, 1)
    mean = jnp.mean(y, axis=-1, keepdims=True)
    var = jnp.mean(jnp.square(y - mean), axis=-1, keepdims=True)
    y = ((y - mean) * lax.rsqrt(var + RW_LN_EPS)).reshape(bsz, s, D_D) * ln_g.astype(F32) + ln_b.astype(F32)
    bonus = jnp.sum(r4 * k4 * r_k.astype(F32), axis=-1, keepdims=True) * v4
    y = (y + bonus.reshape(bsz, s, D_D)) * g
    return y.astype(zd.dtype)

def cross_attention(hn, mn, wq, wkv, wo):
    bsz, s, _ = hn.shape
    q = (hn @ wq).reshape(bsz, s, XA_HEADS, XA_HD)
    k, v = jnp.split(mn @ wkv, 2, axis=-1)
    k = k.reshape(bsz, -1, XA_HEADS, XA_HD)
    v = v.reshape(bsz, -1, XA_HEADS, XA_HD)
    scores = jnp.einsum('bshd,bmhd->bhsm', q, k).astype(F32) * (XA_HD ** -0.5)
    p = jax.nn.softmax(scores, axis=-1).astype(v.dtype)
    o = jnp.einsum('bhsm,bmhd->bshd', p, v).reshape(bsz, s, D_MODEL)
    return o @ wo

def conv_ffn(hn, w_up, conv_w, conv_b, w_down):
    u = causal_dwconv(hn @ w_up, conv_w, conv_b)
    gate, val = jnp.split(u, 2, axis=-1)
    return (jax.nn.silu(gate) * val) @ w_down

def setup_inputs(seed: int = 0) -> dict:
    key = jax.random.key(seed)
    keys = iter(jax.random.split(key, 64))

    def nrm(shape, scale):
        return scale * jax.random.normal(next(keys), shape, F32)

    def uni(shape, lo, hi):
        return jax.random.uniform(next(keys), shape, F32, lo, hi)

    def gain(shape):
        return 1.0 + nrm(shape, 0.02)

    L = DEPTH
    u_lru = uni((L, LRU_BLOCKS, LRU_BW), 0.9, 0.999)
    s_lru = u_lru ** (1.0 / LRU_C)
    n_idx = jnp.arange(S5_STATE, dtype=F32)
    return {
        'x': nrm((BATCH, SEQ, D_MODEL), 1.0),
        'mem': nrm((BATCH, N_MEM, D_MODEL), 1.0),
        'lb_param': nrm((L, D_A), 0.5),
        'mix_norm': gain((L, D_MODEL)),
        'w_in': nrm((L, D_MODEL, P_IN), D_MODEL ** -0.5),
        'w_out': nrm((L, D_MIX, D_MODEL), D_MIX ** -0.5),
        'hg_norm': gain((L, D_A)),
        'lru_conv_w': nrm((L, LRU_CONV, D_B), LRU_CONV ** -0.5),
        'lru_conv_b': nrm((L, D_B), 0.01),
        'lru_wa': nrm((L, LRU_BLOCKS, LRU_BW, LRU_BW), LRU_BW ** -0.5),
        'lru_ba': nrm((L, LRU_BLOCKS, LRU_BW), 0.01),
        'lru_wx': nrm((L, LRU_BLOCKS, LRU_BW, LRU_BW), LRU_BW ** -0.5),
        'lru_bx': nrm((L, LRU_BLOCKS, LRU_BW), 0.01),
        'lru_lam': jnp.log(s_lru) - jnp.log1p(-s_lru),
        'lru_norm': gain((L, D_B)),
        's5_a_re': -0.5 + nrm((L, S5_GROUPS, S5_STATE), 0.01),
        's5_a_im': math.pi * n_idx + nrm((L, S5_GROUPS, S5_STATE), 0.01),
        's5_log_dt': uni((L, S5_GROUPS), math.log(1e-3), math.log(1e-1)),
        's5_b_re': nrm((L, S5_GROUPS, S5_STATE, S5_GROUP), (2 * S5_GROUP) ** -0.5),
        's5_b_im': nrm((L, S5_GROUPS, S5_STATE, S5_GROUP), (2 * S5_GROUP) ** -0.5),
        's5_c_re': nrm((L, S5_GROUPS, S5_GROUP, S5_STATE), (2 * S5_STATE) ** -0.5),
        's5_c_im': nrm((L, S5_GROUPS, S5_GROUP, S5_STATE), (2 * S5_STATE) ** -0.5),
        's5_d': nrm((L, D_C), 1.0),
        's5_w_glu': nrm((L, D_C, D_C), D_C ** -0.5),
        's5_b_glu': nrm((L, D_C), 0.01),
        's5_norm': gain((L, D_C)),
        'rw_mu': uni((L, P_D), 0.0, 1.0),
        'rw_w0': uni((L, D_D), -6.0, -1.0),
        'rw_w_up': nrm((L, RW_DECAY_LORA, D_D), 0.1),
        'rw_a0': nrm((L, D_D), 0.1),
        'rw_a_up': nrm((L, RW_A_LORA, D_D), 0.1),
        'rw_g_up': nrm((L, RW_G_LORA, D_D), RW_G_LORA ** -0.5),
        'rw_k_k': 0.85 + nrm((L, D_D), 0.02),
        'rw_k_a': 1.0 + nrm((L, D_D), 0.02),
        'rw_r_k': nrm((L, RW_HEADS, RW_HD), 0.1),
        'rw_ln_g': gain((L, D_D)),
        'rw_ln_b': nrm((L, D_D), 0.01),
        'xa_norm': gain((L, D_MODEL)),
        'xa_mem_norm': gain((L, D_MODEL)),
        'xa_wq': nrm((L, D_MODEL, D_MODEL), D_MODEL ** -0.5),
        'xa_wkv': nrm((L, D_MODEL, 2 * D_MODEL), D_MODEL ** -0.5),
        'xa_wo': nrm((L, D_MODEL, D_MODEL), D_MODEL ** -0.5),
        'ffn_norm': gain((L, D_MODEL)),
        'ffn_w_up': nrm((L, D_MODEL, 2 * D_FF), D_MODEL ** -0.5),
        'ffn_conv_w': nrm((L, FFN_CONV, 2 * D_FF), FFN_CONV ** -0.5),
        'ffn_conv_b': nrm((L, 2 * D_FF), 0.01),
        'ffn_w_down': nrm((L, D_FF, D_MODEL), D_FF ** -0.5),
        'final_norm': gain((D_MODEL,)),
    }

def reference(x, mem, lb_param, mix_norm, w_in, w_out, hg_norm,
              lru_conv_w, lru_conv_b, lru_wa, lru_ba, lru_wx, lru_bx, lru_lam, lru_norm,
              s5_a_re, s5_a_im, s5_log_dt, s5_b_re, s5_b_im, s5_c_re, s5_c_im, s5_d, s5_w_glu, s5_b_glu, s5_norm,
              rw_mu, rw_w0, rw_w_up, rw_a0, rw_a_up, rw_g_up, rw_k_k, rw_k_a, rw_r_k, rw_ln_g, rw_ln_b,
              xa_norm, xa_mem_norm, xa_wq, xa_wkv, xa_wo,
              ffn_norm, ffn_w_up, ffn_conv_w, ffn_conv_b, ffn_w_down,
              final_norm):
    lb_all = jnp.cumsum(jax.nn.softmax(lb_param.astype(F32), axis=0), axis=0)
    lb_all = jnp.maximum(lb_all - lb_all[:1], 0.0)
    h = x
    for l in range(DEPTH):
        hn = rmsnorm(h, mix_norm[l])
        a_q, a_f, a_i, a_g, b_y, b_x, c_u, d_z = jnp.split(hn @ w_in[l], IN_SPLITS, axis=-1)
        y_a = hgrn2_mixer(a_q, a_f, a_i, a_g, lb_all[l], hg_norm[l])
        y_b = rglru_mixer(b_y, b_x, lru_conv_w[l], lru_conv_b[l], lru_wa[l], lru_ba[l],
                          lru_wx[l], lru_bx[l], lru_lam[l], lru_norm[l])
        y_c = s5_mixer(c_u, s5_a_re[l], s5_a_im[l], s5_log_dt[l], s5_b_re[l], s5_b_im[l],
                       s5_c_re[l], s5_c_im[l], s5_d[l], s5_w_glu[l], s5_b_glu[l], s5_norm[l])
        y_d = rwkv7_mixer(d_z, rw_mu[l], rw_w0[l], rw_w_up[l], rw_a0[l], rw_a_up[l], rw_g_up[l],
                          rw_k_k[l], rw_k_a[l], rw_r_k[l], rw_ln_g[l], rw_ln_b[l])
        h = h + jnp.concatenate([y_a, y_b, y_c, y_d], axis=-1) @ w_out[l]
        h = h + cross_attention(rmsnorm(h, xa_norm[l]), rmsnorm(mem, xa_mem_norm[l]),
                                xa_wq[l], xa_wkv[l], xa_wo[l])
        h = h + conv_ffn(rmsnorm(h, ffn_norm[l]), ffn_w_up[l], ffn_conv_w[l], ffn_conv_b[l], ffn_w_down[l])
    return rmsnorm(h, final_norm)


_drawn_inputs = setup_inputs


def setup_inputs(seed=0):
    import zlib

    import numpy as np

    out = dict(_drawn_inputs(seed))
    spreads = {}
    factors = {'mix_norm': 3.046,
     'hg_norm': 8.0,
     'lru_ba': 33.305,
     'lru_bx': 25.756,
     'lru_norm': 18.447,
     's5_a_re': 200.0,
     's5_b_re': 2.715,
     's5_b_im': 2.695,
     's5_c_re': 2.689,
     's5_b_glu': 22.248,
     's5_norm': 28.083,
     'rw_w_up': 8.0,
     'rw_a0': 7.176,
     'rw_k_k': 200.0,
     'rw_k_a': 8.0,
     'rw_ln_g': 35.681,
     'rw_ln_b': 58.361,
     'xa_norm': 8.0,
     'xa_mem_norm': 8.0,
     'ffn_norm': 13.814,
     'ffn_conv_b': 28.15,
     'final_norm': 24.447,
     's5_c_im': 3.512}
    for name, (base, spread) in spreads.items():
        noise = np.random.default_rng([zlib.crc32(name.encode()), seed]).standard_normal(out[name].shape)
        drawn = base * np.exp(spread * noise) if base else spread * noise
        out[name] = __import__('jax').numpy.asarray(drawn.astype(out[name].dtype))
    for name, factor in factors.items():
        out[name] = (out[name] * factor).astype(out[name].dtype)
    return out
```

```python
from contextlib import ExitStack

import concourse.bass as bass
import numpy as np
from concourse import mybir

F32 = mybir.dt.float32
I32 = mybir.dt.int32
ALU = mybir.AluOpType
ACT = mybir.ActivationFunctionType
AX_X = mybir.AxisListType.X

P = 128
SEQ, D_MODEL, N_MEM = 2048, 1024, 256
KT = D_MODEL // P
G2 = 2
TB = 512
NB = SEQ // TB
TC = 128
NCH = SEQ // TC
CB = TB // TC
EPS = 1e-6
RW_LN_EPS = 64e-5
LRU_C = 8.0
LRU_TAPS = 4
HD = 64
DECAY = -float(np.exp(-0.5))
LEVELS = (64, 32, 16, 8, 4, 2, 1)
XA_HEADS, XA_HD = 4, 256
D_FF = 2816
FF_T = D_FF // P

FEATURES = (("lat", 20), ("k", 16), ("k", 17), ("r", 14), ("r", 15), ("v", 18), ("v", 19), ("bx", 10), ("bx", 11),
            ("by", 8), ("by", 9), ("f", 2), ("f", 3), ("q", 0), ("q", 1), ("g", 6), ("g", 7))
NF = len(FEATURES)
Z_TILES = 7
SCAN = ("q", "k", "cum", "r", "kp", "kk", "b", "csig")
LATE = ("ag", "dg", "bonus", "yb", "yc")


class Signal:

    def __init__(self, sem, n=1, unit=1, seed=0):
        self.sem, self.n, self.unit, self.seed = sem, n, unit, seed

    def at(self, p, k=None, back=0):
        k = self.n if k is None else k + 1
        return self.sem, p * (self.n * self.unit) + ((self.seed - back) * self.n + k) * self.unit

    def seed_by(self, engine):
        engine.sem_inc(self.sem, self.seed * self.n * self.unit)


class Own:

    def __init__(self, engine, sem, p=0, n=0):
        self.engine, self.sem, self.p, self.n, self.k = engine, sem, p, n, 0

    def done(self, instruction, signal=None, k=0):
        if signal is None:
            instruction.then_inc(self.sem, 1)
            self.k += 1
            self.engine.wait_ge(self.sem, self.p * self.n + self.k)
        else:
            instruction.then_inc(signal.sem, 1)
            self.engine.wait_ge(*signal.at(self.p, k))

    def check(self):
        assert self.k == self.n, f"{self.k} instructions of its own in a pass, {self.n} were said"


def load_constants(nc, ctx, mixers, D):
    def sb(name, shape, dt=F32):
        return ctx.enter_context(nc.sbuf_tensor(name, shape, dt))

    def sem(name):
        return ctx.enter_context(nc.semaphore(name))

    n_prm = D["prm"].shape[1]
    prm = sb("prm_sb", [P, n_prm])
    cst = sb("cst", [P, 3 * P + TB])
    derived = sb("derived", [P, 8 * G2])
    masks = mixers.enter_context(nc.sbuf_tensor("masks_sb", [P, len(LEVELS) + 1 + 4, P], F32))
    lora = mixers.enter_context(nc.sbuf_tensor("lora_sb", [P, 6, P], F32))
    lru_w = mixers.enter_context(nc.sbuf_tensor("lru_w_sb", [P, 4, P], F32))
    C = {"prm": prm, "ident": cst[:, 0:P], "headones": cst[:, P:2 * P], "ones": cst[:, 2 * P:3 * P], "reset": cst[:, 3 * P:], "masks": masks,
         "pair_mask": masks[:, len(LEVELS) + 1:],
         "lora": lora, "lru_w": lru_w, "loaded": sem("constants_loaded"), "loaded_n": 5 * 16,
         "prepared": sem("constants_prepared")}
    where = D["prm_at"]

    def col(name, t=0):
        return prm[:, where[name] + t:where[name] + t + 1]

    def cols(name, n):
        return prm[:, where[name]:where[name] + n]

    def col_at(name, t):
        return prm[:, bass.ds(where[name] + t, 1)]

    C["col"], C["cols"], C["col_at"] = col, cols, col_at
    d = [derived[:, G2 * i:G2 * (i + 1)] for i in range(8)]
    C["log_a"], C["neg_log_a"], C["one_minus_lb"], C["lb"], C["one_minus_ka"], C["zero"] = d[0], d[1], d[2], d[3], d[4], d[7]
    own_a, own_v = sem("prep_act_own"), sem("prep_dve_own")
    with nc.Block() as block:
        @block.sync
        def _(sp):
            for dst, src in ((prm[:], D["prm"]), (cst[:], D["cst"]), (masks[:], D["masks"]), (lora[:], D["lora"]),
                             (lru_w[:], D["lru_w"])):
                sp.dma_start(dst, src).then_inc(C["loaded"], 16)

        @block.scalar
        def _(act):
            own = Own(act, own_a)
            act.wait_ge(C["loaded"], C["loaded_n"])
            own.done(act.activation(d[5], cols("lru_lam", G2), ACT.Abs))
            own.done(act.activation(d[5], d[5], ACT.Exp, scale=-1.0))
            own.done(act.activation(d[5], d[5], ACT.Ln, bias=1.0))

        @block.vector
        def _(dve):
            own = Own(dve, own_v)
            dve.wait_ge(C["loaded"], C["loaded_n"])
            own.done(dve.memset(d[7], 0.0))
            own.done(dve.tensor_scalar(d[6], cols("lru_lam", G2), -1.0, 0.0, ALU.mult, ALU.max))
            dve.wait_ge(own_a, 3)
            own.done(dve.tensor_tensor(d[6], d[6], d[5], ALU.add))
            own.done(dve.tensor_scalar(d[0], d[6], -LRU_C, None, ALU.mult))
            own.done(dve.tensor_scalar(d[1], d[6], LRU_C, None, ALU.mult))
            own.done(dve.tensor_tensor(d[3], cols("lb_param", G2), cols("lb_param", G2), ALU.subtract))
            own.done(dve.tensor_scalar(d[3], d[3], 0.0, None, ALU.max))
            own.done(dve.tensor_scalar(d[2], d[3], -1.0, 1.0, ALU.mult, ALU.add))
            own.done(dve.tensor_scalar(d[4], cols("rw_k_a", G2), -1.0, 1.0, ALU.mult, ALU.add))
            dve.memset(d[7], 0.0).then_inc(C["prepared"], 1)
    return C


def project_and_prepare(nc, ctx, D, C):
    with ExitStack() as mem:
        def sb(name, shape, dt=F32):
            return mem.enter_context(nc.sbuf_tensor(name, shape, dt))

        def bank(name, shape):
            return mem.enter_context(nc.psum_tensor(name, shape, F32))

        def sig(name, n=1, unit=1, seed=0):
            return Signal(nc.alloc_semaphore(name), n, unit, seed)

        WR = 4
        w_ring = sb("w_ring", [P, WR, KT, P])
        w_tok = sb("w_tok_sb", [P, KT, 2 * G2 * P])
        x_t = sb("x_t", [P, CB, D_MODEL])
        hn = sb("hn", [P, KT, TB])
        junk = sb("junk", [P, D_MODEL])
        mean_sq = sb("mean_sq", [P, CB])
        rstd = sb("rstd", [P, CB])
        z = sb("z", [P, Z_TILES, 1 + TB])
        z_last = sb("z_last", [P, 1])
        dz = sb("dz", [P, TB])
        bx = sb("bx", [P, G2, LRU_TAPS - 1 + TB])
        T = {n: sb("t_" + n, [P, G2, TB]) for n in (
            "by", "f", "q", "ag", "e", "cum", "k", "csig", "a", "kk", "b", "kp", "dg", "bonus", "sq", "inv",
            "xc", "gr", "gi", "h", "decay")}
        tok = sb("tok", [P, CB, 2 * G2 * P])
        v_tok = sb("v_tok", [P, CB, G2 * P])
        h_last = sb("h_last", [P, G2])
        turn = bank("turn", [P, 2, TB])
        proj = bank("proj", [P, 3, TB])
        aux_a = bank("aux_a", [P, 2, TB])
        aux_v = bank("aux_v", [P, TB])
        col, ident, headones, ones = C["col"], C["ident"], C["headones"], C["ones"]
        chunk_start = C["reset"]

        x_in, wtok_in = sig("x_in", 1, 16), sig("wtok_in", 1, 16)
        w_in = [sig(f"w_in{s}", len(range(s, NF, WR)), 16) for s in range(WR)]
        sumsq, ms_ready, root, xn_ready = sig("sumsq"), sig("ms_ready"), sig("root"), sig("xn_ready")
        turned, hn_ready = sig("turned", KT, 1, 1), sig("hn_ready", KT)
        proj_done, proj_out = sig("proj_done", NF + CB, 1, 1), sig("proj_out", NF + CB, 1, 1)
        aux_done, aux_out = sig("aux_done", 10), sig("aux_out", 10, 1, 1)
        vaux_done, vaux_out = sig("vaux_done", 7, 1, 1), sig("vaux_out", 7, 1, 1)
        z_mixed, lat_act, k_sq, ss_root, rk_ready = (sig("z_mixed", Z_TILES), sig("lat_act"), sig("k_sq", G2),
                                                     sig("ss_root", G2), sig("rk_ready", G2))
        conv_done, a_ready, th_ready, om_ready, om_root = (sig("conv_done", 1, 1, 1), sig("a_ready", G2),
                                                           sig("th_ready", G2), sig("om_ready", G2), sig("om_root", G2))
        lf_done, csig_done = sig("lf_done"), sig("csig_done", G2)
        f_clamped, f_log, lb_log = sig("f_clamped"), sig("f_log"), sig("lb_log")
        out_b, out_b_sq, b_root = sig("out_b"), sig("out_b_sq"), sig("b_root")
        dve_end, act_end = sig("dve_end", 1, 1, 1), sig("act_end", 1, 1, 1)
        stored = sig("stored", (len(SCAN) + 4) * G2 + 3, 16, 1)
        dve_own, act_own = sig("s1_dve_own").sem, sig("s1_act_own").sem
        block = mem.enter_context(nc.Block())

        @block.sync
        def _(sp):
            stored.seed_by(sp)
            sp.dma_start(w_tok[:], D["w_tok"]).then_inc(wtok_in.sem, 16)
            with nc.sync.Fori(0, NB) as p:
                sp.wait_ge(*turned.at(p, back=1))
                sp.dma_start(x_t[:], D["x"][bass.ds(p * TB, TB)].rearrange("(j p) n -> p j n", p=P)).then_inc(x_in.sem, 16)
                for n in range(NF):
                    sp.wait_ge(*(proj_done.at(p, n - WR) if n >= WR else proj_done.at(p, NF - 1, back=1)))
                    sp.dma_start(w_ring[:, n % WR], D["w_feat"][n]).then_inc(w_in[n % WR].sem, 16)
                sp.wait_ge(*dve_end.at(p))
                sp.wait_ge(*act_end.at(p))
                scan = {"q": T["q"][:], "k": T["k"][:], "cum": T["cum"][:], "r": z[:, 3:5, 1:], "kp": T["kp"][:],
                        "kk": T["kk"][:], "b": T["b"][:], "csig": T["csig"][:]}
                late = {"ag": T["ag"][:], "dg": T["dg"][:], "bonus": T["bonus"][:], "yb": T["h"][:]}
                for part, given in (("scan", scan), ("late", late)):
                    for a, name in enumerate(given):
                        for t in range(G2):
                            out = D[part][bass.ds(p * CB, CB), :, a, t].rearrange("c p n -> p c n")
                            sp.dma_start(out, given[name][:, t].rearrange("p (c n) -> p c n", c=CB)).then_inc(stored.sem, 16)
                for name, src in (("va", tok[:, :, 0:G2 * P]), ("cu", tok[:, :, G2 * P:]), ("vd", v_tok[:])):
                    sp.dma_start(D[name][bass.ds(p * CB, CB)].rearrange("c p n -> p c n"), src).then_inc(stored.sem, 16)
            sp.wait_ge(*stored.at(NB - 1))

        @block.tensor
        def _(pe):
            for s in (turned, proj_done, vaux_done):
                s.seed_by(pe)
            pe.wait_ge(C["loaded"], C["loaded_n"])
            pe.wait_ge(*wtok_in.at(0))
            with nc.tensor.Fori(0, NB) as p:
                pe.wait_ge(*xn_ready.at(p))
                for k in range(KT):
                    if k >= 2:
                        pe.wait_ge(*hn_ready.at(p, k - 2))
                    for j in range(CB):
                        mm = pe.transpose(turn[:, k % 2, j * P:(j + 1) * P], x_t[:, j, k * P:(k + 1) * P], ident)
                    mm.then_inc(turned.sem, 1)

                def for_act(m, lhs, rhs):
                    pe.wait_ge(*(aux_out.at(p, m - 2) if m >= 2 else aux_out.at(p, m + 8, back=1)))
                    pe.matmul(aux_a[:, m % 2], lhs, rhs, start=True, stop=True).then_inc(aux_done.sem, 1)

                def dve_bank_free(m):
                    pe.wait_ge(*(vaux_out.at(p, m - 1) if m else vaux_out.at(p, back=1)))

                def small_products(n):
                    if n == 6:
                        pe.wait_ge(*lat_act.at(p))
                        for m in range(6):
                            for_act(m, C["lora"][:, m], z[:, 0, 1:])
                    if n == 8:
                        for t in range(G2):
                            pe.wait_ge(*k_sq.at(p, t))
                            dve_bank_free(t)
                            pe.matmul(aux_v[:], headones, T["sq"][:, t], start=True, stop=True).then_inc(vaux_done.sem, 1)
                    if n == 10:
                        pe.wait_ge(*conv_done.at(p))
                        for m in range(4):
                            for_act(6 + m, C["lru_w"][:, m], T["xc"][:, m % 2])
                    if n == 12:
                        for t in range(G2):
                            pe.wait_ge(*rk_ready.at(p, t))
                            dve_bank_free(2 + t)
                            pe.matmul(aux_v[:], headones, T["sq"][:, t], start=True, stop=True).then_inc(vaux_done.sem, 1)
                    if n == 14:
                        for t in range(G2):
                            dve_bank_free(4 + t)
                            for j in range(CB):
                                mm = pe.transpose(aux_v[:, j * P:(j + 1) * P], z[:, 5 + t, 1 + j * P:1 + (j + 1) * P], ident)
                            mm.then_inc(vaux_done.sem, 1)

                for n in range(NF + CB):
                    pe.wait_ge(*(proj_out.at(p, n - 3) if n >= 3 else proj_out.at(p, NF + CB - 3 + n, back=1)))
                    if n < NF:
                        pe.wait_ge(*w_in[n % WR].at(p, n // WR))
                    for k in range(KT):
                        if n == 0:
                            pe.wait_ge(*hn_ready.at(p, k))
                        if n < NF:
                            lhs, rhs = w_ring[:, n % WR, k], hn[:, k]
                        else:
                            lhs, rhs = hn[:, k, (n - NF) * P:(n - NF + 1) * P], w_tok[:, k]
                        mm = pe.matmul(proj[:, n % 3], lhs, rhs, start=k == 0, stop=k == KT - 1)
                    mm.then_inc(proj_done.sem, 1)
                    small_products(n)
                pe.wait_ge(*out_b_sq.at(p))
                dve_bank_free(6)
                for t in range(G2):
                    mm = pe.matmul(aux_v[:], ones, T["sq"][:, t], start=t == 0, stop=t == G2 - 1)
                mm.then_inc(vaux_done.sem, 1)

        @block.scalar
        def _(act):
            for s in (proj_out, aux_out, act_end):
                s.seed_by(act)
            act.wait_ge(C["prepared"], 1)
            with nc.scalar.Fori(0, NB) as p:
                own = Own(act, act_own, p, 17)
                act.wait_ge(*x_in.at(p))
                for j in range(CB):
                    own.done(act.activation(junk[:], x_t[:, j], ACT.Square, accum_out=mean_sq[:, j:j + 1]),
                             *((sumsq,) if j == CB - 1 else ()))
                act.wait_ge(*ms_ready.at(p))
                own.done(act.activation(rstd[:], mean_sq[:], ACT.Sqrt), root)
                act.wait_ge(*stored.at(p, back=1))
                act.wait_ge(*dve_end.at(p, back=1))
                act.wait_ge(*vaux_done.at(p, back=1))

                def take(n, dst, func=ACT.Copy):
                    act.wait_ge(*proj_done.at(p, n))
                    own.done(act.activation(dst, proj[:, n % 3], func), proj_out, n)

                def take_small(m, dst, func, bias=0.0):
                    act.wait_ge(*aux_done.at(p, m))
                    own.done(act.activation(dst, aux_a[:, m % 2], func, bias=bias), aux_out, m)

                for n in range(Z_TILES):
                    take(n, z[:, n, 1:])
                    if n == 3:
                        act.wait_ge(*z_mixed.at(p, 0))
                        own.done(act.activation(z[0:32, 0, 1:], z[0:32, 0, 1:], ACT.Tanh))
                        own.done(act.activation(z[64:128, 0, 1:], z[64:128, 0, 1:], ACT.Sigmoid), lat_act)
                for t in range(G2):
                    take_small(t, T["decay"][:, t], ACT.Sigmoid, col("rw_w0", t))
                for t in range(G2):
                    take_small(2 + t, T["a"][:, t], ACT.Sigmoid, col("rw_a0", t))
                for t in range(G2):
                    take_small(4 + t, T["dg"][:, t], ACT.Copy)
                for t in range(G2):
                    take(7 + t, bx[:, t, LRU_TAPS - 1:])
                for t in range(G2):
                    act.wait_ge(*z_mixed.at(p, 1 + t))
                    own.done(act.activation(T["sq"][:, t], z[:, 1 + t, 1:], ACT.Square, scale=col("rw_k_k", t)), k_sq, t)
                for t in range(G2):
                    take(9 + t, T["by"][:, t], ACT.Gelu_apprx_tanh)
                for t in range(G2):
                    act.wait_ge(*vaux_out.at(p, t))
                    own.done(act.activation(T["inv"][:, t], T["inv"][:, t], ACT.Sqrt), ss_root, t)
                for m in range(2 * G2):
                    take_small(6 + m, T["gr" if m < G2 else "gi"][:, m % G2], ACT.Sigmoid,
                               col("lru_ba" if m < G2 else "lru_bx", m % G2))
                for t in range(G2):
                    take(11 + t, T["f"][:, t])
                for t in range(G2):
                    own.done(act.activation(T["k"][:, t], T["f"][:, t], ACT.Sigmoid, scale=-1.0))
                    own.done(act.activation(T["k"][:, t], T["k"][:, t], ACT.Copy, scale=C["one_minus_lb"][:, t:t + 1]))
                act.wait_ge(*f_clamped.at(p))
                for t in range(G2):
                    own.done(act.activation(T["e"][:, t], T["f"][:, t], ACT.Abs))
                    own.done(act.activation(T["e"][:, t], T["e"][:, t], ACT.Exp, scale=-1.0))
                    own.done(act.activation(T["e"][:, t], T["e"][:, t], ACT.Ln, bias=1.0), *((f_log,) if t else ()))
                for t in range(G2):
                    own.done(act.activation(T["ag"][:, t], T["ag"][:, t], ACT.Exp, scale=-1.0))
                    own.done(act.activation(T["ag"][:, t], T["ag"][:, t], ACT.Ln, bias=1.0, scale=C["lb"][:, t:t + 1]),
                             *((lb_log,) if t else ()))
                for t in range(G2):
                    act.wait_ge(*csig_done.at(p, t))
                    own.done(act.activation(T["decay"][:, t], T["gr"][:, t], ACT.Exp, scale=C["log_a"][:, t:t + 1]),
                             a_ready, t)
                for t in range(G2):
                    own.done(act.activation(T["gr"][:, t], T["gr"][:, t], ACT.Tanh, scale=C["neg_log_a"][:, t:t + 1]),
                             th_ready, t)
                for t in range(G2):
                    take(13 + t, T["q"][:, t], ACT.Silu)
                act.wait_ge(*lf_done.at(p))
                for t in range(G2):
                    take(15 + t, T["ag"][:, t], ACT.Silu)
                for j in range(CB):
                    take(NF + j, tok[:, j])
                for t in range(G2):
                    act.wait_ge(*om_ready.at(p, t))
                    own.done(act.activation(T["gr"][:, t], T["gr"][:, t], ACT.Sqrt), om_root, t)
                act.wait_ge(*out_b.at(p))
                for t in range(G2):
                    own.done(act.activation(T["sq"][:, t], T["h"][:, t], ACT.Square), *((out_b_sq,) if t else ()))
                act.wait_ge(*vaux_out.at(p, 6))
                own.done(act.activation(T["inv"][:, 0], T["inv"][:, 0], ACT.Sqrt), b_root)
                own.done(act.activation(junk[:, 0:1], junk[:, 0:1], ACT.Copy), act_end)
                own.check()

        @block.vector
        def _(dve):
            for s in (vaux_out, conv_done, dve_end):
                s.seed_by(dve)
            dve.wait_ge(C["prepared"], 1)
            start = Own(dve, sig("s1_dve_start").sem)
            start.done(dve.memset(z[:, :, 0:1], 0.0))
            start.done(dve.memset(bx[:, :, 0:LRU_TAPS - 1], 0.0))
            start.done(dve.memset(h_last[:], 0.0))
            with nc.vector.Fori(0, NB) as p:
                own = Own(dve, dve_own, p, 64)
                dve.wait_ge(*sumsq.at(p))
                own.done(dve.tensor_scalar(mean_sq[:], mean_sq[:], 1.0 / D_MODEL, EPS, ALU.mult, ALU.add), ms_ready)
                dve.wait_ge(*root.at(p))
                own.done(dve.reciprocal(rstd[:], rstd[:]))
                for j in range(CB):
                    own.done(dve.tensor_scalar(x_t[:, j], x_t[:, j], rstd[:, j:j + 1], None, ALU.mult),
                             *((xn_ready,) if j == CB - 1 else ()))
                dve.wait_ge(*proj_done.at(p, back=1))
                for k in range(KT):
                    dve.wait_ge(*turned.at(p, k))
                    own.done(dve.tensor_scalar(hn[:, k], turn[:, k % 2], col("mix_norm", k), None, ALU.mult), hn_ready, k)
                dve.wait_ge(*stored.at(p, back=1))
                for n in range(Z_TILES):
                    dve.wait_ge(*proj_out.at(p, n))
                    own.done(dve.tensor_copy(z_last[:], z[:, n, TB:]))
                    own.done(dve.tensor_tensor(dz[:], z[:, n, 0:TB], z[:, n, 1:], ALU.subtract))
                    own.done(dve.tensor_copy(z[:, n, 0:1], z_last[:]))
                    own.done(dve.scalar_tensor_tensor(z[:, n, 1:], dz[:], col("rw_mu", n), z[:, n, 1:], ALU.mult, ALU.add),
                             z_mixed, n)
                for t in range(G2):
                    dve.wait_ge(*proj_out.at(p, 7 + t))
                    xc = T["xc"][:, t]
                    last = LRU_TAPS - 1
                    own.done(dve.tensor_scalar(xc, bx[:, t, last:last + TB], col(f"lru_conv_w{last}", t), col("lru_conv_b", t),
                                               ALU.mult, ALU.add))
                    for tap in range(last):
                        own.done(dve.scalar_tensor_tensor(xc, bx[:, t, tap:tap + TB], col(f"lru_conv_w{tap}", t), xc,
                                                          ALU.mult, ALU.add))
                own.done(dve.tensor_copy(bx[:, :, 0:LRU_TAPS - 1], bx[:, :, TB:]), conv_done)
                for t in range(G2):
                    dve.wait_ge(*aux_out.at(p, t))
                    own.done(dve.tensor_tensor_scan(T["csig"][:, t], chunk_start, T["decay"][:, t], 0.0, ALU.mult, ALU.add),
                             csig_done, t)
                for t in range(G2):
                    dve.wait_ge(*vaux_done.at(p, t))
                    own.done(dve.tensor_scalar(T["inv"][:, t], aux_v[:], 1e-24, None, ALU.max), vaux_out, t)
                for t in range(G2):
                    k = z[:, 1 + t, 1:]
                    dve.wait_ge(*ss_root.at(p, t))
                    own.done(dve.reciprocal(T["inv"][:, t], T["inv"][:, t]))
                    own.done(dve.scalar_tensor_tensor(T["kk"][:, t], k, col("rw_k_k", t), T["inv"][:, t], ALU.mult, ALU.mult))
                    dve.wait_ge(*aux_out.at(p, 2 + t))
                    own.done(dve.tensor_tensor(T["b"][:, t], T["kk"][:, t], T["a"][:, t], ALU.mult))
                    own.done(dve.tensor_scalar(T["a"][:, t], T["a"][:, t], col("rw_k_a", t), C["one_minus_ka"][:, t:t + 1],
                                               ALU.mult, ALU.add))
                    own.done(dve.tensor_tensor(T["kp"][:, t], k, T["a"][:, t], ALU.mult))
                    own.done(dve.scalar_tensor_tensor(T["sq"][:, t], z[:, 3 + t, 1:], col("rw_r_k", t), T["kp"][:, t],
                                                      ALU.mult, ALU.mult), rk_ready, t)
                for t in range(G2):
                    dve.wait_ge(*proj_out.at(p, 11 + t))
                    own.done(dve.tensor_scalar(T["ag"][:, t], T["f"][:, t], -40.0, None, ALU.max),
                             *((f_clamped,) if t else ()))
                for t in range(G2):
                    dve.wait_ge(*vaux_done.at(p, 2 + t))
                    own.done(dve.tensor_tensor(T["bonus"][:, t], z[:, 5 + t, 1:], aux_v[:], ALU.mult), vaux_out, 2 + t)
                dve.wait_ge(*f_log.at(p))
                for t in range(G2):
                    own.done(dve.scalar_tensor_tensor(T["e"][:, t], T["f"][:, t], 0.0, T["e"][:, t], ALU.min, ALU.subtract))
                dve.wait_ge(*lb_log.at(p))
                for t in range(G2):
                    own.done(dve.tensor_tensor(T["e"][:, t], T["e"][:, t], T["ag"][:, t], ALU.add),
                             *((lf_done,) if t else ()))
                for t in range(G2):
                    own.done(dve.tensor_tensor_scan(T["cum"][:, t], chunk_start, T["e"][:, t], 0.0, ALU.mult, ALU.add))
                for t in range(G2):
                    dve.wait_ge(*th_ready.at(p, t))
                    own.done(dve.tensor_tensor(T["inv"][:, t], T["decay"][:, t], T["decay"][:, t], ALU.mult))
                    own.done(dve.scalar_tensor_tensor(T["gr"][:, t], T["inv"][:, t], 1.0, T["gr"][:, t], ALU.add, ALU.mult),
                             om_ready, t)
                    own.done(dve.tensor_tensor(T["xc"][:, t], T["xc"][:, t], T["gi"][:, t], ALU.mult))
                for t in range(G2):
                    dve.wait_ge(*vaux_done.at(p, 4 + t))
                    own.done(dve.tensor_copy(v_tok[:, :, t * P:(t + 1) * P], aux_v[:].rearrange("p (j n) -> p j n", j=CB)),
                             vaux_out, 4 + t)
                for t in range(G2):
                    dve.wait_ge(*om_root.at(p, t))
                    own.done(dve.tensor_tensor(T["xc"][:, t], T["xc"][:, t], T["gr"][:, t], ALU.mult))
                    own.done(dve.tensor_tensor_scan(T["h"][:, t], T["decay"][:, t], T["xc"][:, t], h_last[:, t:t + 1],
                                                    ALU.mult, ALU.add))
                    own.done(dve.tensor_copy(h_last[:, t:t + 1], T["h"][:, t, TB - 1:TB]))
                    own.done(dve.tensor_tensor(T["h"][:, t], T["h"][:, t], T["by"][:, t], ALU.mult),
                             *((out_b,) if t else ()))
                for t in range(G2):
                    dve.wait_ge(*proj_out.at(p, 15 + t))
                    own.done(dve.tensor_scalar(T["ag"][:, t], T["ag"][:, t], col("hg_norm", t), None, ALU.mult))
                dve.wait_ge(*vaux_done.at(p, 6))
                own.done(dve.tensor_scalar(T["inv"][:, 0], aux_v[:], 1.0 / (G2 * P), EPS, ALU.mult, ALU.add), vaux_out, 6)
                dve.wait_ge(*b_root.at(p))
                own.done(dve.reciprocal(T["inv"][:, 0], T["inv"][:, 0]))
                for t in range(G2):
                    own.done(dve.scalar_tensor_tensor(T["h"][:, t], T["h"][:, t], col("lru_norm", t), T["inv"][:, 0],
                                                      ALU.mult, ALU.mult), *((dve_end,) if t else ()))
                own.check()


def scan_chunks(nc, ctx, D, C):
    with ExitStack() as mem:
        def sb(name, shape, dt=F32):
            return mem.enter_context(nc.sbuf_tensor(name, shape, dt))

        def bank(name, shape):
            return mem.enter_context(nc.psum_tensor(name, shape, F32))

        def sig(name, n=1, unit=1, seed=0):
            return Signal(nc.alloc_semaphore(name), n, unit, seed)

        H = G2 * 2
        NL = len(LEVELS)
        MID = TC // 2 - 1
        feats = [sb(f"feats{u}", [P, len(SCAN) - 1, G2, TC]) for u in range(2)]
        cs = [sb(f"cs{u}", [P, G2, 1 + TC]) for u in range(2)]
        va = [sb(f"va{u}", [P, G2 * P]) for u in range(2)]
        vd = [sb(f"vd{u}", [P, G2 * P]) for u in range(2)]
        halves = [sb(f"halves{u}", [P, NL, G2, TC]) for u in range(2)]
        e_from = [sb(f"e_from{u}", [P, G2, 1 + TC]) for u in range(2)]
        e_to = [sb(f"e_to{u}", [P, G2, TC]) for u in range(2)]
        kr = [sb(f"kr{u}", [P, G2, 2, TC]) for u in range(2)]
        bk = [sb(f"bk{u}", [P, 2, G2, TC]) for u in range(2)]
        qc = [sb(f"qc{u}", [P, G2, TC]) for u in range(2)]
        kc = [sb(f"kc{u}", [P, G2, TC]) for u in range(2)]
        small = [sb(f"small{u}", [P, 6, G2]) for u in range(2)]
        scores_d = sb("scores_d", [P, H, 4, TC])
        scores_a = sb("scores_a", [P, 2, G2, TC])
        off = sb("off", [P, NL, H, TC])
        invs = sb("invs", [P, 2, 2, 2, TC])
        w = sb("w", [P, H, TC])
        bk_tok = sb("bk_tok", [P, 2, G2, TC])
        kc_tok = sb("kc_tok", [P, G2, TC])
        rhs = sb("rhs", [P, G2 * P])
        sa = sb("sa", [P, G2 * P])
        state_a = sb("state_a", [P, G2, P])
        state_d = sb("state_d", [P, G2, P])
        state_mid = sb("state_mid", [P, G2, P])
        grown = sb("grown", [P, G2, P])
        grown_a = sb("grown_a", [P, G2, P])
        oy = [sb(f"oy{u}", [P, 2, G2, TC]) for u in range(2)]
        ps_a = bank("ps_a", [P, 2, 2, G2, TC])
        ps_d = bank("ps_d", [P, H, 4 * TC])
        ps_s = bank("ps_s", [P, 4 * TC])
        ps_o = bank("ps_o", [P, 4 * TC])
        ps_y, ps_x = (ps_d[:, 0], ps_d[:, 1]), (ps_d[:, 2], ps_d[:, 3])

        def inv(h):
            return invs[:, h // 2, 0, h % 2]

        def inv_t(h):
            return invs[:, h // 2, 1, h % 2]

        ident, headones, masks = C["ident"], C["headones"], C["masks"]
        Q, K, CUM, R, KP, KK, B = range(len(SCAN) - 1)

        loaded = [sig(f"loaded{u}", 4, 16) for u in range(2)]
        mids, small_exp, exp_d, kr_ready = (sig(n) for n in ("mids", "small_exp", "exp_d", "kr_ready"))
        exponents, exp_a, halves_ready, exp_qk, qk_ready = (sig(n) for n in (
            "exponents", "exp_a", "halves_ready", "exp_qk", "qk_ready"))
        pe_done = sig("pe_done", 1, 1, 2)
        pairs_d, scored_d = sig("pairs_d", 2), sig("scored_d", 2)
        bk_turned, bk_out, kc_turned, kc_out = (sig(n) for n in ("bk_turned", "bk_out", "kc_turned", "kc_out"))
        off_ready, first_inv, inv_turned, inv_out = sig("off_ready", NL), sig("first_inv"), sig("inv_turned"), sig("inv_out")
        NS = 2 * (NL - 1)
        y_done, w_ready, x_done, x_out = sig("y_done", NS), sig("w_ready", NS), sig("x_done", NS), sig("x_out", NS, 1, 1)
        pairs_a, scored_a = sig("pairs_a", 4), sig("scored_a", 4, 1, 1)
        mid_ready, states = sig("mid_ready"), sig("states", 1, 1, 1)
        rhs_done, rhs_ready, sa_done, sa_ready, ds_done = (sig(n) for n in (
            "rhs_done", "rhs_ready", "sa_done", "sa_ready", "ds_done"))
        oy_out = sig("oy_out", 1, 1, 1)
        stored = [sig(f"oy_stored{u}", 1, 16, 1) for u in range(2)]
        own = {n: sig("s2_own_" + n).sem for n in ("act", "act_prep", "dve", "dve_prep", "pool", "pool_prep", "start", "hold")}
        block = mem.enter_context(nc.Block())

        def chunks(fori, prepare, run):
            prepare(0, 0, 0)
            with fori(0, NCH // 2 - 1) as i:
                run(2 * i, i, 0, (2 * i + 1, i, 1))
                run(2 * i + 1, i, 1, (2 * i + 2, i + 1, 0))
            i = NCH // 2 - 1
            run(2 * i, i, 0, (2 * i + 1, i, 1))
            run(2 * i + 1, i, 1, None)

        @block.sync
        def _(sp):
            for s in stored:
                s.seed_by(sp)

            def load(p, i, u):
                sp.wait_ge(*pe_done.at(p, back=2))
                at = bass.ds(p, 1)
                for dst, src in ((feats[u][:], D["scan"][at, :, 0:len(SCAN) - 1]), (cs[u][:, :, 1:], D["scan"][at, :, len(SCAN) - 1]),
                                 (va[u][:], D["va"][at]), (vd[u][:], D["vd"][at])):
                    names = " ".join("bcd"[:len(src.shape) - 2])
                    sp.dma_start(dst, src.rearrange(f"a p {names} -> (a p) {names}")).then_inc(loaded[u].sem, 16)

            def run(p, i, u, following):
                if following:
                    load(*following)
                sp.wait_ge(*oy_out.at(p))
                sp.dma_start(D["oy"][bass.ds(p, 1)].rearrange("a p k t n -> (a p) k t n"), oy[u][:]).then_inc(stored[u].sem, 16)

            chunks(nc.sync.Fori, load, run)
            for s in stored:
                sp.wait_ge(*s.at(NCH // 2 - 1))

        @block.gpsimd
        def _(pool):
            def prepare(p, i, u):
                me = Own(pool, own["pool_prep"], p, 0)
                pool.wait_ge(*loaded[u].at(i))
                pool.wait_ge(*pe_done.at(p, back=2))
                q, k, cum = feats[u][:, Q], feats[u][:, K], feats[u][:, CUM]

                def sides(x, b):
                    x = x.rearrange("p t (g h b) -> p t g h b", h=2, b=b)
                    return x[:, :, :, 0], x[:, :, :, 1]

                for m, b in enumerate(LEVELS):
                    (c0, c1), (x0, x1) = sides(cum, b), sides(halves[u][:, m], b)
                    middle = c0[:, :, :, b - 1:b].broadcast_to([P, G2, TC // (2 * b), b])
                    pool.tensor_tensor(x0, middle, c0, ALU.subtract)
                    last = pool.tensor_tensor(x1, c1, middle, ALU.subtract)
                last.then_inc(exponents.sem, 1)
                pool.wait_ge(*exp_a.at(p))
                for m, b in enumerate(LEVELS):
                    (k0, _), (_, q1), (x0, x1) = sides(k, b), sides(q, b), sides(halves[u][:, m], b)
                    pool.tensor_tensor(x0, x0, k0, ALU.mult)
                    last = pool.tensor_tensor(x1, x1, q1, ALU.mult)
                me.done(last, halves_ready)

            def run(p, i, u, following):
                pool.wait_ge(*scored_d.at(p, 1))
                for m in range(NL):
                    mask = masks[:, NL - 1 - m:NL - m].broadcast_to([P, H, TC])
                    pool.tensor_tensor(off[:, m], scores_d[:, :, 0], mask, ALU.mult).then_inc(off_ready.sem, 1)
                if following:
                    prepare(*following)

            pool.wait_ge(C["loaded"], C["loaded_n"])
            chunks(nc.gpsimd.Fori, prepare, run)

        @block.scalar
        def _(act):
            act.wait_ge(C["prepared"], 1)

            def prepare_d(p, i, u):
                me = Own(act, own["act_prep"], p, 0)
                act.wait_ge(*mids.at(p))
                s = small[u]
                for t in range(G2):
                    act.activation(e_from[u][:, t], cs[u][:, t], ACT.Exp, bias=s[:, 0, t:t + 1], scale=DECAY)
                    act.activation(e_to[u][:, t], cs[u][:, t, 1:], ACT.Exp, bias=s[:, 1, t:t + 1], scale=-DECAY)
                act.activation(s[:, 3], s[:, 1], ACT.Exp)
                act.activation(s[:, 4], s[:, 2], ACT.Exp, scale=DECAY).then_inc(exp_d.sem, 1)
                return me

            def prepare_a(p, i, u):
                cum = feats[u][:, CUM]
                act.wait_ge(*pe_done.at(p, back=2))
                act.activation(qc[u][:], cum, ACT.Exp)
                for t in range(G2):
                    act.activation(kc[u][:, t], cum[:, t], ACT.Exp, bias=cum[:, t, TC - 1:TC], scale=-1.0)
                act.activation(small[u][:, 5], cum[:, :, TC - 1], ACT.Exp).then_inc(exp_qk.sem, 1)
                act.wait_ge(*exponents.at(p))
                act.activation(halves[u][:], halves[u][:], ACT.Exp).then_inc(exp_a.sem, 1)

            def prepare(p, i, u):
                act.wait_ge(*loaded[u].at(i))
                prepare_d(p, i, u)
                prepare_a(p, i, u)

            def run(p, i, u, following):
                act.wait_ge(*bk_turned.at(p))
                act.activation(bk_tok[:].rearrange("p a t n -> p (a t n)"), ps_s[:], ACT.Copy).then_inc(bk_out.sem, 1)
                act.wait_ge(*kc_turned.at(p))
                act.activation(kc_tok[:].rearrange("p t n -> p (t n)"), ps_o[:, 0:G2 * TC], ACT.Copy).then_inc(kc_out.sem, 1)
                act.wait_ge(*inv_turned.at(p))
                for g in range(2):
                    last = act.activation(invs[:, g, 0].rearrange("p h n -> p (h n)"), ps_x[g][:, 0:2 * TC], ACT.Copy)
                last.then_inc(inv_out.sem, 1)
                for s in range(NS):
                    g = s % 2
                    first = 0 if s < NS - 2 else 1
                    act.wait_ge(*x_done.at(p, s))
                    act.activation(invs[:, g, first:].rearrange("p a h n -> p (a h n)"), ps_x[g][:, 2 * TC * first:],
                                   ACT.Copy).then_inc(x_out.sem, 1)
                    if s == 1 and following:
                        act.wait_ge(*loaded[following[2]].at(following[1]))
                        prepare_d(*following)
                    if s == 5 and following:
                        prepare_a(*following)
                act.wait_ge(*rhs_done.at(p))
                act.activation(rhs[:], ps_s[:, 0:G2 * P], ACT.Copy, scale=-1.0).then_inc(rhs_ready.sem, 1)
                act.wait_ge(*sa_done.at(p))
                act.activation(sa[:], ps_s[:, G2 * P:], ACT.Copy).then_inc(sa_ready.sem, 1)
                act.wait_ge(*pe_done.at(p))
                act.wait_ge(*stored[u].at(i, back=1))
                act.activation(oy[u][:].rearrange("p k t n -> p (k t n)"), ps_o[:], ACT.Copy).then_inc(oy_out.sem, 1)

            oy_out.seed_by(act)
            x_out.seed_by(act)
            chunks(nc.scalar.Fori, prepare, run)

        @block.vector
        def _(dve):
            start = Own(dve, own["start"])
            dve.wait_ge(C["prepared"], 1)
            for x in (state_a[:], state_d[:], scores_a[:], scores_d[:], cs[0][:, :, 0:1], cs[1][:, :, 0:1]):
                last = dve.memset(x, 0.0)
            start.done(last)
            scored_a.seed_by(dve)
            states.seed_by(dve)

            def hold(sem, value):
                dve.wait_ge(sem, value)
                dve.sem_inc(own["hold"], 1)

            def prepare_mid(p, i, u):
                dve.wait_ge(*loaded[u].at(i))
                dve.wait_ge(*pe_done.at(p, back=2))
                mid, s = cs[u][:, :, 1 + MID], small[u]
                dve.tensor_scalar(s[:, 0], mid, -DECAY, None, ALU.mult)
                dve.tensor_scalar(s[:, 1], mid, DECAY, None, ALU.mult)
                dve.tensor_tensor(s[:, 2], cs[u][:, :, TC], mid, ALU.subtract).then_inc(mids.sem, 1)

            def prepare_rest(p, i, u):
                f = feats[u]
                dve.wait_ge(*exp_d.at(p))
                dve.tensor_tensor(kr[u][:, :, 0], f[:, KK], e_from[u][:, :, 0:TC], ALU.mult)
                dve.tensor_tensor(kr[u][:, :, 1], f[:, R], e_from[u][:, :, 1:], ALU.mult)
                dve.tensor_tensor(bk[u][:, 0], f[:, B], e_to[u][:], ALU.mult)
                dve.tensor_tensor(bk[u][:, 1], f[:, KP], e_to[u][:], ALU.mult).then_inc(kr_ready.sem, 1)
                dve.wait_ge(*exp_qk.at(p))
                dve.tensor_tensor(qc[u][:], qc[u][:], f[:, Q], ALU.mult)
                dve.tensor_tensor(kc[u][:], kc[u][:], f[:, K], ALU.mult).then_inc(qk_ready.sem, 1)

            def prepare(p, i, u):
                prepare_mid(p, i, u)
                prepare_rest(p, i, u)

            def run(p, i, u, following):
                me = Own(dve, own["dve"], p, 5)
                s = small[u]
                dve.wait_ge(*states.at(p, back=1))
                dve.wait_ge(*pe_done.at(p, back=1))
                for t in range(G2):
                    last = dve.tensor_scalar(state_mid[:, t], state_d[:, t], s[:, 3, t:t + 1], None, ALU.mult)
                last.then_inc(mid_ready.sem, 1)
                dve.wait_ge(C["loaded"], C["loaded_n"])
                mask = C["pair_mask"][:].rearrange("p m n -> p (m n)").bitcast(I32)
                for g in range(2):
                    hold(*pairs_d.at(p, g))
                    for h in (2 * g, 2 * g + 1):
                        last = dve.copy_predicated(scores_d[:, h].rearrange("p m n -> p (m n)"), mask, ps_d[:, h])
                    last.then_inc(scored_d.sem, 1)
                dve.wait_ge(*off_ready.at(p, 0))
                eye = ident.rearrange("p (a n) -> p a n", a=1).broadcast_to([P, 2, TC])
                for g in range(2):
                    last = dve.tensor_tensor(invs[:, g, 1], eye, off[:, 0, 2 * g:2 * g + 2], ALU.subtract)
                last.then_inc(first_inv.sem, 1)
                for n in range(NS):
                    g = n % 2
                    dve.wait_ge(*y_done.at(p, n))
                    dve.tensor_tensor(w[:, 2 * g:2 * g + 2], eye, ps_y[g][:, 0:2 * TC].rearrange("p (h n) -> p h n", h=2),
                                      ALU.subtract).then_inc(w_ready.sem, 1)
                    if g == 1 and n // 2 < 4:
                        pick_pairs(me, p, n // 2)
                    if n == 1 and following:
                        prepare_mid(*following)
                    if n == 7 and following:
                        prepare_rest(*following)
                dve.wait_ge(*ds_done.at(p))
                for t in range(G2):
                    dve.scalar_tensor_tensor(grown[:, t], ps_s[:, t * P:(t + 1) * P], s[:, 4, t:t + 1], headones, ALU.mult,
                                             ALU.mult)
                me.done(dve.tensor_tensor(grown_a[:], ps_s[:, G2 * P:].rearrange("p (t n) -> p t n", t=G2),
                                          headones.rearrange("p (a n) -> p a n", a=1).broadcast_to([P, G2, P]), ALU.mult))
                for t in range(G2):
                    dve.scalar_tensor_tensor(state_d[:, t], state_mid[:, t], s[:, 4, t:t + 1], grown[:, t], ALU.mult, ALU.add)
                    last = dve.scalar_tensor_tensor(state_a[:, t], state_a[:, t], s[:, 5, t:t + 1], grown_a[:, t], ALU.mult,
                                                    ALU.add)
                last.then_inc(states.sem, 1)
                me.check()

            def pick_pairs(me, p, r):
                hold(*pairs_a.at(p, r))
                for j in range(2):
                    mask = masks[:, 2 * r + j:2 * r + j + 1].bitcast(I32)
                    for q in range(2):
                        last = dve.copy_predicated(scores_a[:, q], mask.broadcast_to([P, G2, TC]), ps_a[:, q, j])
                    if j == 0:
                        last.then_inc(me.sem, 1)
                        me.k += 1
                        hold(me.sem, p * me.n + me.k)
                last.then_inc(scored_a.sem, 1)

            chunks(nc.vector.Fori, prepare, run)

        @block.tensor
        def _(pe):
            pe.wait_ge(C["loaded"], C["loaded_n"])
            pe_done.seed_by(pe)

            def rows(q):
                return slice(q * HD, (q + 1) * HD)

            def head(h):
                return slice(h * HD, (h + 1) * HD)

            def run(p, i, u, _):
                f = feats[u]
                pe.wait_ge(*kr_ready.at(p))
                pe.wait_ge(*states.at(p, back=1))
                pe.wait_ge(*oy_out.at(p, back=1))
                pe.wait_ge(*x_out.at(p, back=1))
                for h in range(H):
                    t, q = h // 2, h % 2
                    for m in range(2):
                        mm = pe.matmul(ps_d[:, h, 2 * m * TC:(2 * m + 2) * TC], bk[u][rows(q), m, t],
                                       kr[u][rows(q), t].rearrange("p a n -> p (a n)"), start=True, stop=True)
                    if q == 1:
                        mm.then_inc(pairs_d.sem, 1)
                pe.wait_ge(*qk_ready.at(p))
                for t in range(G2):
                    mm = pe.transpose(ps_o[:, t * TC:(t + 1) * TC], kc[u][:, t], ident)
                mm.then_inc(kc_turned.sem, 1)
                for m in range(2):
                    for t in range(G2):
                        mm = pe.transpose(ps_s[:, (2 * m + t) * TC:(2 * m + t + 1) * TC], bk[u][:, m, t], ident)
                mm.then_inc(bk_turned.sem, 1)

                def pairs(r):
                    if r == 0:
                        pe.wait_ge(*halves_ready.at(p))
                    pe.wait_ge(*(scored_a.at(p, r - 1) if r else scored_a.at(p, back=1)))
                    for j in range(2):
                        m = 2 * r + j
                        for t in range(G2):
                            for q in range(2):
                                x = halves[u][rows(q), m, t] if m < NL else None
                                lhs, rhs_ = (x, x) if m < NL else (f[rows(q), K, t], f[rows(q), Q, t])
                                mm = pe.matmul(ps_a[:, q, j, t], lhs, rhs_, start=True, stop=True)
                    mm.then_inc(pairs_a.sem, 1)

                pe.wait_ge(*first_inv.at(p))
                for h in range(H):
                    mm = pe.transpose(ps_x[h // 2][:, h % 2 * TC:(h % 2 + 1) * TC], inv_t(h), ident)
                mm.then_inc(inv_turned.sem, 1)
                for level in range(NL - 1):
                    pe.wait_ge(*off_ready.at(p, level + 1))
                    for g in range(2):
                        if level == 0:
                            pe.wait_ge(*inv_out.at(p))
                        else:
                            pe.wait_ge(*x_out.at(p, 2 * (level - 1) + g))
                        for h in (2 * g, 2 * g + 1):
                            mm = pe.matmul(ps_y[g][:, h % 2 * TC:(h % 2 + 1) * TC], off[:, level + 1, h], inv(h), start=True,
                                           stop=True)
                        mm.then_inc(y_done.sem, 1)
                    if level < 4:
                        pairs(level)
                    for g in range(2):
                        pe.wait_ge(*w_ready.at(p, 2 * level + g))
                        for h in (2 * g, 2 * g + 1):
                            at = slice(h % 2 * TC, (h % 2 + 1) * TC)
                            if level < NL - 2:
                                pe.matmul(ps_x[g][:, 0:2 * TC][:, at], inv_t(h), w[:, h], start=True, stop=True)
                            mm = pe.matmul(ps_x[g][:, 2 * TC:][:, at], w[:, h], inv_t(h), start=True, stop=True)
                        mm.then_inc(x_done.sem, 1)
                pe.wait_ge(*bk_out.at(p))
                pe.wait_ge(*mid_ready.at(p))
                for t in range(G2):
                    at = slice(t * P, (t + 1) * P)
                    pe.matmul(ps_s[:, at], kr[u][:, t, 0], state_mid[:, t], start=True, stop=False)
                    for h in (2 * t, 2 * t + 1):
                        mm = pe.matmul(ps_s[:, head(h)], scores_d[:, h, 2], vd[u][:, head(h)], start=False, stop=h % 2 == 1)
                mm.then_inc(rhs_done.sem, 1)
                pe.wait_ge(*scored_a.at(p, 3))
                pe.wait_ge(*kc_out.at(p))
                for t in range(G2):
                    at = slice(t * TC, (t + 1) * TC)
                    pe.matmul(ps_o[:, at], state_a[:, t], qc[u][:, t], start=True, stop=False)
                    for q in range(2):
                        pe.matmul(ps_o[rows(q), at], va[u][:, head(2 * t + q)], scores_a[:, q, t], start=False, stop=True)
                pe.wait_ge(*rhs_ready.at(p))
                pe.wait_ge(*x_out.at(p, NS - 1))
                for h in range(H):
                    mm = pe.matmul(ps_s[:, G2 * P + h * HD:G2 * P + (h + 1) * HD], inv_t(h), rhs[:, head(h)], start=True,
                                   stop=True)
                mm.then_inc(sa_done.sem, 1)
                pe.wait_ge(*sa_ready.at(p))
                for t in range(G2):
                    at = slice(t * P, (t + 1) * P)
                    pe.matmul(ps_s[:, at], bk_tok[:, 0, t], sa[:, at], start=True, stop=False)
                    pe.matmul(ps_s[:, at], bk_tok[:, 1, t], vd[u][:, at], start=False, stop=True)
                for t in range(G2):
                    at = slice(t * P, (t + 1) * P)
                    mm = pe.matmul(ps_s[:, G2 * P + t * P:G2 * P + (t + 1) * P], kc_tok[:, t], va[u][:, at], start=True, stop=True)
                mm.then_inc(ds_done.sem, 1)
                for t in range(G2):
                    at = slice((G2 + t) * TC, (G2 + t + 1) * TC)
                    pe.matmul(ps_o[:, at], state_mid[:, t], kr[u][:, t, 1], start=True, stop=False)
                    for q in range(2):
                        h = 2 * t + q
                        pe.matmul(ps_o[rows(q), at], sa[:, head(h)], scores_d[:, h, 1], start=False, stop=False)
                        mm = pe.matmul(ps_o[rows(q), at], vd[u][:, head(h)], scores_d[:, h, 3], start=False, stop=True)
                mm.then_inc(pe_done.sem, 1)

            chunks(nc.tensor.Fori, lambda p, i, u: None, run)


def state_space(nc, ctx, D, C):
    with ExitStack() as mem:
        def sb(name, shape, dt=F32):
            return mem.enter_context(nc.sbuf_tensor(name, shape, dt))

        def sig(name, n=1, unit=1, seed=0):
            return Signal(nc.alloc_semaphore(name), n, unit, seed)

        NG, NP, GC = 16, 64, 16
        L = P // GC
        NS = SEQ // L
        HALF = NS // 2
        STEPS = NS.bit_length() - 1
        NBANK = 8
        raw = sb("s5_raw", [P, 3, NG])
        b_in, c_in = sb("b_in", [P, 2, NG, GC]), sb("c_in", [P, 2, NG, GC])
        d_skip = sb("d_skip", [P, NG])
        sign = sb("sign", [P, 2])
        corner = sb("corner", [P, P])
        w_glu = sb("w_glu", [P, G2, G2, P])
        v = [sb(f"s5_v{n}", [P, NG]) for n in range(8)]
        re, im = sb("pow_re", [P, L + 1, NG]), sb("pow_im", [P, L + 1, NG])
        sre, sim = sb("sgn_re", [P, L + 1, NG]), sb("sgn_im", [P, L + 1, NG])
        simb = sb("sgn_imb", [P, L + 1, NG])
        mr, mi = sb("step_re", [P, 2, NG]), sb("step_im", [P, 2, NG])
        coef = sb("coef", [P, 2, NG, 2])
        b_bar = sb("b_bar", [P, 2, NG, GC])
        b_pad = sb("b_pad", [P, NG, 2 * L - 1, GC])
        w_p = sb("w_p", [P, NG, L, GC])
        c_pad = sb("c_pad", [P, NG, 2 * L, GC])
        tmp = sb("s5_tmp", [P, NG, GC])
        w_in = sb("s5_w_in", [P, NG, P])
        taps = sb("taps", [P, NG, P])
        step = [sb(f"step{u}", [P, NG, P]) for u in range(2)]
        u_sub = sb("u_sub", [P, 2, L * NG * GC])
        u_g = sb("u_g", [P, NG, NS])
        h = sb("s5_h", [P, NG, 1 + NS])
        yt = sb("yt", [P, G2, SEQ])
        gate = sb("gate", [P, G2, SEQ])
        y_sub = u_sub[:].rearrange("p h (t c) -> p h t c", t=L)
        sq = u_g[:].rearrange("p g n -> p (g n)").rearrange("p (t n) -> p t n", t=G2)
        inv = sb("s5_inv", [P, SEQ])
        ps = mem.enter_context(nc.psum_tensor("s5_ps", [P, NBANK, TB], F32))
        ident, ones, col = C["ident"], C["ones"], C["col"]

        loaded, u_in = sig("s5_loaded", 7, 16), sig("u_in", 1, 16)
        decay_arg, dt_done, root_arg, powers1 = sig("decay_arg"), sig("dt_done"), sig("angle"), sig("sines")
        weights, c_ready = sig("s5_weights"), sig("c_ready")
        u_turned, u_out = sig("u_turned", NBANK), sig("u_out", NBANK)
        t_done, t_out = sig("taps_done", 4), sig("taps_out", 4)
        wt_done, wt_out = sig("wt_done", 4), sig("wt_out", 4)
        v_done, v_out = sig("v_done", NBANK), sig("v_out", NBANK)
        m_ready, l_done, l_out = sig("m_ready", STEPS), sig("l_done", STEPS * NBANK), sig("l_out", STEPS * NBANK)
        y_done, y_out = sig("y_done5", NBANK), sig("y_out5", NBANK)
        yt_done, yt_out = sig("yt_done", NBANK), sig("yt_out", NBANK)
        glu_done, glu_out = sig("glu_done", NBANK), sig("glu_out", NBANK)
        o_ready, sq_ready = sig("o_ready", NBANK), sig("sq_ready", NBANK)
        n_done, n_out, n_root, yc_ready = sig("n_done", NB), sig("n_out", NB), sig("n_root", NB), sig("yc_ready", NB)
        stored = sig("yc_stored", NB * G2, 16)
        u_grouped = sig("u_grouped")
        own_v, own_a = sig("s5_dve_own").sem, sig("s5_act_own").sem
        block = mem.enter_context(nc.Block())

        @block.sync
        def _(sp):
            for dst, src in ((raw, "s5_raw"), (b_in, "s5_b"), (c_in, "s5_c"), (d_skip, "s5_d"), (sign, "s5_sign"),
                             (corner, "s5_corner"), (w_glu, "s5_glu")):
                sp.dma_start(dst[:], D[src]).then_inc(loaded.sem, 16)
            src = D["cu"].rearrange("c n x -> (c n x)").rearrange("(h s m) -> s h m", h=2, s=HALF)
            sp.dma_start(u_sub[:], src).then_inc(u_in.sem, 16)
            for b in range(NB):
                sp.wait_ge(*yc_ready.at(0, b))
                for t in range(G2):
                    sp.dma_start(D["late"][b * CB:(b + 1) * CB, :, len(LATE) - 1, t].rearrange("c p n -> p c n"),
                                 yt[:, t, b * TB:(b + 1) * TB].rearrange("p (c n) -> p c n", c=CB)).then_inc(stored.sem, 16)
            sp.wait_ge(*stored.at(0))

        @block.scalar
        def _(act):
            me = Own(act, own_a)
            act.wait_ge(*loaded.at(0))
            me.done(act.activation(v[0][:], raw[:, 2], ACT.Exp), dt_done)
            act.wait_ge(*decay_arg.at(0))
            me.done(act.activation(v[1][:], v[1][:], ACT.Exp))
            act.wait_ge(*root_arg.at(0))
            me.done(act.activation(v[3][:], v[2][:], ACT.Sin))
            me.done(act.activation(v[4][:], v[2][:], ACT.Sin, scale=0.5), powers1)
            for n in range(NBANK):
                act.wait_ge(*u_turned.at(0, n))
                act.activation(u_g[:, 2 * n:2 * n + 2].rearrange("p g n -> p (g n)"), ps[:, n], ACT.Copy).then_inc(u_out.sem, 1)
            for n in range(4):
                act.wait_ge(*wt_done.at(0, n))
                act.activation(w_in[:, 4 * n:4 * n + 4].rearrange("p g n -> p (g n)"), ps[:, 4 + n], ACT.Copy).then_inc(wt_out.sem, 1)
            for n in range(NBANK):
                act.wait_ge(*v_done.at(0, n))
                act.activation(h[:, 2 * n:2 * n + 2, 1:], ps[:, n].rearrange("p (g n) -> p g n", g=2), ACT.Copy).then_inc(v_out.sem, 1)
            for n in range(NBANK):
                half, g = n // 4, n % 4 * 4
                act.wait_ge(*y_done.at(0, n))
                act.activation(y_sub[:, half, :, g * GC:(g + 4) * GC].rearrange("p t (g c) -> p g t c", g=4),
                               ps[:, n].rearrange("p (g t c) -> p g t c", g=4, t=L), ACT.Gelu_apprx_tanh).then_inc(y_out.sem, 1)
            for n in range(NBANK):
                t, b = n // NB, n % NB
                act.wait_ge(*glu_done.at(0, n))
                act.activation(gate[:, t, b * TB:(b + 1) * TB], ps[:, n], ACT.Sigmoid, bias=col("s5_b_glu", t)).then_inc(glu_out.sem, 1)
            for b in range(NB):
                for t in range(G2):
                    act.wait_ge(*o_ready.at(0, t * NB + b))
                    act.activation(sq[:, t, b * TB:(b + 1) * TB], yt[:, t, b * TB:(b + 1) * TB], ACT.Square).then_inc(sq_ready.sem, 1)
            for b in range(NB):
                act.wait_ge(*n_out.at(0, b))
                act.activation(inv[:, b * TB:(b + 1) * TB], inv[:, b * TB:(b + 1) * TB], ACT.Sqrt).then_inc(n_root.sem, 1)

        @block.vector
        def _(dve):
            me = Own(dve, own_v)
            tt, ts, stt = dve.tensor_tensor, dve.tensor_scalar, dve.scalar_tensor_tensor
            ADD, SUB, MUL = ALU.add, ALU.subtract, ALU.mult
            for x in (b_pad[:], c_pad[:], h[:, :, 0:1], re[:, 0], im[:, 0]):
                last = dve.memset(x, 0.0)
            me.done(last)
            me.done(dve.memset(re[:, 0], 1.0))
            dve.wait_ge(*loaded.at(0))
            lr, li = raw[:, 0], raw[:, 1]
            dve.wait_ge(*dt_done.at(0))
            me.done(tt(v[1][:], lr, v[0][:], MUL), decay_arg)
            me.done(tt(v[2][:], li, v[0][:], MUL))
            me.done(ts(v[5][:], v[2][:], float(1 / (2 * np.pi)), 12582912.0, MUL, ADD))
            me.done(ts(v[5][:], v[5][:], -12582912.0, None, ADD))
            me.done(stt(v[2][:], v[5][:], -6.28125, v[2][:], MUL, ADD))
            me.done(stt(v[2][:], v[5][:], -float(2 * np.pi - 6.28125), v[2][:], MUL, ADD))
            me.done(ts(v[2][:], v[2][:], 3.1415925, -3.1415925, ALU.min, ALU.max), root_arg)
            dve.wait_ge(*powers1.at(0))
            me.done(tt(v[4][:], v[4][:], v[4][:], MUL))
            me.done(ts(v[4][:], v[4][:], -2.0, 1.0, MUL, ADD))
            me.done(tt(re[:, 1], v[4][:], v[1][:], MUL))
            me.done(tt(im[:, 1], v[3][:], v[1][:], MUL))

            def times(out_re, out_im, x_re, x_im, y_re, y_im):
                tt(v[5][:], x_im, y_im, MUL)
                tt(v[6][:], x_im, y_re, MUL)
                tt(v[7][:], x_re, y_im, MUL)
                me.done(tt(v[4][:], x_re, y_re, MUL))
                tt(out_re, v[4][:], v[5][:], SUB)
                me.done(tt(out_im, v[6][:], v[7][:], ADD))

            for n in range(1, L):
                times(re[:, n + 1], im[:, n + 1], re[:, n], im[:, n], re[:, 1], im[:, 1])
            me.done(ts(v[0][:], re[:, 1], -1.0, None, ADD))
            tt(v[1][:], lr, lr, MUL)
            me.done(tt(v[2][:], li, li, MUL))
            me.done(tt(v[1][:], v[1][:], v[2][:], ADD))
            me.done(dve.reciprocal(v[1][:], v[1][:]))
            me.done(ts(v[3][:], li, -1.0, None, MUL))
            times(v[2][:], v[0][:], v[0][:], im[:, 1], lr, v[3][:])
            me.done(tt(v[2][:], v[2][:], v[1][:], MUL))
            me.done(tt(v[0][:], v[0][:], v[1][:], MUL))
            me.done(ts(v[0][:], v[0][:], sign[:, 0:1], None, MUL))
            ts(sre[:], re[:], sign[:, 1:2], None, MUL)
            ts(simb[:], im[:], sign[:, 0:1], None, MUL)
            me.done(ts(sim[:], im[:], -1.0, None, MUL))

            def wide(x):
                return x.rearrange("p (g c) -> p g c", c=1).broadcast_to([P, NG, GC])

            for n in range(2):
                me.done(tt(tmp[:], b_in[:, 1 - n], wide(v[0][:]), MUL))
                me.done(tt(b_bar[:, n], b_in[:, n], wide(v[2][:]), MUL))
                me.done(tt(b_bar[:, n], b_bar[:, n], tmp[:], SUB if n else ADD))
            me.done(dve.tensor_copy(b_pad[:, :, L - 1], b_bar[:, 0]))
            for n in range(L + 1):
                me.done(tt(tmp[:], c_in[:, 1], wide(sim[:, n]), MUL))
                me.done(tt(c_pad[:, :, L - 1 + n], c_in[:, 0], wide(sre[:, n]), MUL))
                me.done(tt(c_pad[:, :, L - 1 + n], c_pad[:, :, L - 1 + n], tmp[:], ADD), *((c_ready,) if n == L else ()))
            for n in range(L):
                me.done(tt(tmp[:], b_bar[:, 1], wide(simb[:, n]), MUL))
                me.done(tt(w_p[:, :, L - 1 - n], b_bar[:, 0], wide(re[:, n]), MUL))
                me.done(tt(w_p[:, :, L - 1 - n], w_p[:, :, L - 1 - n], tmp[:], ADD), *((weights,) if n == L - 1 else ()))

            def make_step(n):
                s_re, s_im = (re[:, L], im[:, L]) if n == 0 else (mr[:, n % 2], mi[:, n % 2])
                if n:
                    o_re, o_im = (re[:, L], im[:, L]) if n == 1 else (mr[:, (n - 1) % 2], mi[:, (n - 1) % 2])
                    times(s_re, s_im, o_re, o_im, o_re, o_im)
                c = coef[:, n % 2]
                for half in range(2):
                    r = slice(half * NP, (half + 1) * NP)
                    dve.tensor_copy(c[r, :, half], s_re[r])
                    last = ts(c[r, :, 1 - half], s_im[r], sign[r, 1:2], None, MUL)
                me.done(last)
                if n >= 2:
                    dve.wait_ge(*l_done.at(0, (n - 1) * NBANK - 1))
                me.done(tt(step[n % 2][:].rearrange("p g (a m) -> p g a m", a=2),
                           corner[:].rearrange("p (b a m) -> p b a m", a=2, b=1).broadcast_to([P, NG, 2, NP]),
                           c.rearrange("p g (a b) -> p g a b", b=1).broadcast_to([P, NG, 2, NP]), MUL), m_ready, n)

            make_step(0)
            for n in range(4):
                dve.wait_ge(*t_done.at(0, n))
                for g in range(4 * n, 4 * n + 4):
                    last = stt(taps[:, g], ident, d_skip[:, g:g + 1], ps[:, n, g % 4 * P:(g % 4 + 1) * P], MUL, ADD)
                last.then_inc(t_out.sem, 1)
            for n in range(STEPS):
                if n + 1 < STEPS:
                    make_step(n + 1)
                d = 1 << n
                for m in range(NBANK):
                    dve.wait_ge(*l_done.at(0, n * NBANK + m))
                    to = h[:, 2 * m:2 * m + 2, 1 + d:]
                    tt(to, to, ps[:, m].rearrange("p (g n) -> p g n", g=2)[:, :, 0:NS - d], ADD).then_inc(l_out.sem, 1)
            for n in range(NBANK):
                half, t, j = n // 4, n // 2 % 2, n % 2 * 4
                dve.wait_ge(*yt_done.at(0, n))
                to = yt[:, t].rearrange("p (h s l) -> p h l s", h=2, l=L)[:, half, j:j + 4]
                dve.tensor_copy(to, ps[:, n].rearrange("p (l s) -> p l s", l=4)).then_inc(yt_out.sem, 1)
            for n in range(NBANK):
                t, b = n // NB, n % NB
                at = slice(b * TB, (b + 1) * TB)
                dve.wait_ge(*glu_out.at(0, n))
                dve.wait_ge(*glu_done.at(0))
                tt(yt[:, t, at], yt[:, t, at], gate[:, t, at], MUL).then_inc(o_ready.sem, 1)
            for b in range(NB):
                at = slice(b * TB, (b + 1) * TB)
                dve.wait_ge(*n_done.at(0, b))
                ts(inv[:, at], ps[:, b], 1.0 / (G2 * P), EPS, MUL, ADD).then_inc(n_out.sem, 1)
            for b in range(NB):
                at = slice(b * TB, (b + 1) * TB)
                dve.wait_ge(*n_root.at(0, b))
                me.done(dve.reciprocal(inv[:, at], inv[:, at]))
                dve.wait_ge(*sq_ready.at(0, G2 * b + 1))
                for t in range(G2):
                    last = stt(yt[:, t, at], yt[:, t, at], col("s5_norm", t), inv[:, at], MUL, MUL)
                last.then_inc(yc_ready.sem, 1)

        @block.gpsimd
        def _(pool):
            pool.wait_ge(*u_in.at(0))
            for half in range(2):
                last = pool.tensor_copy(gate[:, half].rearrange("p (g t c) -> p g t c", g=NG, t=L),
                                        u_sub[:, half].rearrange("p (t g c) -> p g t c", g=NG, t=L))
            last.then_inc(u_grouped.sem, 1)

        @block.tensor
        def _(pe):
            pe.wait_ge(C["loaded"], C["loaded_n"])
            pe.wait_ge(*u_grouped.at(0))
            u4 = gate[:].rearrange("p h (g m) -> p h g m", g=NG)
            for n in range(NBANK):
                for g in (2 * n, 2 * n + 1):
                    for half in range(2):
                        at = (g % 2 * 2 + half) * P
                        mm = pe.transpose(ps[:, n, at:at + P], u4[:, half, g], ident)
                mm.then_inc(u_turned.sem, 1)
            pe.wait_ge(*loaded.at(0))
            pe.wait_ge(*c_ready.at(0))
            for n in range(4):
                pe.wait_ge(*u_out.at(0, n))
                for g in range(4 * n, 4 * n + 4):
                    for s in range(L):
                        mm = pe.matmul(ps[:, n, g % 4 * P:(g % 4 + 1) * P],
                                       b_pad[:, g, L - 1 - s:2 * L - 1 - s].rearrange("p s c -> p (s c)"),
                                       c_pad[:, g, L - 1 - s:2 * L - 1 - s].rearrange("p s c -> p (s c)"),
                                       start=s == 0, stop=s == L - 1)
                mm.then_inc(t_done.sem, 1)
            pe.wait_ge(*weights.at(0))
            for n in range(4):
                pe.wait_ge(*u_out.at(0, 4 + n))
                for g in range(4 * n, 4 * n + 4):
                    mm = pe.transpose(ps[:, 4 + n, g % 4 * P:(g % 4 + 1) * P], w_p[:, g].rearrange("p s c -> p (s c)"), ident)
                mm.then_inc(wt_done.sem, 1)
            for n in range(NBANK):
                if n < 4:
                    pe.wait_ge(*t_out.at(0, n))
                pe.wait_ge(*wt_out.at(0, max(n - 4, n // 2)))
                for g in (2 * n, 2 * n + 1):
                    mm = pe.matmul(ps[:, n, g % 2 * NS:(g % 2 + 1) * NS], w_in[:, g], u_g[:, g], start=True, stop=True)
                mm.then_inc(v_done.sem, 1)
            for n in range(STEPS):
                pe.wait_ge(*m_ready.at(0, n))
                d = 1 << n
                for m in range(NBANK):
                    pe.wait_ge(*(l_out.at(0, (n - 1) * NBANK + m) if n else v_out.at(0, m)))
                    for g in (2 * m, 2 * m + 1):
                        at = g % 2 * NS
                        mm = pe.matmul(ps[:, m, at:at + NS - d], step[n % 2][:, g], h[:, g, 1:1 + NS - d], start=True, stop=True)
                    mm.then_inc(l_done.sem, 1)
            pe.wait_ge(*t_out.at(0))
            for n in range(NBANK):
                half, g0 = n // 4, n % 4 * 4
                pe.wait_ge(*l_out.at(0, (STEPS - 1) * NBANK + max(n, g0 // 2 + 1)))
                for g in range(g0, g0 + 4):
                    to = ps[:, n, g % 4 * P:(g % 4 + 1) * P]
                    pe.matmul(to, u_g[:, g, half * HALF:(half + 1) * HALF], taps[:, g], start=True, stop=False)
                    mm = pe.matmul(to, h[:, g, half * HALF:(half + 1) * HALF], c_pad[:, g, L:].rearrange("p s c -> p (s c)"),
                                   start=False, stop=True)
                mm.then_inc(y_done.sem, 1)
            for n in range(NBANK):
                half, t, j = n // 4, n // 2 % 2, n % 2 * 4
                pe.wait_ge(*y_out.at(0, max(n, 4 * half + 3)))
                for k in range(4):
                    mm = pe.transpose(ps[:, n, k * P:(k + 1) * P], y_sub[:, half, j + k, t * P:(t + 1) * P], ident)
                mm.then_inc(yt_done.sem, 1)
            for n in range(NBANK):
                t, b = n // NB, n % NB
                pe.wait_ge(*yt_out.at(0))
                for k in range(G2):
                    mm = pe.matmul(ps[:, n], w_glu[:, k, t], yt[:, k, b * TB:(b + 1) * TB], start=k == 0, stop=k == G2 - 1)
                mm.then_inc(glu_done.sem, 1)
            for b in range(NB):
                pe.wait_ge(*glu_out.at(0, b))
                pe.wait_ge(*sq_ready.at(0, G2 * b + 1))
                for k in range(G2):
                    mm = pe.matmul(ps[:, b], ones, sq[:, k, b * TB:(b + 1) * TB], start=k == 0, stop=k == G2 - 1)
                mm.then_inc(n_done.sem, 1)


def attend_memory(nc, ctx, D, C):
    with ExitStack() as mem:
        def sb(name, shape, dt=F32):
            return mem.enter_context(nc.sbuf_tensor(name, shape, dt))

        def sig(name, n=1, unit=1, seed=0):
            return Signal(nc.alloc_semaphore(name), n, unit, seed)

        MT = N_MEM // P
        KVT = 2 * KT
        HDT = XA_HD // P
        D_HALF = D_MODEL // 2
        w_out = sb("w_out_sb", [P, KT, D_MODEL])
        key_w = sb("key_w", [P, KT, XA_HEADS * N_MEM])
        val_w = sb("val_w", [P, XA_HEADS * MT, D_MODEL])
        ident, headones, col, cols = C["ident"], C["headones"], C["col"], C["cols"]

        with ExitStack() as pre:
            def psb(name, shape):
                return pre.enter_context(nc.sbuf_tensor(name, shape, F32))

            NW = 4
            m_t = psb("m_t", [P, MT, D_MODEL])
            m_junk = psb("m_junk", [P, D_MODEL])
            m_sq = psb("m_sq", [P, MT])
            mn = psb("mn", [P, KT, N_MEM])
            kv = psb("kv", [P, KVT, N_MEM])
            ring = psb("xa_ring", [P, NW, D_MODEL])
            ps = pre.enter_context(nc.psum_tensor("m_ps", [P, 8, TB], F32))
            NT = KVT + KT + KT
            m_in, w_in = sig("m_in", 1, 16), [sig(f"xa_w_in{s}", NT // NW, 16) for s in range(NW)]
            w_out_in = sig("w_out_in", 1, 16)
            m_sumsq, m_ms, m_root, m_scaled = sig("m_sumsq"), sig("m_ms"), sig("m_root"), sig("m_scaled")
            m_turned, mn_ready = sig("m_turned", KT), sig("mn_ready", KT)
            kv_done, kv_out = sig("kv_done", KVT), sig("kv_out", KVT)
            kw_done, kw_out = sig("kw_done", 4 * XA_HEADS), sig("kw_out", 4 * XA_HEADS)
            vw_done, vw_out = sig("vw_done", 4 * XA_HEADS), sig("vw_out", 4 * XA_HEADS)
            own_v, own_a = sig("s3m_dve_own").sem, sig("s3m_act_own").sem

            def multiplied(n):
                if n < KVT:
                    return kv_done.at(0, n)
                if n < KVT + KT:
                    return kw_done.at(0, (n - KVT) // HDT * 4 + 3)
                return vw_done.at(0, (n - KVT - KT) // HDT * 4 + 3)

            with nc.Block() as block:
                @block.sync
                def _(sp):
                    sp.dma_start(m_t[:], D["mem"].rearrange("(j p) n -> p j n", p=P)).then_inc(m_in.sem, 16)
                    for n in range(NT):
                        if n >= NW:
                            sp.wait_ge(*multiplied(n - NW))
                        if n < KVT:
                            src = D["wkv"][n]
                        elif n < KVT + KT:
                            src = D["wq_t"][n - KVT]
                        else:
                            src = D["wo"][n - KVT - KT]
                        sp.dma_start(ring[:, n % NW], src).then_inc(w_in[n % NW].sem, 16)
                    sp.dma_start(w_out[:], D["w_out"]).then_inc(w_out_in.sem, 16)
                    sp.wait_ge(*w_out_in.at(0))

                @block.scalar
                def _(act):
                    me = Own(act, own_a)
                    act.wait_ge(*m_in.at(0))
                    for j in range(MT):
                        me.done(act.activation(m_junk[:], m_t[:, j], ACT.Square, accum_out=m_sq[:, j:j + 1]),
                                *((m_sumsq,) if j == MT - 1 else ()))
                    act.wait_ge(*m_ms.at(0))
                    me.done(act.activation(m_sq[:], m_sq[:], ACT.Sqrt), m_root)
                    for n in range(KVT):
                        act.wait_ge(*kv_done.at(0, n))
                        act.activation(kv[:, n], ps[:, n % 4, 0:N_MEM], ACT.Copy).then_inc(kv_out.sem, 1)
                    for n in range(4 * XA_HEADS):
                        act.wait_ge(*vw_done.at(0, n))
                        h, j, half = n // 4, n // 2 % 2, n % 2
                        act.activation(val_w[:, h * MT + j, half * D_HALF:(half + 1) * D_HALF], ps[:, 4 + n % 4],
                                       ACT.Copy).then_inc(vw_out.sem, 1)

                @block.vector
                def _(dve):
                    me = Own(dve, own_v)
                    dve.wait_ge(*m_sumsq.at(0))
                    me.done(dve.tensor_scalar(m_sq[:], m_sq[:], 1.0 / D_MODEL, EPS, ALU.mult, ALU.add), m_ms)
                    dve.wait_ge(*m_root.at(0))
                    me.done(dve.reciprocal(m_sq[:], m_sq[:]))
                    for j in range(MT):
                        last = dve.tensor_scalar(m_t[:, j], m_t[:, j], m_sq[:, j:j + 1], None, ALU.mult)
                    last.then_inc(m_scaled.sem, 1)
                    for k in range(KT):
                        dve.wait_ge(*m_turned.at(0, k))
                        dve.tensor_scalar(mn[:, k], ps[:, k, 0:N_MEM], col("xa_mem_norm", k), None, ALU.mult)\
                           .then_inc(mn_ready.sem, 1)
                    for n in range(4 * XA_HEADS):
                        dve.wait_ge(*kw_done.at(0, n))
                        h, k = n // 4, n % 4 * 2
                        dve.tensor_copy(key_w[:, k:k + 2, h * N_MEM:(h + 1) * N_MEM],
                                        ps[:, n % 4].rearrange("p (k m) -> p k m", k=2)).then_inc(kw_out.sem, 1)

                @block.tensor
                def _(pe):
                    pe.wait_ge(*m_scaled.at(0))
                    for k in range(KT):
                        for j in range(MT):
                            mm = pe.transpose(ps[:, k, j * P:(j + 1) * P], m_t[:, j, k * P:(k + 1) * P], ident)
                        mm.then_inc(m_turned.sem, 1)
                    pe.wait_ge(*mn_ready.at(0))
                    for n in range(KVT):
                        pe.wait_ge(*w_in[n % NW].at(0, n // NW))
                        if n >= 4:
                            pe.wait_ge(*kv_out.at(0, n - 4))
                        for k in range(KT):
                            mm = pe.matmul(ps[:, n % 4, 0:N_MEM], ring[:, n % NW, k * P:(k + 1) * P], mn[:, k], start=k == 0,
                                           stop=k == KT - 1)
                        mm.then_inc(kv_done.sem, 1)
                    pe.wait_ge(*kv_out.at(0))
                    for h in range(XA_HEADS):
                        for d in range(HDT):
                            n = KVT + h * HDT + d
                            pe.wait_ge(*w_in[n % NW].at(0, n // NW))
                        for k in range(KT):
                            n = h * 4 + k // 2
                            if k % 2 == 0 and n >= 4:
                                pe.wait_ge(*kw_out.at(0, n - 4))
                            for d in range(HDT):
                                w = ring[:, (KVT + h * HDT + d) % NW, k * P:(k + 1) * P]
                                mm = pe.matmul(ps[:, n % 4, k % 2 * N_MEM:(k % 2 + 1) * N_MEM], w, kv[:, h * HDT + d],
                                               start=d == 0, stop=d == HDT - 1)
                            if k % 2:
                                mm.then_inc(kw_done.sem, 1)
                    for h in range(XA_HEADS):
                        for d in range(HDT):
                            n = KVT + KT + h * HDT + d
                            pe.wait_ge(*w_in[n % NW].at(0, n // NW))
                        for m in range(4):
                            j, half, n = m // 2, m % 2, h * 4 + m
                            if n >= 4:
                                pe.wait_ge(*vw_out.at(0, n - 4))
                            for d in range(HDT):
                                w = ring[:, (KVT + KT + h * HDT + d) % NW, half * D_HALF:(half + 1) * D_HALF]
                                mm = pe.matmul(ps[:, 4 + n % 4], kv[:, KT + h * HDT + d, j * P:(j + 1) * P], w, start=d == 0,
                                               stop=d == HDT - 1)
                            mm.then_inc(vw_done.sem, 1)

        x_t = [sb(f"s3_x{u}", [P, D_MODEL]) for u in range(2)]
        oy = [sb(f"s3_oy{u}", [P, 2, G2, TC]) for u in range(2)]
        late = [sb(f"s3_late{u}", [P, 3, G2, TC]) for u in range(2)]
        mix = [sb(f"mix{u}", [P, KT, TC]) for u in range(2)]
        sq_o, sq_y = sb("sq_o", [P, G2, TC]), sb("sq_y", [P, G2, TC])
        head_var = sb("head_var", [P, 2, G2, TC])
        hn_tok, h2_tok = sb("hn_tok", [P, D_MODEL]), sb("h2_tok", [P, D_MODEL])
        s3_junk = sb("s3_junk", [P, D_MODEL])
        ms1, ms2 = sb("ms1", [P, 1]), sb("ms2", [P, 1])
        hn_t, h3_t = sb("hn_t", [P, KT, TC]), sb("h3_t", [P, KT, TC])
        top = sb("top", [P, XA_HEADS])
        total = sb("total", [P, XA_HEADS])
        prob = sb("prob", [P, XA_HEADS, N_MEM])
        prob_t = sb("prob_t", [P, XA_HEADS * MT, TC])
        ps_w = mem.enter_context(nc.psum_tensor("ps_w", [P, 2, TB], F32))
        ps_s = mem.enter_context(nc.psum_tensor("ps_score", [P, 2, TB], F32))
        ps_v = mem.enter_context(nc.psum_tensor("ps_v", [P, 2, TB], F32))
        ps_m = mem.enter_context(nc.psum_tensor("ps_m", [P, 2, TB], F32))
        SCALE = XA_HD ** -0.5

        loaded = [sig(f"s3_loaded{u}", 3, 16) for u in range(2)]
        x_loaded = [sig(f"s3_x_loaded{u}", 1, 16) for u in range(2)]
        names = {"fin_sq": 0, "fin1": 0, "centred": 0, "cent_sq": 0, "fin2": 0, "var_ready": 0, "var_root": 0, "mixed": 0,
                 "w_done": 2, "h1_ready": 0, "ss1": 0, "ms1_ready": 0, "root1": 0, "hn_scaled": 0, "turned0": 0, "turned1": 0,
                 "hn_out0": 0, "hn_out1": 0, "score_done": 0, "top_ready": 0, "exp_done": 0, "prob_ready": 0,
                 "p_turned0": 0, "p_turned1": 0, "p_out0": 0, "p_out1": 0, "v_done3": 0, "h2_ready": 0, "ss2": 0,
                 "ms2_ready": 0, "root2": 0, "h2_scaled": 0, "turned2": 0, "turned3": 0, "h3_out0": 0, "h3_out1": 0}
        S = {n: sig("s3_" + n, 1, 1, seed) for n, seed in names.items()}
        h2_stored, h3_stored = sig("h2_stored", 1, 16, 1), sig("h3_stored", 1, 16, 1)
        own = {n: sig("s3_own_" + n).sem for n in ("dve_fin", "dve_soft", "dve_n1", "dve_n2", "act", "sp_hold")}
        block = mem.enter_context(nc.Block())
        AG, DG, BONUS = range(3)

        def tiles(fori, parts, first):
            first()
            for p in range(2):
                parts(p, 0, p % 2, p > 0, True, True)
            with fori(0, NCH // 2 - 2) as i:
                for u in range(2):
                    parts(2 * i + 2 + u, i + 1, u, True, True, True)
            for p in (NCH - 2, NCH - 1):
                parts(p, NCH // 2 - 1, p % 2, True, p < NCH - 1, False)

        @block.sync
        def _(sp):
            for s in (h2_stored, h3_stored):
                s.seed_by(sp)

            def load(p, u):
                at = bass.ds(p, 1)
                sp.dma_start(oy[u][:], D["oy"][at].rearrange("a p k t n -> (a p) k t n")).then_inc(loaded[u].sem, 16)
                sp.dma_start(late[u][:], D["late"][at, :, 0:3].rearrange("a p k t n -> (a p) k t n")).then_inc(loaded[u].sem, 16)
                sp.dma_start(mix[u][:, G2:3 * G2].rearrange("p (k t) n -> p k t n", t=G2),
                             D["late"][at, :, 3:5].rearrange("a p k t n -> (a p) k t n")).then_inc(loaded[u].sem, 16)

            def load_x(p, u):
                sp.dma_start(x_t[u][:], D["x"][bass.ds(p * TC, TC)]).then_inc(x_loaded[u].sem, 16)

            def hold(at):
                sp.wait_ge(*at)
                sp.sem_inc(own["sp_hold"], 1)

            def parts(p, i, u, has_before, has_next, has_after):
                if has_after:
                    hold(S["w_done"].at(p))
                    load(p + 2, u)
                hold(S["h2_scaled"].at(p))
                sp.dma_start(D["h2"][bass.ds(p * TC, TC)], x_t[u][:]).then_inc(h2_stored.sem, 16)
                if has_after:
                    hold(h2_stored.at(p))
                    load_x(p + 2, u)
                if has_before:
                    store_turned(p - 1)

            def store_turned(p):
                hold(S["h3_out1"].at(p))
                sp.dma_start(D["h3t"][:, :, bass.ds(p * TC, TC)].rearrange("k p n -> p k n"), h3_t[:]).then_inc(h3_stored.sem, 16)

            tiles(nc.sync.Fori, parts, lambda: [(load(p, p), load_x(p, p)) for p in range(2)])
            store_turned(NCH - 1)
            sp.wait_ge(*h2_stored.at(NCH - 1))
            sp.wait_ge(*h3_stored.at(NCH - 1))

        @block.tensor
        def _(pe):
            S["w_done"].seed_by(pe)

            def fin1(p, u):
                pe.wait_ge(*S["fin_sq"].at(p))
                pe.matmul(ps_m[:, 0, 0:G2 * TC], headones, sq_o[:].rearrange("p t n -> p (t n)"), start=True, stop=True)
                pe.matmul(ps_m[:, 0, G2 * TC:], headones, oy[u][:, 1].rearrange("p t n -> p (t n)"), start=True,
                          stop=True).then_inc(S["fin1"].sem, 1)

            def fin2(p, u):
                pe.wait_ge(*S["cent_sq"].at(p))
                pe.matmul(ps_m[:, 1, 0:G2 * TC], headones, sq_y[:].rearrange("p t n -> p (t n)"), start=True,
                          stop=True).then_inc(S["fin2"].sem, 1)

            def project(p, u):
                pe.wait_ge(*S["mixed"].at(p))
                for half in range(2):
                    for k in range(KT):
                        mm = pe.matmul(ps_w[:, half], mix[u][:, k], w_out[:, k, half * D_HALF:(half + 1) * D_HALF],
                                       start=k == 0, stop=k == KT - 1)
                mm.then_inc(S["w_done"].sem, 1)

            def turn(src, ready, dones, p):
                pe.wait_ge(*ready.at(p))
                for b in range(2):
                    for k in range(4):
                        mm = pe.transpose(ps_m[:, b, k * P:(k + 1) * P], src[:, (4 * b + k) * P:(4 * b + k + 1) * P], ident)
                    mm.then_inc(dones[b].sem, 1)

            def parts(p, i, u, has_before, has_next, has_after):
                pe.wait_ge(*S["hn_out1"].at(p))
                for half in range(2):
                    for k in range(KT):
                        mm = pe.matmul(ps_s[:, half], hn_t[:, k], key_w[:, k, half * TB:(half + 1) * TB], start=k == 0,
                                       stop=k == KT - 1)
                mm.then_inc(S["score_done"].sem, 1)
                if has_before:
                    if has_next:
                        pe.wait_ge(*S["mixed"].at(p + 1))
                    turn(h2_tok, S["h2_scaled"], (S["turned2"], S["turned3"]), p - 1)
                if has_next:
                    project(p + 1, 1 - u)
                if has_before:
                    pe.wait_ge(*S["h3_out1"].at(p - 1))
                turn(prob[:].rearrange("p h m -> p (h m)"), S["prob_ready"], (S["p_turned0"], S["p_turned1"]), p)
                pe.wait_ge(*S["p_out1"].at(p))
                if has_after:
                    fin1(p + 2, u)
                for half in range(2):
                    for k in range(KT):
                        mm = pe.matmul(ps_v[:, half], prob_t[:, k], val_w[:, k, half * TB:(half + 1) * TB], start=k == 0,
                                       stop=k == KT - 1)
                mm.then_inc(S["v_done3"].sem, 1)
                if has_after:
                    fin2(p + 2, u)
                if has_next:
                    if has_after:
                        pe.wait_ge(*S["var_ready"].at(p + 2))
                    turn(hn_tok, S["hn_scaled"], (S["turned0"], S["turned1"]), p + 1)

            def first():
                for p in range(2):
                    fin1(p, p)
                    fin2(p, p)
                    pe.wait_ge(*S["var_ready"].at(p))
                project(0, 0)
                turn(hn_tok, S["hn_scaled"], (S["turned0"], S["turned1"]), 0)

            tiles(nc.tensor.Fori, parts, first)
            turn(h2_tok, S["h2_scaled"], (S["turned2"], S["turned3"]), NCH - 1)

        @block.scalar
        def _(act):
            def fin_sq(p, u, i):
                act.wait_ge(*loaded[u].at(i))
                act.activation(sq_o[:], oy[u][:, 0], ACT.Square).then_inc(S["fin_sq"].sem, 1)

            def cent_sq(p, u):
                act.wait_ge(*S["centred"].at(p))
                act.activation(sq_y[:], oy[u][:, 1], ACT.Square).then_inc(S["cent_sq"].sem, 1)

            def var_root(p):
                act.wait_ge(*S["var_ready"].at(p))
                act.activation(head_var[:], head_var[:], ACT.Sqrt).then_inc(S["var_root"].sem, 1)

            def norm(p, u, ready, ms, ss, ms_ready, root):
                act.wait_ge(*S[ready].at(p))
                act.activation(s3_junk[:], x_t[u][:], ACT.Square, accum_out=ms[:]).then_inc(S[ss].sem, 1)
                act.wait_ge(*S[ms_ready].at(p))
                act.activation(ms[:], ms[:], ACT.Sqrt).then_inc(S[root].sem, 1)

            def parts(p, i, u, has_before, has_next, has_after):
                act.wait_ge(*S["top_ready"].at(p))
                act.wait_ge(*S["hn_scaled"].at(p))
                for h in range(XA_HEADS):
                    s = ps_s[:, h // 2, h % 2 * N_MEM:(h % 2 + 1) * N_MEM]
                    last = act.activation(prob[:, h], s, ACT.Exp, bias=top[:, h:h + 1], scale=SCALE,
                                          accum_out=total[:, h:h + 1])
                last.then_inc(S["exp_done"].sem, 1)
                if has_after:
                    fin_sq(p + 2, u, i + 1)
                for b in range(2):
                    act.wait_ge(*S[f"p_turned{b}"].at(p))
                    act.activation(prob_t[:, 4 * b:4 * b + 4].rearrange("p k n -> p (k n)"), ps_m[:, b], ACT.Copy)\
                       .then_inc(S[f"p_out{b}"].sem, 1)
                if has_next:
                    norm(p + 1, 1 - u, "h1_ready", ms1, "ss1", "ms1_ready", "root1")
                if has_after:
                    cent_sq(p + 2, u)
                norm(p, u, "h2_ready", ms2, "ss2", "ms2_ready", "root2")
                if has_after:
                    var_root(p + 2)

            def first():
                for p in range(2):
                    fin_sq(p, p, 0)
                    cent_sq(p, p)
                    var_root(p)
                norm(0, 0, "h1_ready", ms1, "ss1", "ms1_ready", "root1")

            tiles(nc.scalar.Fori, parts, first)

        @block.vector
        def _(dve):
            def centre(p, u):
                dve.wait_ge(*S["fin1"].at(p))
                dve.tensor_scalar(head_var[:, 0].rearrange("p t n -> p (t n)"), ps_m[:, 0, 0:G2 * TC], 1.0 / HD, EPS, ALU.mult,
                                  ALU.add)
                y = oy[u][:, 1].rearrange("p t n -> p (t n)")
                dve.scalar_tensor_tensor(y, ps_m[:, 0, G2 * TC:], -1.0 / HD, y, ALU.mult, ALU.add).then_inc(S["centred"].sem, 1)

            def finish(p, u):
                me = Own(dve, own["dve_fin"], p, 4)
                dve.wait_ge(*S["fin2"].at(p))
                dve.tensor_scalar(head_var[:, 1].rearrange("p t n -> p (t n)"), ps_m[:, 1, 0:G2 * TC], 1.0 / HD, RW_LN_EPS,
                                  ALU.mult, ALU.add).then_inc(S["var_ready"].sem, 1)
                dve.wait_ge(*S["var_root"].at(p))
                dve.wait_ge(*S["w_done"].at(p, back=2))
                me.done(dve.reciprocal(head_var[:], head_var[:]))
                o, y = mix[u][:, 0:G2], mix[u][:, 3 * G2:]
                dve.tensor_tensor(o, oy[u][:, 0], head_var[:, 0], ALU.mult)
                me.done(dve.tensor_tensor(y, oy[u][:, 1], head_var[:, 1], ALU.mult))
                dve.tensor_tensor(o, o, late[u][:, AG], ALU.mult)
                for t in range(G2):
                    last = dve.tensor_scalar(y[:, t], y[:, t], col("rw_ln_g", t), col("rw_ln_b", t), ALU.mult, ALU.add)
                me.done(last)
                me.done(dve.tensor_tensor(y, y, late[u][:, BONUS], ALU.add))
                me.done(dve.tensor_tensor(y, y, late[u][:, DG], ALU.mult), S["mixed"])
                me.check()

            def residual(p, u, done, ps, ready):
                dve.wait_ge(*S[done].at(p))
                x = x_t[u][:]
                dve.tensor_tensor(x, x, ps[:].rearrange("p a n -> p (a n)"), ALU.add).then_inc(S[ready].sem, 1)

            def scale(p, u, name, ms, ss, ms_ready, root, dst, scaled, free):
                me = Own(dve, own[name], p, 1)
                dve.wait_ge(*S[ss].at(p))
                dve.tensor_scalar(ms[:], ms[:], 1.0 / D_MODEL, EPS, ALU.mult, ALU.add).then_inc(S[ms_ready].sem, 1)
                dve.wait_ge(*S[root].at(p))
                me.done(dve.reciprocal(ms[:], ms[:]))
                if free:
                    dve.wait_ge(*free)
                dve.tensor_scalar(dst[:], x_t[u][:], ms[:, 0:1], None, ALU.mult).then_inc(S[scaled].sem, 1)

            def turned(p, names, gain, dst, outs, free=None):
                if free:
                    dve.wait_ge(*free)
                for b in range(2):
                    dve.wait_ge(*S[names[b]].at(p))
                    g = cols(gain, KT)[:, 4 * b:4 * b + 4].rearrange("p (k n) -> p k n", n=1).broadcast_to([P, 4, TC])
                    dve.tensor_tensor(dst[:, 4 * b:4 * b + 4], ps_m[:, b].rearrange("p (k n) -> p k n", k=4), g,
                                      ALU.mult).then_inc(S[outs[b]].sem, 1)

            def n1(p, u):
                scale(p, u, "dve_n1", ms1, "ss1", "ms1_ready", "root1", hn_tok, "hn_scaled", None)

            def parts(p, i, u, has_before, has_next, has_after):
                me = Own(dve, own["dve_soft"], p, 2)
                dve.wait_ge(*S["score_done"].at(p))
                me.done(dve.tensor_reduce(top[:], ps_s[:].rearrange("p a (h m) -> p (a h) m", m=N_MEM), AX_X, ALU.max))
                dve.tensor_scalar(top[:], top[:], -SCALE, None, ALU.mult).then_inc(S["top_ready"].sem, 1)
                dve.wait_ge(*S["exp_done"].at(p))
                me.done(dve.reciprocal(total[:], total[:]))
                dve.tensor_tensor(prob[:], prob[:], total[:].rearrange("p (h m) -> p h m", m=1).broadcast_to([P, XA_HEADS, N_MEM]),
                                  ALU.mult).then_inc(S["prob_ready"].sem, 1)
                if has_before:
                    turned(p - 1, ("turned2", "turned3"), "ffn_norm", h3_t, ("h3_out0", "h3_out1"), h3_stored.at(p - 1, back=1))
                if has_next:
                    dve.wait_ge(*x_loaded[1 - u].at(i + u))
                    residual(p + 1, 1 - u, "w_done", ps_w, "h1_ready")
                    n1(p + 1, 1 - u)
                if has_after:
                    centre(p + 2, u)
                residual(p, u, "v_done3", ps_v, "h2_ready")
                scale(p, u, "dve_n2", ms2, "ss2", "ms2_ready", "root2", h2_tok, "h2_scaled", None)
                if has_after:
                    finish(p + 2, u)
                if has_next:
                    turned(p + 1, ("turned0", "turned1"), "xa_norm", hn_t, ("hn_out0", "hn_out1"))

            def first():
                for p in range(2):
                    centre(p, p)
                    finish(p, p)
                dve.wait_ge(*x_loaded[0].at(0))
                residual(0, 0, "w_done", ps_w, "h1_ready")
                n1(0, 0)
                turned(0, ("turned0", "turned1"), "xa_norm", hn_t, ("hn_out0", "hn_out1"))

            tiles(nc.vector.Fori, parts, first)
            turned(NCH - 1, ("turned2", "turned3"), "ffn_norm", h3_t, ("h3_out0", "h3_out1"), h3_stored.at(NCH - 1, back=1))


def gated_mlp(nc, ctx, D, C):
    with ExitStack() as mem:
        def sb(name, shape, dt=F32):
            return mem.enter_context(nc.sbuf_tensor(name, shape, dt))

        def sig(name, n=1, unit=1, seed=0):
            return Signal(nc.alloc_semaphore(name), n, unit, seed)

        TH = SEQ // 2
        NT = TH // TC
        DH = D_MODEL // 2
        PAIRS = FF_T // 2
        hn = sb("ffn_hn", [P, KT, TH])
        h3 = sb("h3", [P, NT, D_MODEL])
        hidden = sb("hidden", [P, FF_T, TH])
        raw = sb("ffn_raw", [P, 2, 2, 2 + TH])
        tails = sb("tails", [P, FF_T, 2, 2])
        value = sb("ffn_value", [P, TH])
        w_up = sb("w_up_ring", [P, 2, 2, KT * P])
        w_dn = sb("w_dn_ring", [P, 2, 2, DH])
        gain = sb("final_gain", [P, D_MODEL])
        sumsq, rms = sb("ffn_sumsq", [P, NT]), sb("ffn_rms", [P, NT])
        ps = mem.enter_context(nc.psum_tensor("ffn_ps", [P, 8, TB], F32))

        hn_in, h2_in, gain_in = sig("ffn_hn_in", 1, 16), sig("ffn_h2_in", 1, 16), sig("gain_in", 1, 16)
        up_in = [sig(f"w_up_in{u}", 1, 16) for u in range(2)]
        dn_in = [sig(f"w_dn_in{u}", 1, 16) for u in range(2)]
        up_done, up_out = sig("up_done", 2), sig("up_out", 2)
        sp_hold = sig("ffn_sp_hold")
        conv_gate, gated, hidden_ready = sig("conv_gate"), sig("gated"), sig("hidden_ready", 1, 1, 2)
        dn_used = sig("w_dn_used", 2 * PAIRS)
        dn_done, added = sig("dn_done", 2 * NT), sig("added", 2 * NT)
        squared, ms_ready, root_ready, out_ready = sig("squared"), sig("ffn_ms"), sig("ffn_root"), sig("out_ready", NT)
        stored = sig("out_stored", NT, 16)
        own_conv, own_norm = [sig(f"own_conv{half}").sem for half in range(2)], sig("own_norm").sem
        own_act = sig("ffn_own_act").sem
        block = mem.enter_context(nc.Block())

        def feature_tiles(fori, run, half, start=0):
            with fori(start, PAIRS) as i:
                for u in range(2):
                    run(2 * i + u, half * FF_T + 2 * i + u, half * PAIRS + i, u)

        @block.sync
        def _(sp):
            def load_up(f, u):
                sp.dma_start(w_up[:, u], D["w_up"][bass.ds(f, 1)].rearrange("a p g n -> (a p) g n")).then_inc(up_in[u].sem, 16)

            def load_hn(half):
                sp.dma_start(hn[:], D["h3t"][:, :, half * TH:(half + 1) * TH].rearrange("k p n -> p k n"))\
                  .then_inc(hn_in.sem, 16)

            load_hn(0)
            load_up(0, 0)
            load_up(1, 1)
            sp.dma_start(gain[:], D["final_gain"]).then_inc(gain_in.sem, 16)
            for half in range(2):
                with nc.sync.Fori(0, PAIRS - 1) as i:
                    for u in range(2):
                        sp.wait_ge(*up_done.at(half * FF_T + 2 * i + u))
                        sp.sem_inc(sp_hold.sem, 1)
                        load_up(2 * i + 2 + u, u)
                sp.wait_ge(*up_done.at((half + 1) * FF_T - 1))
                if half == 0:
                    load_hn(1)
                    load_up(0, 0)
                    load_up(1, 1)
                for t in range(NT):
                    sp.wait_ge(*out_ready.at(half, t))
                    at = half * TH + t * TC
                    sp.dma_start(D["out"][at:at + TC], h3[:, t]).then_inc(stored.sem, 16)
                sp.wait_ge(*stored.at(half))

        @block.gpsimd
        def _(pool):
            for half in range(2):
                if half:
                    pool.wait_ge(*stored.at(half - 1))
                pool.dma_start(h3[:], D["h2"][half * TH:(half + 1) * TH].rearrange("(t p) n -> p t n", p=P))\
                    .then_inc(h2_in.sem, 16)
                for n in range(2 * PAIRS):
                    use = half * 2 * PAIRS + n
                    if use >= 2:
                        pool.wait_ge(*dn_used.at(0, use - 2))
                    pool.dma_start(w_dn[:, n % 2], D["w_down"][n // PAIRS, n % PAIRS]).then_inc(dn_in[n % 2].sem, 16)

        @block.tensor
        def _(pe):
            for half in range(2):
                pe.wait_ge(*hn_in.at(half))
                if half:
                    pe.wait_ge(*added.at(half - 1))

                def up(f, p, i, u, wait_out=True):
                    pe.wait_ge(*up_in[u].at(i))
                    if wait_out:
                        pe.wait_ge(*up_out.at(p - 2))
                    for g in range(2):
                        for b in range(2):
                            for k in range(KT):
                                mm = pe.matmul(ps[:, 4 * u + 2 * g + b], w_up[:, u, g, k * P:(k + 1) * P],
                                               hn[:, k, b * TB:(b + 1) * TB], start=k == 0, stop=k == KT - 1)
                        mm.then_inc(up_done.sem, 1)

                for u in range(2):
                    up(u, half * FF_T + u, half * PAIRS, u, half > 0)
                feature_tiles(nc.tensor.Fori, up, half, 1)

                pe.wait_ge(*up_out.at((half + 1) * FF_T - 1))
                for c in range(2):
                    for f in range(FF_T):
                        n = c * PAIRS + f // 2
                        if c == 0 and f in (0, FF_T - 1):
                            pe.wait_ge(*hidden_ready.at((half + 1) * FF_T - (2 if f == 0 else 1)))
                        if f % 2 == 0:
                            pe.wait_ge(*dn_in[n % 2].at(half * PAIRS + n // 2))
                        for t in range(NT):
                            if c and f == 0:
                                pe.wait_ge(*added.at(half, t))
                            mm = pe.matmul(ps[:, t], hidden[:, f, t * TC:(t + 1) * TC], w_dn[:, n % 2, f % 2], start=f == 0,
                                           stop=f == FF_T - 1)
                            if f == FF_T - 1:
                                mm.then_inc(dn_done.sem, 1)
                        if f % 2 and f < FF_T - 1:
                            mm.then_inc(dn_used.sem, 1)
                    pe.wait_ge(*dn_done.at(half, (c + 1) * NT - 1))
                    pe.sem_inc(dn_used.sem, 1)

        @block.scalar
        def _(act):
            me = Own(act, own_act)
            for half in range(2):
                def run(f, p, i, u):
                    for g in range(2):
                        act.wait_ge(*up_done.at(p, g))
                        if g == 0:
                            act.wait_ge(*hidden_ready.at(p, back=2))
                        act.activation(raw[:, u, g, 2:], ps[:, 4 * u + 2 * g:4 * u + 2 * g + 2].rearrange("p a n -> p (a n)"),
                                       ACT.Copy).then_inc(up_out.sem, 1)
                    act.wait_ge(*conv_gate.at(p))
                    at = hidden[:, bass.ds(f, 1)].rearrange("p a n -> p (a n)")
                    act.activation(at, at, ACT.Silu).then_inc(gated.sem, 1)

                feature_tiles(nc.scalar.Fori, run, half)
                for t in range(NT):
                    act.wait_ge(*added.at(half, NT + t))
                    me.done(act.activation(value[:], h3[:, t], ACT.Square, accum_out=sumsq[:, t:t + 1]))
                act.sem_inc(squared.sem, 1)
                act.wait_ge(*ms_ready.at(half))
                act.activation(rms[:], rms[:], ACT.Sqrt).then_inc(root_ready.sem, 1)

        @block.vector
        def _(dve):
            hidden_ready.seed_by(dve)
            me = Own(dve, own_norm)
            me.done(dve.memset(raw[:, :, :, 0:2], 0.0))
            for half in range(2):
                def taps(src, dst, f, me, signal=None):
                    def at(x):
                        return C["col_at"](x, f)

                    me.done(dve.tensor_scalar(dst, src[:, 2:2 + TH], at("ffn_conv_w2"), at("ffn_conv_b"), ALU.mult, ALU.add))
                    me.done(dve.scalar_tensor_tensor(dst, src[:, 1:1 + TH], at("ffn_conv_w1"), dst, ALU.mult, ALU.add))
                    last = dve.scalar_tensor_tensor(dst, src[:, 0:TH], at("ffn_conv_w0"), dst, ALU.mult, ALU.add)
                    if signal:
                        last.then_inc(signal.sem, 1)
                    else:
                        me.done(last)

                def run(f, p, i, u):
                    me = Own(dve, own_conv[half], p - half * FF_T, 5 + half)
                    dve.wait_ge(*up_out.at(p))
                    tail = tails[:, bass.ds(f, 1)].rearrange("p a g n -> p (a g) n")
                    if half == 0:
                        dve.tensor_copy(tail, raw[:, u, :, TH:])
                    else:
                        me.done(dve.tensor_copy(raw[:, u, :, 0:2], tail))
                    at = hidden[:, bass.ds(f, 1)].rearrange("p a n -> p (a n)")
                    taps(raw[:, u, 0], at, f, me, conv_gate)
                    taps(raw[:, u, 1], value[:], f + FF_T, me)
                    dve.wait_ge(*gated.at(p))
                    dve.tensor_tensor(at, at, value[:], ALU.mult).then_inc(hidden_ready.sem, 1)

                feature_tiles(nc.vector.Fori, run, half)
                dve.wait_ge(*h2_in.at(half))
                for c in range(2):
                    for t in range(NT):
                        dve.wait_ge(*dn_done.at(half, c * NT + t))
                        h = h3[:, t, c * DH:(c + 1) * DH]
                        dve.tensor_tensor(h, h, ps[:, t], ALU.add).then_inc(added.sem, 1)
                dve.wait_ge(*squared.at(half))
                dve.tensor_scalar(rms[:], sumsq[:], 1.0 / D_MODEL, EPS, ALU.mult, ALU.add).then_inc(ms_ready.sem, 1)
                dve.wait_ge(*root_ready.at(half))
                me.done(dve.reciprocal(rms[:], rms[:]))
                dve.wait_ge(*gain_in.at(0))
                for t in range(NT):
                    dve.scalar_tensor_tensor(h3[:, t], h3[:, t], rms[:, t:t + 1], gain[:], ALU.mult, ALU.mult)\
                       .then_inc(out_ready.sem, 1)


def channels(v):
    return np.ascontiguousarray(np.asarray(v).reshape(-1, P).T)


def parameter_columns(i):
    mu = i["rw_mu"][0].reshape(-1, P)
    parts = {
        "mix_norm": channels(i["mix_norm"]), "lb_param": channels(i["lb_param"]), "hg_norm": channels(i["hg_norm"]),
        "rw_mu": np.stack([mu[c - FEATURES[3][1]] for _, c in FEATURES[:Z_TILES]], 1),
        "lru_norm": channels(i["lru_norm"]), "s5_norm": channels(i["s5_norm"]), "s5_b_glu": channels(i["s5_b_glu"]),
        "xa_norm": channels(i["xa_norm"]), "xa_mem_norm": channels(i["xa_mem_norm"]), "ffn_norm": channels(i["ffn_norm"]),
        "ffn_conv_b": channels(i["ffn_conv_b"]),
    }
    for n in ("rw_w0", "rw_a0", "rw_k_k", "rw_k_a", "rw_r_k", "rw_ln_g", "rw_ln_b", "lru_ba", "lru_bx", "lru_lam",
              "lru_conv_b"):
        parts[n] = channels(i[n])
    for tap in range(LRU_TAPS):
        parts[f"lru_conv_w{tap}"] = channels(i["lru_conv_w"][0, tap])
    for tap in range(3):
        parts[f"ffn_conv_w{tap}"] = channels(i["ffn_conv_w"][0, tap])
    at, n = {}, 0
    for name, a in parts.items():
        at[name] = n
        n += a.shape[1]
    return np.ascontiguousarray(np.concatenate(list(parts.values()), 1)), at


def constants():
    t = np.arange(P)
    heads = (t[:, None] // HD == t[None] // HD)
    reset = np.broadcast_to((np.arange(TB) % TC != 0), (P, TB))
    cst = np.concatenate([np.eye(P), heads, np.ones((P, P)), reset], 1).astype(np.float32)
    s, t = t[:, None], t[None]
    masks = [(s // (2 * b) == t // (2 * b)) & (s % (2 * b) < b) & (t % (2 * b) >= b) for b in LEVELS] + [s == t]
    pair_mask = np.stack([s < t, s <= t, s < t, s <= t], 1).astype(np.float32)
    return cst, np.concatenate([np.stack(masks, 1).astype(np.float32), pair_mask], 1)


def lay_out(i):
    a, k = {}, lambda w: w.reshape(KT, P, -1).transpose(1, 0, 2)
    w_in = i["w_in"][0]
    a["x"] = i["x"][0]
    a["w_feat"] = np.stack([k(w_in[:, c * P:(c + 1) * P]) for _, c in FEATURES])
    a["w_tok"] = k(np.concatenate([w_in[:, 512:768], w_in[:, 1536:1792]], 1))
    a["prm"], at = parameter_columns(i)
    a["cst"], a["masks"] = constants()
    lora = np.zeros((P, 6, P), np.float32)
    for m, (name, r0, r1) in enumerate((("rw_w_up", 0, 32), ("rw_a_up", 32, 64), ("rw_g_up", 64, 128))):
        lora[r0:r1, 2 * m:2 * m + 2] = i[name][0].reshape(r1 - r0, 2, P)
    a["lora"] = lora
    lru_w = np.zeros((P, 4, P), np.float32)
    for m, name in enumerate(("lru_wa", "lru_wx")):
        for g in range(4):
            r = g % 2 * HD
            lru_w[r:r + HD, 2 * m + g // 2, r:r + HD] = i[name][0, g]
    a["lru_w"] = lru_w
    stack = np.concatenate
    a["s5_raw"] = np.stack([stack([x.T, x.T]) for x in (i["s5_a_re"][0], i["s5_a_im"][0],
                                                        np.broadcast_to(i["s5_log_dt"][0][:, None], (16, HD)))], 1)
    b_re, b_im = (i[n][0].transpose(1, 0, 2) for n in ("s5_b_re", "s5_b_im"))
    c_re, c_im = (i[n][0].transpose(2, 0, 1) for n in ("s5_c_re", "s5_c_im"))
    for name, x, y in (("s5_b", b_re, b_im), ("s5_c", c_re, c_im)):
        a[name] = np.stack([stack([x, y]), stack([y, x])], 1)
    a["s5_d"] = np.tile(i["s5_d"][0].reshape(16, 16).T, (8, 1))
    half = np.arange(P)[:, None] < HD
    a["s5_sign"] = np.where(half, [[-1, 1]], [[1, -1]]).astype(np.float32)
    a["s5_corner"] = (np.arange(P)[:, None] % HD == np.arange(P)[None] % HD).astype(np.float32)
    a["s5_glu"] = i["s5_w_glu"][0].reshape(2, P, 2, P).transpose(1, 0, 2, 3)
    a["mem"] = i["mem"][0]
    wkv = i["xa_wkv"][0]
    a["wkv"] = np.stack([k(wkv[:, n:n + P]).reshape(P, -1) for n in range(0, 2 * D_MODEL, P)])
    a["wq_t"] = i["xa_wq"][0].T.reshape(KT, P, D_MODEL)
    a["wo"] = i["xa_wo"][0].reshape(KT, P, D_MODEL)
    a["w_out"] = k(i["w_out"][0])
    a["w_up"] = i["ffn_w_up"][0].reshape(KT, P, 2, FF_T, P).transpose(3, 1, 2, 0, 4).reshape(FF_T, P, 2, D_MODEL)
    a["w_down"] = i["ffn_w_down"][0].reshape(FF_T // 2, 2, P, 2, D_MODEL // 2).transpose(3, 0, 2, 1, 4)
    a["final_gain"] = np.broadcast_to(i["final_norm"], (P, D_MODEL))
    return {n: np.ascontiguousarray(v) for n, v in a.items()}, at


SCRATCH = {"scan": (NCH, P, len(SCAN), G2, TC), "late": (NCH, P, len(LATE), G2, TC), "va": (NCH, P, G2 * P), "cu": (NCH, P, G2 * P),
           "vd": (NCH, P, G2 * P), "oy": (NCH, P, 2, G2, TC), "h2": (SEQ, D_MODEL), "h3t": (KT, P, SEQ)}


def build(nc, D):
    with ExitStack() as ctx:
        with ExitStack() as mixers:
            C = load_constants(nc, ctx, mixers, D)
            for stage in (project_and_prepare, scan_chunks, state_space):
                with nc.cleanup_on_exit():
                    stage(nc, ctx, D, C)
        for stage in (attend_memory, gated_mlp):
            with nc.cleanup_on_exit():
                stage(nc, ctx, D, C)


def kernel(**inputs):
    import concourse.bacc as bacc
    from concourse.bass_utils import run_bass_kernel_spmd

    arrays, prm_at = lay_out({name: np.asarray(a) for name, a in inputs.items()})
    nc = bacc.Bacc("TRN2", target_bir_lowering=False, num_devices=1)
    D = {n: nc.dram_tensor("in_" + n, a.shape, F32, kind="ExternalInput").ap() for n, a in arrays.items()}
    D["prm_at"] = prm_at
    for n, shape in SCRATCH.items():
        D[n] = nc.dram_tensor("scratch_" + n, shape, F32, kind="Internal").ap()
    D["out"] = nc.dram_tensor("out", (SEQ, D_MODEL), F32, kind="ExternalOutput").ap()
    build(nc, D)
    r = run_bass_kernel_spmd(nc, [{"in_" + n: a for n, a in arrays.items()}], core_ids=[0])
    return r.results[0]["out"].reshape(1, SEQ, D_MODEL)
```

```python
from contextlib import ExitStack

import concourse.bass as bass
import numpy as np
from concourse import mybir

F32 = mybir.dt.float32
F32R = mybir.dt.float32r
I32 = mybir.dt.int32
ALU = mybir.AluOpType
ACT = mybir.ActivationFunctionType
AX_X = mybir.AxisListType.X

P = 128
SEQ, D_MODEL, N_MEM = 2048, 1024, 256
KT = D_MODEL // P
G2 = 2
TB = 512
NB = SEQ // TB
TC = 128
NCH = SEQ // TC
CB = TB // TC
EPS = 1e-6
RW_LN_EPS = 64e-5
LRU_C = 8.0
LRU_TAPS = 4
HD = 64
DECAY = -float(np.exp(-0.5))
LEVELS = (64, 32, 16, 8, 4, 2, 1)
XA_HEADS, XA_HD = 4, 256
D_FF = 2816
FF_T = D_FF // P

FEATURES = (("lat", 20), ("k", 16), ("k", 17), ("r", 14), ("r", 15), ("v", 18), ("v", 19), ("bx", 10), ("bx", 11),
            ("by", 8), ("by", 9), ("f", 2), ("f", 3), ("q", 0), ("q", 1), ("g", 6), ("g", 7),
            ("a_v", 4), ("a_v", 5), ("c_u", 12), ("c_u", 13))
NF = len(FEATURES)
Z_TILES = 7
SCAN = ("q", "k", "cum", "r", "kp", "kk", "b", "csig")
LATE = ("ag", "dg", "bonus", "yb", "yc")


class Signal:

    def __init__(self, sem, n=1, unit=1, seed=0):
        self.sem, self.n, self.unit, self.seed = sem, n, unit, seed

    def at(self, p, k=None, back=0):
        k = self.n if k is None else k + 1
        return self.sem, p * (self.n * self.unit) + ((self.seed - back) * self.n + k) * self.unit

    def seed_by(self, engine):
        engine.sem_inc(self.sem, self.seed * self.n * self.unit)


class Own:

    def __init__(self, engine, sem, p=0, n=0):
        self.engine, self.sem, self.p, self.n, self.k = engine, sem, p, n, 0

    def done(self, instruction, signal=None, k=0):
        if signal is None:
            instruction.then_inc(self.sem, 1)
            self.k += 1
            self.engine.wait_ge(self.sem, self.p * self.n + self.k)
        else:
            instruction.then_inc(signal.sem, 1)
            self.engine.wait_ge(*signal.at(self.p, k))

    def check(self):
        assert self.k == self.n, f"{self.k} instructions of its own in a pass, {self.n} were said"


def load_constants(nc, ctx, mixers, D):
    def sb(name, shape, dt=F32):
        return ctx.enter_context(nc.sbuf_tensor(name, shape, dt))

    def sem(name):
        return ctx.enter_context(nc.semaphore(name))

    n_prm = D["prm"].shape[1]
    prm = sb("prm_sb", [P, n_prm])
    cst = sb("cst", [P, 3 * P + TB])
    derived = sb("derived", [P, 8 * G2])
    masks = mixers.enter_context(nc.sbuf_tensor("masks_sb", [P, len(LEVELS) + 1 + 4, P], F32))
    lora = mixers.enter_context(nc.sbuf_tensor("lora_sb", [P, 6, P], F32))
    lru_w = mixers.enter_context(nc.sbuf_tensor("lru_w_sb", [P, 4, P], F32))
    C = {"prm": prm, "ident": cst[:, 0:P], "headones": cst[:, P:2 * P], "ones": cst[:, 2 * P:3 * P], "reset": cst[:, 3 * P:], "masks": masks,
         "pair_mask": masks[:, len(LEVELS) + 1:],
         "lora": lora, "lru_w": lru_w, "loaded": sem("constants_loaded"), "loaded_n": 5 * 16,
         "prepared": sem("constants_prepared")}
    where = D["prm_at"]

    def col(name, t=0):
        return prm[:, where[name] + t:where[name] + t + 1]

    def cols(name, n):
        return prm[:, where[name]:where[name] + n]

    def col_at(name, t):
        return prm[:, bass.ds(where[name] + t, 1)]

    C["col"], C["cols"], C["col_at"] = col, cols, col_at
    d = [derived[:, G2 * i:G2 * (i + 1)] for i in range(8)]
    C["log_a"], C["neg_log_a"], C["one_minus_lb"], C["lb"], C["one_minus_ka"], C["zero"] = d[0], d[1], d[2], d[3], d[4], d[7]
    own_a, own_v = sem("prep_act_own"), sem("prep_dve_own")
    with nc.Block() as block:
        @block.sync
        def _(sp):
            for dst, src in ((prm[:], D["prm"]), (cst[:], D["cst"]), (masks[:], D["masks"]), (lora[:], D["lora"]),
                             (lru_w[:], D["lru_w"])):
                sp.dma_start(dst, src).then_inc(C["loaded"], 16)

        @block.scalar
        def _(act):
            own = Own(act, own_a)
            act.wait_ge(C["loaded"], C["loaded_n"])
            own.done(act.activation(d[5], cols("lru_lam", G2), ACT.Abs))
            own.done(act.activation(d[5], d[5], ACT.Exp, scale=-1.0))
            own.done(act.activation(d[5], d[5], ACT.Ln, bias=1.0))

        @block.vector
        def _(dve):
            own = Own(dve, own_v)
            dve.wait_ge(C["loaded"], C["loaded_n"])
            own.done(dve.memset(d[7], 0.0))
            own.done(dve.tensor_scalar(d[6], cols("lru_lam", G2), -1.0, 0.0, ALU.mult, ALU.max))
            dve.wait_ge(own_a, 3)
            own.done(dve.tensor_tensor(d[6], d[6], d[5], ALU.add))
            own.done(dve.tensor_scalar(d[0], d[6], -LRU_C, None, ALU.mult))
            own.done(dve.tensor_scalar(d[1], d[6], LRU_C, None, ALU.mult))
            own.done(dve.tensor_tensor(d[3], cols("lb_param", G2), cols("lb_param", G2), ALU.subtract))
            own.done(dve.tensor_scalar(d[3], d[3], 0.0, None, ALU.max))
            own.done(dve.tensor_scalar(d[2], d[3], -1.0, 1.0, ALU.mult, ALU.add))
            own.done(dve.tensor_scalar(d[4], cols("rw_k_a", G2), -1.0, 1.0, ALU.mult, ALU.add))
            dve.memset(d[7], 0.0).then_inc(C["prepared"], 1)
    return C


def project_and_prepare(nc, ctx, D, C):
    with ExitStack() as mem:
        def sb(name, shape, dt=F32):
            return mem.enter_context(nc.sbuf_tensor(name, shape, dt))

        def bank(name, shape):
            return mem.enter_context(nc.psum_tensor(name, shape, F32))

        def sig(name, n=1, unit=1, seed=0):
            return Signal(nc.alloc_semaphore(name), n, unit, seed)

        WR = 3
        w_ring = sb("w_ring", [P, WR, D_MODEL])
        w_high, w_low = (sb("w_" + n, [P, WR, D_MODEL], F32R) for n in ("high", "low"))
        x_t = sb("x_t", [P, CB, D_MODEL])
        hn = [sb(f"hn_{n}", [P, KT, TB], F32R) for n in ("high", "low")]
        mean_sq = sb("mean_sq", [P, CB])
        rstd = sb("rstd", [P, CB])
        z = sb("z", [P, Z_TILES, 1 + TB])
        z_last = sb("z_last", [P, 1])
        bx = sb("bx", [P, G2, LRU_TAPS - 1 + TB])
        T = {n: sb("t_" + n, [P, G2, TB]) for n in (
            "by", "f", "q", "ag", "e", "k", "csig", "a", "kk", "b", "kp", "dg", "bonus", "sq", "inv",
            "xc", "gr", "gi", "decay")}
        T["cum"], T["h"] = T["e"], T["gi"]
        junk = T["f"][:].rearrange("p t n -> p (t n)")
        dz = T["inv"][:, 0]
        tok = sb("tok", [P, CB, 2 * G2 * P])
        v_tok = sb("v_tok", [P, CB, G2 * P])
        h_last = sb("h_last", [P, G2])
        turn = bank("turn", [P, 2, TB])
        proj = bank("proj", [P, 3, TB])
        aux_a = bank("aux_a", [P, 2, TB])
        aux_v = bank("aux_v", [P, TB])
        col, ident, headones, ones = C["col"], C["ident"], C["headones"], C["ones"]
        chunk_start = C["reset"]

        TOK = NF - 2 * G2
        NA = 10 + 2 * G2
        x_in = sig("x_in", 1, 16)
        w_high_ready, w_split = sig("w_high_ready", NF), sig("w_split", NF)
        w_in = [sig(f"w_in{s}", len(range(s, NF, WR)), 16) for s in range(WR)]
        sumsq, ms_ready, root, xn_ready = sig("sumsq"), sig("ms_ready"), sig("root"), sig("xn_ready")
        turned, hn_ready = sig("turned", KT), sig("hn_ready", KT)
        proj_done, proj_out = sig("proj_done", NF, 1, 1), sig("proj_out", NF, 1, 1)
        aux_done, aux_out = sig("aux_done", NA), sig("aux_out", NA, 1, 1)
        vaux_done, vaux_out = sig("vaux_done", 7, 1, 1), sig("vaux_out", 7, 1, 1)
        z_mixed, lat_act, k_sq, ss_root, rk_ready = (sig("z_mixed", Z_TILES), sig("lat_act"), sig("k_sq", G2),
                                                     sig("ss_root"), sig("rk_ready", G2))
        conv_done, a_ready, th_ready, om_ready, om_root = (sig("conv_done", 1, 1, 1), sig("a_ready", G2),
                                                           sig("th_ready", G2), sig("om_ready", G2), sig("om_root", G2))
        lf_done, csig_done = sig("lf_done"), sig("csig_done", G2)
        f_clamped, f_log, lb_log = sig("f_clamped"), sig("f_log"), sig("lb_log")
        out_b, out_b_sq, b_root = sig("out_b"), sig("out_b_sq"), sig("b_root")
        r_stored = sig("r_stored", G2, 16, 1)
        dve_end = sig("dve_end", 1, 1, 1)
        stored = sig("stored", (len(SCAN) + 3) * G2 + 3, 16, 1)
        dve_own, act_own = sig("s1_dve_own").sem, sig("s1_act_own").sem
        norm_dve, norm_act, gain_dve = (sig(n).sem for n in ("norm_dve_own", "norm_act_own", "gain_dve_own"))
        s1_hold = sig("s1_hold").sem
        block = mem.enter_context(nc.Block())

        def blocks(fori, run):
            with fori(0, NB - 1) as p:
                run(p, True)
            run(NB - 1, False)

        @block.sync
        def _(sp):
            def load_x(p):
                sp.dma_start(x_t[:], D["x"][bass.ds(p * TB, TB)].rearrange("(j p) n -> p j n", p=P)).then_inc(x_in.sem, 16)

            def load_w(n):
                sp.dma_start(w_ring[:, n % WR], D["w_feat"][n].rearrange("p k n -> p (k n)")).then_inc(w_in[n % WR].sem, 16)

            load_x(0)
            for n in range(WR):
                load_w(n)

            def results(p):
                at = bass.ds(p * CB, CB)
                for part, names in (("scan", SCAN), ("late", LATE[:4])):
                    for a, name in enumerate(names):
                        for t in range(G2 if name != "r" else 0):
                            src = T["h" if name == "yb" else name][:, t]
                            yield D[part][at, :, a, t].rearrange("c p n -> p c n"), src.rearrange("p (c n) -> p c n", c=CB)
                for name, src in (("va", tok[:, :, 0:G2 * P]), ("cu", tok[:, :, G2 * P:]), ("vd", v_tok[:])):
                    yield D[name][at].rearrange("c p n -> p c n"), src

            def store(results):
                for out, src in results:
                    sp.dma_start(out, src).then_inc(stored.sem, 16)

            def run(p, has_next, has_before=True):
                if has_before:
                    sp.wait_ge(*dve_end.at(p - 1))
                    sp.sem_inc(s1_hold, 1)
                    left = list(results(p - 1))
                if has_next:
                    sp.wait_ge(*turned.at(p))
                    sp.sem_inc(s1_hold, 1)
                    load_x(p + 1)
                for n in range(WR, NF + (WR if has_next else 0)):
                    sp.wait_ge(*proj_done.at(p, n - WR))
                    load_w(n % NF)
                    if has_before and n < WR + 5:
                        store(left[(n - WR) * 5:(n - WR + 1) * 5])
                    if n == 9:
                        sp.wait_ge(*z_mixed.at(p, 4))
                        sp.sem_inc(s1_hold, 1)
                        for t in range(G2):
                            out = D["scan"][bass.ds(p * CB, CB), :, SCAN.index("r"), t].rearrange("c p n -> p c n")
                            sp.dma_start(out, z[:, 3 + t, 1:].rearrange("p (c n) -> p c n", c=CB)).then_inc(r_stored.sem, 16)

            r_stored.seed_by(sp)
            stored.seed_by(sp)
            run(0, True, False)
            with nc.sync.Fori(1, NB - 1) as p:
                run(p, True)
            run(NB - 1, False)
            sp.wait_ge(*dve_end.at(NB - 1))
            store(results(NB - 1))
            sp.wait_ge(*stored.at(NB - 1))
            sp.wait_ge(*r_stored.at(NB - 1))

        def late_tile(m):
            return T["a" if m < G2 else "f"][:, m % G2]

        @block.gpsimd
        def _(pool):
            def run(p, has_next):
                for n in range(NF):
                    pool.wait_ge(*w_high_ready.at(p, n))
                    pool.tensor_tensor(w_low[:, n % WR], w_ring[:, n % WR], w_high[:, n % WR], ALU.subtract).then_inc(w_split.sem, 1)

            blocks(nc.gpsimd.Fori, run)

        @block.tensor
        def _(pe):
            for s in (proj_done, vaux_done):
                s.seed_by(pe)
            pe.wait_ge(C["loaded"], C["loaded_n"])

            def turn_block(p):
                pe.wait_ge(*xn_ready.at(p))
                for k in range(KT):
                    if k >= 2:
                        pe.wait_ge(*hn_ready.at(p, k - 2))
                    for j in range(CB):
                        mm = pe.transpose(turn[:, k % 2, j * P:(j + 1) * P], x_t[:, j, k * P:(k + 1) * P], ident)
                    mm.then_inc(turned.sem, 1)

            def run(p, has_next):

                def for_act(m, lhs, rhs):
                    pe.wait_ge(*(aux_out.at(p, m - 2) if m >= 2 else aux_out.at(p, m + NA - 2, back=1)))
                    pe.matmul(aux_a[:, m % 2], lhs, rhs, start=True, stop=True).then_inc(aux_done.sem, 1)

                def dve_bank_free(m):
                    pe.wait_ge(*(vaux_out.at(p, m - 1) if m else vaux_out.at(p, back=1)))

                def small_products(n):
                    if n == 6:
                        pe.wait_ge(*lat_act.at(p))
                        for m in range(6):
                            for_act(m, C["lora"][:, m], z[:, 0, 1:])
                    if n in (9, 10):
                        t = n - 9
                        pe.wait_ge(*k_sq.at(p, t))
                        dve_bank_free(t)
                        pe.matmul(aux_v[:], headones, T["sq"][:, t], start=True, stop=True).then_inc(vaux_done.sem, 1)
                    if n == 11:
                        pe.wait_ge(*conv_done.at(p))
                        for m in range(4):
                            for_act(6 + m, C["lru_w"][:, m], T["xc"][:, m % 2])
                    if n in (14, 15):
                        t = n - 14
                        pe.wait_ge(*rk_ready.at(p, t))
                        dve_bank_free(2 + t)
                        pe.matmul(aux_v[:], headones, T["sq"][:, t], start=True, stop=True).then_inc(vaux_done.sem, 1)
                    if n in (16, 17):
                        t = n - 16
                        dve_bank_free(4 + t)
                        for j in range(CB):
                            mm = pe.transpose(aux_v[:, j * P:(j + 1) * P], z[:, 5 + t, 1 + j * P:1 + (j + 1) * P], ident)
                        mm.then_inc(vaux_done.sem, 1)

                def with_tokens_across(m):
                    pe.wait_ge(*proj_out.at(p, TOK + m))
                    pe.wait_ge(*aux_out.at(p, 10 + m - 2))
                    for j in range(CB):
                        mm = pe.transpose(aux_a[:, m % 2, j * P:(j + 1) * P], late_tile(m)[:, j * P:(j + 1) * P], ident)
                    mm.then_inc(aux_done.sem, 1)

                for n in range(NF):
                    pe.wait_ge(*(proj_out.at(p, n - 3) if n >= 3 else proj_out.at(p, NF - 3 + n, back=1)))
                    pe.wait_ge(*w_split.at(p, n))
                    for k in range(KT):
                        if n == 0:
                            pe.wait_ge(*hn_ready.at(p, k))
                        at = slice(k * P, (k + 1) * P)
                        for i, (lhs, rhs) in enumerate(((w_high[:, n % WR, at], hn[0]), (w_high[:, n % WR, at], hn[1]),
                                                        (w_low[:, n % WR, at], hn[0]))):
                            mm = pe.matmul(proj[:, n % 3], lhs, rhs[:, k], start=k == i == 0, stop=k == KT - 1 and i == 2)
                    mm.then_inc(proj_done.sem, 1)
                    small_products(n)
                    if n > TOK:
                        with_tokens_across(n - 1 - TOK)
                with_tokens_across(2 * G2 - 1)
                if has_next:
                    turn_block(p + 1)
                pe.wait_ge(*out_b_sq.at(p))
                dve_bank_free(6)
                for t in range(G2):
                    mm = pe.matmul(aux_v[:], ones, T["sq"][:, t], start=t == 0, stop=t == G2 - 1)
                mm.then_inc(vaux_done.sem, 1)

            turn_block(0)
            blocks(nc.tensor.Fori, run)

        @block.scalar
        def _(act):
            for s in (proj_out, aux_out):
                s.seed_by(act)
            act.wait_ge(C["prepared"], 1)

            def squares(p):
                own = Own(act, norm_act, p, CB - 1)
                act.wait_ge(*x_in.at(p))
                for j in range(CB):
                    own.done(act.activation(junk, x_t[:, j], ACT.Square, accum_out=mean_sq[:, j:j + 1]),
                             *((sumsq,) if j == CB - 1 else ()))
                own.check()

            def high(p, n):
                act.wait_ge(*w_in[n % WR].at(p, n // WR))
                act.activation(w_high[:, n % WR], w_ring[:, n % WR], ACT.Copy).then_inc(w_high_ready.sem, 1)

            def norm_root(p):
                act.wait_ge(*ms_ready.at(p))
                act.activation(rstd[:], mean_sq[:], ACT.Sqrt).then_inc(root.sem, 1)

            ACT_OWN = 6

            def run(p, has_next):
                own = Own(act, act_own, p, ACT_OWN)
                act.wait_ge(*dve_end.at(p, back=1))
                act.wait_ge(*vaux_done.at(p, back=1))

                def take(n, dst, func=ACT.Copy):
                    if n + 2 < NF:
                        high(p, n + 2)
                    act.wait_ge(*proj_done.at(p, n))
                    own.done(act.activation(dst, proj[:, n % 3], func), proj_out, n)

                def take_small(m, dst, func, bias=0.0):
                    act.wait_ge(*aux_done.at(p, m))
                    own.done(act.activation(dst, aux_a[:, m % 2], func, bias=bias), aux_out, m)

                for n in range(Z_TILES):
                    if n == 3:
                        act.wait_ge(*r_stored.at(p, back=1))
                    take(n, z[:, n, 1:])
                    if n == 3:
                        act.wait_ge(*z_mixed.at(p, 0))
                        own.done(act.activation(z[0:32, 0, 1:], z[0:32, 0, 1:], ACT.Tanh))
                        own.done(act.activation(z[64:128, 0, 1:], z[64:128, 0, 1:], ACT.Sigmoid), lat_act)
                for t in range(G2):
                    take_small(t, T["decay"][:, t], ACT.Sigmoid, col("rw_w0", t))
                for t in range(G2):
                    take_small(2 + t, T["a"][:, t], ACT.Sigmoid, col("rw_a0", t))
                act.wait_ge(*stored.at(p, back=1))
                for t in range(G2):
                    take_small(4 + t, T["dg"][:, t], ACT.Copy)
                for t in range(G2):
                    take(7 + t, bx[:, t, LRU_TAPS - 1:])
                for t in range(G2):
                    act.wait_ge(*z_mixed.at(p, 1 + t))
                    own.done(act.activation(T["sq"][:, t], z[:, 1 + t, 1:], ACT.Square, scale=col("rw_k_k", t)), k_sq, t)
                if has_next:
                    squares(p + 1)
                for t in range(G2):
                    take(9 + t, T["by"][:, t], ACT.Gelu_apprx_tanh)
                act.wait_ge(*vaux_out.at(p, 1))
                own.done(act.activation(T["inv"][:], T["inv"][:], ACT.Sqrt), ss_root)
                if has_next:
                    norm_root(p + 1)
                for m in range(2 * G2):
                    take_small(6 + m, T["gr" if m < G2 else "gi"][:, m % G2], ACT.Sigmoid,
                               col("lru_ba" if m < G2 else "lru_bx", m % G2))
                for t in range(G2):
                    take(11 + t, T["f"][:, t])
                own.done(act.activation(T["k"][:], T["f"][:], ACT.Sigmoid, scale=-1.0))
                for t in range(G2):
                    act.activation(T["k"][:, t], T["k"][:, t], ACT.Copy, scale=C["one_minus_lb"][:, t:t + 1])
                own.done(act.activation(T["e"][:], T["f"][:], ACT.Abs))
                own.done(act.activation(T["e"][:], T["e"][:], ACT.Exp, scale=-1.0))
                act.wait_ge(*f_clamped.at(p))
                own.done(act.activation(T["ag"][:], T["ag"][:], ACT.Exp, scale=-1.0))
                for t in range(G2):
                    act.wait_ge(*csig_done.at(p, t))
                    act.activation(T["decay"][:, t], T["gr"][:, t], ACT.Exp, scale=C["log_a"][:, t:t + 1]).then_inc(a_ready.sem, 1)
                own.done(act.activation(T["e"][:], T["e"][:], ACT.Ln, bias=1.0), f_log)
                for t in range(G2):
                    last = act.activation(T["ag"][:, t], T["ag"][:, t], ACT.Ln, bias=1.0, scale=C["lb"][:, t:t + 1])
                own.done(last, lb_log)
                for t in range(G2):
                    own.done(act.activation(T["gr"][:, t], T["gr"][:, t], ACT.Tanh, scale=C["neg_log_a"][:, t:t + 1]),
                             th_ready, t)
                for t in range(G2):
                    take(13 + t, T["q"][:, t], ACT.Silu)
                act.wait_ge(*lf_done.at(p))
                for t in range(G2):
                    take(15 + t, T["ag"][:, t], ACT.Silu)
                take(TOK, late_tile(0))
                for m in range(2 * G2):
                    if m + 1 < 2 * G2:
                        take(TOK + m + 1, late_tile(m + 1))
                    act.wait_ge(*aux_done.at(p, 10 + m))
                    if m == 2 * G2 - 1 and has_next:
                        for n in range(2):
                            high(p + 1, n)
                    own.done(act.activation(tok[:, :, m * P:(m + 1) * P], aux_a[:, m % 2].rearrange("p (j n) -> p j n", j=CB),
                                            ACT.Copy), aux_out, 10 + m)
                for t in range(G2):
                    act.wait_ge(*om_ready.at(p, t))
                    own.done(act.activation(T["gr"][:, t], T["gr"][:, t], ACT.Sqrt), om_root, t)
                act.wait_ge(*out_b.at(p))
                for t in range(G2):
                    own.done(act.activation(T["sq"][:, t], T["h"][:, t], ACT.Square), *((out_b_sq,) if t else ()))
                act.wait_ge(*vaux_out.at(p, 6))
                own.done(act.activation(T["inv"][:, 0], T["inv"][:, 0], ACT.Sqrt), b_root)
                own.check()

            squares(0)
            norm_root(0)
            for n in range(2):
                high(0, n)
            blocks(nc.scalar.Fori, run)

        @block.vector
        def _(dve):
            for s in (vaux_out, conv_done, dve_end):
                s.seed_by(dve)
            dve.wait_ge(C["prepared"], 1)
            start = Own(dve, sig("s1_dve_start").sem)
            start.done(dve.memset(z[:, :, 0:1], 0.0))
            start.done(dve.memset(bx[:, :, 0:LRU_TAPS - 1], 0.0))
            start.done(dve.memset(h_last[:], 0.0))

            def mean_square(p):
                dve.wait_ge(*sumsq.at(p))
                dve.tensor_scalar(mean_sq[:], mean_sq[:], 1.0 / D_MODEL, EPS, ALU.mult, ALU.add).then_inc(ms_ready.sem, 1)

            def scale_block(p):
                own = Own(dve, norm_dve, p, 1)
                dve.wait_ge(*root.at(p))
                own.done(dve.reciprocal(rstd[:], rstd[:]))
                for j in range(CB):
                    last = dve.tensor_scalar(x_t[:, j], x_t[:, j], rstd[:, j:j + 1], None, ALU.mult)
                last.then_inc(xn_ready.sem, 1)

            def gained(p):
                own = Own(dve, gain_dve, p, KT)
                for k in range(KT):
                    dve.wait_ge(*turned.at(p, k))
                    own.done(dve.tensor_scalar(hn[0][:, k], turn[:, k % 2], col("mix_norm", k), None, ALU.mult))
                    dve.scalar_tensor_tensor(hn[1][:, k], turn[:, k % 2], col("mix_norm", k), hn[0][:, k], ALU.mult,
                                             ALU.subtract).then_inc(hn_ready.sem, 1)

            def run(p, has_next):
                own = Own(dve, dve_own, p, 60)
                for n in range(Z_TILES):
                    if n == 3:
                        dve.wait_ge(*r_stored.at(p, back=1))
                    dve.wait_ge(*proj_out.at(p, n))
                    own.done(dve.tensor_copy(z_last[:], z[:, n, TB:]))
                    own.done(dve.tensor_tensor(dz[:], z[:, n, 0:TB], z[:, n, 1:], ALU.subtract))
                    own.done(dve.tensor_copy(z[:, n, 0:1], z_last[:]))
                    own.done(dve.scalar_tensor_tensor(z[:, n, 1:], dz[:], col("rw_mu", n), z[:, n, 1:], ALU.mult, ALU.add),
                             z_mixed, n)
                for t in range(G2):
                    dve.wait_ge(*proj_out.at(p, 7 + t))
                    xc = T["xc"][:, t]
                    last = LRU_TAPS - 1
                    own.done(dve.tensor_scalar(xc, bx[:, t, last:last + TB], col(f"lru_conv_w{last}", t), col("lru_conv_b", t),
                                               ALU.mult, ALU.add))
                    for tap in range(last):
                        own.done(dve.scalar_tensor_tensor(xc, bx[:, t, tap:tap + TB], col(f"lru_conv_w{tap}", t), xc,
                                                          ALU.mult, ALU.add))
                own.done(dve.tensor_copy(bx[:, :, 0:LRU_TAPS - 1], bx[:, :, TB:]), conv_done)
                dve.wait_ge(*stored.at(p, back=1))
                for t in range(G2):
                    dve.wait_ge(*aux_out.at(p, t))
                    own.done(dve.tensor_tensor_scan(T["csig"][:, t], chunk_start, T["decay"][:, t], 0.0, ALU.mult, ALU.add),
                             csig_done, t)
                if has_next:
                    mean_square(p + 1)
                for t in range(G2):
                    dve.wait_ge(*vaux_done.at(p, t))
                    own.done(dve.tensor_scalar(T["inv"][:, t], aux_v[:], 1e-24, None, ALU.max), vaux_out, t)
                for t in range(G2):
                    k = z[:, 1 + t, 1:]
                    dve.wait_ge(*ss_root.at(p))
                    own.done(dve.reciprocal(T["inv"][:, t], T["inv"][:, t]))
                    own.done(dve.scalar_tensor_tensor(T["kk"][:, t], k, col("rw_k_k", t), T["inv"][:, t], ALU.mult, ALU.mult))
                    dve.wait_ge(*aux_out.at(p, 2 + t))
                    own.done(dve.tensor_tensor(T["b"][:, t], T["kk"][:, t], T["a"][:, t], ALU.mult))
                    own.done(dve.tensor_scalar(T["a"][:, t], T["a"][:, t], col("rw_k_a", t), C["one_minus_ka"][:, t:t + 1],
                                               ALU.mult, ALU.add))
                    own.done(dve.tensor_tensor(T["kp"][:, t], k, T["a"][:, t], ALU.mult))
                    own.done(dve.scalar_tensor_tensor(T["sq"][:, t], z[:, 3 + t, 1:], col("rw_r_k", t), T["kp"][:, t],
                                                      ALU.mult, ALU.mult), rk_ready, t)
                if has_next:
                    scale_block(p + 1)
                for t in range(G2):
                    dve.wait_ge(*proj_out.at(p, 11 + t))
                    own.done(dve.tensor_scalar(T["ag"][:, t], T["f"][:, t], -40.0, None, ALU.max),
                             *((f_clamped,) if t else ()))
                for t in range(G2):
                    dve.wait_ge(*vaux_done.at(p, 2 + t))
                    own.done(dve.tensor_tensor(T["bonus"][:, t], z[:, 5 + t, 1:], aux_v[:], ALU.mult), vaux_out, 2 + t)
                dve.wait_ge(*f_log.at(p))
                for t in range(G2):
                    own.done(dve.scalar_tensor_tensor(T["e"][:, t], T["f"][:, t], 0.0, T["e"][:, t], ALU.min, ALU.subtract))
                dve.wait_ge(*lb_log.at(p))
                for t in range(G2):
                    own.done(dve.tensor_tensor(T["e"][:, t], T["e"][:, t], T["ag"][:, t], ALU.add),
                             *((lf_done,) if t else ()))
                for t in range(G2):
                    own.done(dve.tensor_tensor_scan(T["cum"][:, t], chunk_start, T["e"][:, t], 0.0, ALU.mult, ALU.add))
                for t in range(G2):
                    dve.wait_ge(*th_ready.at(p, t))
                    own.done(dve.tensor_tensor(T["inv"][:, t], T["decay"][:, t], T["decay"][:, t], ALU.mult))
                    own.done(dve.scalar_tensor_tensor(T["gr"][:, t], T["inv"][:, t], 1.0, T["gr"][:, t], ALU.add, ALU.mult),
                             om_ready, t)
                    own.done(dve.tensor_tensor(T["xc"][:, t], T["xc"][:, t], T["gi"][:, t], ALU.mult))
                for t in range(G2):
                    dve.wait_ge(*vaux_done.at(p, 4 + t))
                    own.done(dve.tensor_copy(v_tok[:, :, t * P:(t + 1) * P], aux_v[:].rearrange("p (j n) -> p j n", j=CB)),
                             vaux_out, 4 + t)
                if has_next:
                    gained(p + 1)
                for t in range(G2):
                    dve.wait_ge(*om_root.at(p, t))
                    own.done(dve.tensor_tensor(T["xc"][:, t], T["xc"][:, t], T["gr"][:, t], ALU.mult))
                    own.done(dve.tensor_tensor_scan(T["h"][:, t], T["decay"][:, t], T["xc"][:, t], h_last[:, t:t + 1],
                                                    ALU.mult, ALU.add))
                    own.done(dve.tensor_copy(h_last[:, t:t + 1], T["h"][:, t, TB - 1:TB]))
                    own.done(dve.tensor_tensor(T["h"][:, t], T["h"][:, t], T["by"][:, t], ALU.mult),
                             *((out_b,) if t else ()))
                for t in range(G2):
                    dve.wait_ge(*proj_out.at(p, 15 + t))
                    own.done(dve.tensor_scalar(T["ag"][:, t], T["ag"][:, t], col("hg_norm", t), None, ALU.mult))
                dve.wait_ge(*vaux_done.at(p, 6))
                own.done(dve.tensor_scalar(T["inv"][:, 0], aux_v[:], 1.0 / (G2 * P), EPS, ALU.mult, ALU.add), vaux_out, 6)
                dve.wait_ge(*b_root.at(p))
                own.done(dve.reciprocal(T["inv"][:, 0], T["inv"][:, 0]))
                for t in range(G2):
                    own.done(dve.scalar_tensor_tensor(T["h"][:, t], T["h"][:, t], col("lru_norm", t), T["inv"][:, 0],
                                                      ALU.mult, ALU.mult), *((dve_end,) if t else ()))
                own.check()

            mean_square(0)
            scale_block(0)
            gained(0)
            blocks(nc.vector.Fori, run)


def scan_chunks(nc, ctx, D, C):
    with ExitStack() as mem:
        def sb(name, shape, dt=F32):
            return mem.enter_context(nc.sbuf_tensor(name, shape, dt))

        def bank(name, shape):
            return mem.enter_context(nc.psum_tensor(name, shape, F32))

        def sig(name, n=1, unit=1, seed=0):
            return Signal(nc.alloc_semaphore(name), n, unit, seed)

        H = G2 * 2
        NL = len(LEVELS)
        MID = TC // 2 - 1
        feats = [sb(f"feats{u}", [P, len(SCAN) - 1, G2, TC]) for u in range(2)]
        cs = [sb(f"cs{u}", [P, G2, 1 + TC]) for u in range(2)]
        va = [sb(f"va{u}", [P, G2 * P]) for u in range(2)]
        vd = [sb(f"vd{u}", [P, G2 * P]) for u in range(2)]
        halves = [sb(f"halves{u}", [P, NL, G2, TC]) for u in range(2)]
        e_from = [sb(f"e_from{u}", [P, G2, 1 + TC]) for u in range(2)]
        e_to = [sb(f"e_to{u}", [P, G2, TC]) for u in range(2)]
        kr = [sb(f"kr{u}", [P, G2, 2, TC]) for u in range(2)]
        bk = [sb(f"bk{u}", [P, 2, G2, TC]) for u in range(2)]
        qc = [sb(f"qc{u}", [P, G2, TC]) for u in range(2)]
        kc = [sb(f"kc{u}", [P, G2, TC]) for u in range(2)]
        small = [sb(f"small{u}", [P, 6, G2]) for u in range(2)]
        scores_d = sb("scores_d", [P, H, 4, TC])
        scores_a = sb("scores_a", [P, 2, G2, TC])
        off = sb("off", [P, NL, H, TC])
        invs = sb("invs", [P, 2, 2, 2, TC])
        w = sb("w", [P, H, TC])
        bk_tok = sb("bk_tok", [P, 2, G2, TC])
        kc_tok = sb("kc_tok", [P, G2, TC])
        rhs = sb("rhs", [P, G2 * P])
        sa = sb("sa", [P, G2 * P])
        state_a = sb("state_a", [P, G2, P])
        state_d = sb("state_d", [P, G2, P])
        state_mid = sb("state_mid", [P, G2, P])
        grown = sb("grown", [P, G2, P])
        grown_a = sb("grown_a", [P, G2, P])
        oy = [sb(f"oy{u}", [P, 2, G2, TC]) for u in range(2)]
        ps_a = bank("ps_a", [P, 2, 2, G2, TC])
        ps_d = bank("ps_d", [P, H, 4 * TC])
        ps_s = bank("ps_s", [P, 4 * TC])
        ps_o = bank("ps_o", [P, 4 * TC])
        ps_y, ps_x = (ps_d[:, 0], ps_d[:, 1]), (ps_d[:, 2], ps_d[:, 3])

        def inv(h):
            return invs[:, h // 2, 0, h % 2]

        def inv_t(h):
            return invs[:, h // 2, 1, h % 2]

        ident, headones, masks = C["ident"], C["headones"], C["masks"]
        Q, K, CUM, R, KP, KK, B = range(len(SCAN) - 1)

        loaded = [sig(f"loaded{u}", 4, 16) for u in range(2)]
        mids, small_exp, exp_d, kr_ready = (sig(n) for n in ("mids", "small_exp", "exp_d", "kr_ready"))
        exponents, exp_a, halves_ready, exp_qk, qk_ready = (sig(n) for n in (
            "exponents", "exp_a", "halves_ready", "exp_qk", "qk_ready"))
        pe_done = sig("pe_done", 1, 1, 2)
        pairs_d, scored_d = sig("pairs_d", 2), sig("scored_d", 2)
        bk_turned, bk_out, kc_turned, kc_out = (sig(n) for n in ("bk_turned", "bk_out", "kc_turned", "kc_out"))
        off_ready, first_inv, inv_turned, inv_out = sig("off_ready", NL), sig("first_inv"), sig("inv_turned"), sig("inv_out")
        NS = 2 * (NL - 1)
        y_done, w_ready, x_done, x_out = sig("y_done", NS), sig("w_ready", NS), sig("x_done", NS), sig("x_out", NS, 1, 1)
        pairs_a, scored_a = sig("pairs_a", 4), sig("scored_a", 4, 1, 1)
        mid_ready, states = sig("mid_ready"), sig("states", 1, 1, 1)
        rhs_done, rhs_ready, sa_done, sa_ready, ds_done = (sig(n) for n in (
            "rhs_done", "rhs_ready", "sa_done", "sa_ready", "ds_done"))
        oy_out = sig("oy_out", 1, 1, 1)
        stored = [sig(f"oy_stored{u}", 1, 16, 1) for u in range(2)]
        own = {n: sig("s2_own_" + n).sem for n in ("act", "act_prep", "dve", "dve_prep", "pool", "pool_prep", "start", "hold")}
        block = mem.enter_context(nc.Block())

        def chunks(fori, prepare, run):
            prepare(0, 0, 0)
            with fori(0, NCH // 2 - 1) as i:
                run(2 * i, i, 0, (2 * i + 1, i, 1))
                run(2 * i + 1, i, 1, (2 * i + 2, i + 1, 0))
            i = NCH // 2 - 1
            run(2 * i, i, 0, (2 * i + 1, i, 1))
            run(2 * i + 1, i, 1, None)

        @block.sync
        def _(sp):
            for s in stored:
                s.seed_by(sp)

            def load(p, i, u):
                sp.wait_ge(*pe_done.at(p, back=2))
                at = bass.ds(p, 1)
                for dst, src in ((feats[u][:], D["scan"][at, :, 0:len(SCAN) - 1]), (cs[u][:, :, 1:], D["scan"][at, :, len(SCAN) - 1]),
                                 (va[u][:], D["va"][at]), (vd[u][:], D["vd"][at])):
                    names = " ".join("bcd"[:len(src.shape) - 2])
                    sp.dma_start(dst, src.rearrange(f"a p {names} -> (a p) {names}")).then_inc(loaded[u].sem, 16)

            def run(p, i, u, following):
                if following:
                    load(*following)
                sp.wait_ge(*oy_out.at(p))
                sp.dma_start(D["oy"][bass.ds(p, 1)].rearrange("a p k t n -> (a p) k t n"), oy[u][:]).then_inc(stored[u].sem, 16)

            chunks(nc.sync.Fori, load, run)
            for s in stored:
                sp.wait_ge(*s.at(NCH // 2 - 1))

        @block.gpsimd
        def _(pool):
            def prepare(p, i, u):
                me = Own(pool, own["pool_prep"], p, 0)
                pool.wait_ge(*loaded[u].at(i))
                pool.wait_ge(*pe_done.at(p, back=2))
                q, k, cum = feats[u][:, Q], feats[u][:, K], feats[u][:, CUM]

                def sides(x, b):
                    x = x.rearrange("p t (g h b) -> p t g h b", h=2, b=b)
                    return x[:, :, :, 0], x[:, :, :, 1]

                for m, b in enumerate(LEVELS):
                    (c0, c1), (x0, x1) = sides(cum, b), sides(halves[u][:, m], b)
                    middle = c0[:, :, :, b - 1:b].broadcast_to([P, G2, TC // (2 * b), b])
                    pool.tensor_tensor(x0, middle, c0, ALU.subtract)
                    last = pool.tensor_tensor(x1, c1, middle, ALU.subtract)
                last.then_inc(exponents.sem, 1)
                pool.wait_ge(*exp_a.at(p))
                for m, b in enumerate(LEVELS):
                    (k0, _), (_, q1), (x0, x1) = sides(k, b), sides(q, b), sides(halves[u][:, m], b)
                    pool.tensor_tensor(x0, x0, k0, ALU.mult)
                    last = pool.tensor_tensor(x1, x1, q1, ALU.mult)
                me.done(last, halves_ready)

            def run(p, i, u, following):
                pool.wait_ge(*scored_d.at(p, 1))
                for m in range(NL):
                    mask = masks[:, NL - 1 - m:NL - m].broadcast_to([P, H, TC])
                    pool.tensor_tensor(off[:, m], scores_d[:, :, 0], mask, ALU.mult).then_inc(off_ready.sem, 1)
                if following:
                    prepare(*following)

            pool.wait_ge(C["loaded"], C["loaded_n"])
            chunks(nc.gpsimd.Fori, prepare, run)

        @block.scalar
        def _(act):
            act.wait_ge(C["prepared"], 1)

            def prepare_d(p, i, u):
                me = Own(act, own["act_prep"], p, 0)
                act.wait_ge(*mids.at(p))
                s = small[u]
                for t in range(G2):
                    act.activation(e_from[u][:, t], cs[u][:, t], ACT.Exp, bias=s[:, 0, t:t + 1], scale=DECAY)
                    act.activation(e_to[u][:, t], cs[u][:, t, 1:], ACT.Exp, bias=s[:, 1, t:t + 1], scale=-DECAY)
                act.activation(s[:, 3], s[:, 1], ACT.Exp)
                act.activation(s[:, 4], s[:, 2], ACT.Exp, scale=DECAY).then_inc(exp_d.sem, 1)
                return me

            def prepare_a(p, i, u):
                cum = feats[u][:, CUM]
                act.wait_ge(*pe_done.at(p, back=2))
                act.activation(qc[u][:], cum, ACT.Exp)
                for t in range(G2):
                    act.activation(kc[u][:, t], cum[:, t], ACT.Exp, bias=cum[:, t, TC - 1:TC], scale=-1.0)
                act.activation(small[u][:, 5], cum[:, :, TC - 1], ACT.Exp).then_inc(exp_qk.sem, 1)
                act.wait_ge(*exponents.at(p))
                act.activation(halves[u][:], halves[u][:], ACT.Exp).then_inc(exp_a.sem, 1)

            def prepare(p, i, u):
                act.wait_ge(*loaded[u].at(i))
                prepare_d(p, i, u)
                prepare_a(p, i, u)

            def run(p, i, u, following):
                act.wait_ge(*bk_turned.at(p))
                act.activation(bk_tok[:].rearrange("p a t n -> p (a t n)"), ps_s[:], ACT.Copy).then_inc(bk_out.sem, 1)
                act.wait_ge(*kc_turned.at(p))
                act.activation(kc_tok[:].rearrange("p t n -> p (t n)"), ps_o[:, 0:G2 * TC], ACT.Copy).then_inc(kc_out.sem, 1)
                act.wait_ge(*inv_turned.at(p))
                for g in range(2):
                    last = act.activation(invs[:, g, 0].rearrange("p h n -> p (h n)"), ps_x[g][:, 0:2 * TC], ACT.Copy)
                last.then_inc(inv_out.sem, 1)
                for s in range(NS):
                    g = s % 2
                    first = 0 if s < NS - 2 else 1
                    act.wait_ge(*x_done.at(p, s))
                    act.activation(invs[:, g, first:].rearrange("p a h n -> p (a h n)"), ps_x[g][:, 2 * TC * first:],
                                   ACT.Copy).then_inc(x_out.sem, 1)
                    if s == 1 and following:
                        act.wait_ge(*loaded[following[2]].at(following[1]))
                        prepare_d(*following)
                    if s == 5 and following:
                        prepare_a(*following)
                act.wait_ge(*rhs_done.at(p))
                act.activation(rhs[:], ps_s[:, 0:G2 * P], ACT.Copy, scale=-1.0).then_inc(rhs_ready.sem, 1)
                act.wait_ge(*sa_done.at(p))
                act.activation(sa[:], ps_s[:, G2 * P:], ACT.Copy).then_inc(sa_ready.sem, 1)
                act.wait_ge(*pe_done.at(p))
                act.wait_ge(*stored[u].at(i, back=1))
                act.activation(oy[u][:].rearrange("p k t n -> p (k t n)"), ps_o[:], ACT.Copy).then_inc(oy_out.sem, 1)

            oy_out.seed_by(act)
            x_out.seed_by(act)
            chunks(nc.scalar.Fori, prepare, run)

        @block.vector
        def _(dve):
            start = Own(dve, own["start"])
            dve.wait_ge(C["prepared"], 1)
            for x in (state_a[:], state_d[:], scores_a[:], scores_d[:], cs[0][:, :, 0:1], cs[1][:, :, 0:1]):
                last = dve.memset(x, 0.0)
            start.done(last)
            scored_a.seed_by(dve)
            states.seed_by(dve)

            def hold(sem, value):
                dve.wait_ge(sem, value)
                dve.sem_inc(own["hold"], 1)

            def prepare_mid(p, i, u):
                dve.wait_ge(*loaded[u].at(i))
                dve.wait_ge(*pe_done.at(p, back=2))
                mid, s = cs[u][:, :, 1 + MID], small[u]
                dve.tensor_scalar(s[:, 0], mid, -DECAY, None, ALU.mult)
                dve.tensor_scalar(s[:, 1], mid, DECAY, None, ALU.mult)
                dve.tensor_tensor(s[:, 2], cs[u][:, :, TC], mid, ALU.subtract).then_inc(mids.sem, 1)

            def prepare_rest(p, i, u):
                f = feats[u]
                dve.wait_ge(*exp_d.at(p))
                dve.tensor_tensor(kr[u][:, :, 0], f[:, KK], e_from[u][:, :, 0:TC], ALU.mult)
                dve.tensor_tensor(kr[u][:, :, 1], f[:, R], e_from[u][:, :, 1:], ALU.mult)
                dve.tensor_tensor(bk[u][:, 0], f[:, B], e_to[u][:], ALU.mult)
                dve.tensor_tensor(bk[u][:, 1], f[:, KP], e_to[u][:], ALU.mult).then_inc(kr_ready.sem, 1)
                dve.wait_ge(*exp_qk.at(p))
                dve.tensor_tensor(qc[u][:], qc[u][:], f[:, Q], ALU.mult)
                dve.tensor_tensor(kc[u][:], kc[u][:], f[:, K], ALU.mult).then_inc(qk_ready.sem, 1)

            def prepare(p, i, u):
                prepare_mid(p, i, u)
                prepare_rest(p, i, u)

            def run(p, i, u, following):
                me = Own(dve, own["dve"], p, 5)
                s = small[u]
                dve.wait_ge(*states.at(p, back=1))
                dve.wait_ge(*pe_done.at(p, back=1))
                for t in range(G2):
                    last = dve.tensor_scalar(state_mid[:, t], state_d[:, t], s[:, 3, t:t + 1], None, ALU.mult)
                last.then_inc(mid_ready.sem, 1)
                dve.wait_ge(C["loaded"], C["loaded_n"])
                mask = C["pair_mask"][:].rearrange("p m n -> p (m n)").bitcast(I32)
                for g in range(2):
                    hold(*pairs_d.at(p, g))
                    for h in (2 * g, 2 * g + 1):
                        last = dve.copy_predicated(scores_d[:, h].rearrange("p m n -> p (m n)"), mask, ps_d[:, h])
                    last.then_inc(scored_d.sem, 1)
                dve.wait_ge(*off_ready.at(p, 0))
                eye = ident.rearrange("p (a n) -> p a n", a=1).broadcast_to([P, 2, TC])
                for g in range(2):
                    last = dve.tensor_tensor(invs[:, g, 1], eye, off[:, 0, 2 * g:2 * g + 2], ALU.subtract)
                last.then_inc(first_inv.sem, 1)
                for n in range(NS):
                    g = n % 2
                    dve.wait_ge(*y_done.at(p, n))
                    dve.tensor_tensor(w[:, 2 * g:2 * g + 2], eye, ps_y[g][:, 0:2 * TC].rearrange("p (h n) -> p h n", h=2),
                                      ALU.subtract).then_inc(w_ready.sem, 1)
                    if g == 1 and n // 2 < 4:
                        pick_pairs(me, p, n // 2)
                    if n == 1 and following:
                        prepare_mid(*following)
                    if n == 7 and following:
                        prepare_rest(*following)
                dve.wait_ge(*ds_done.at(p))
                for t in range(G2):
                    dve.scalar_tensor_tensor(grown[:, t], ps_s[:, t * P:(t + 1) * P], s[:, 4, t:t + 1], headones, ALU.mult,
                                             ALU.mult)
                me.done(dve.tensor_tensor(grown_a[:], ps_s[:, G2 * P:].rearrange("p (t n) -> p t n", t=G2),
                                          headones.rearrange("p (a n) -> p a n", a=1).broadcast_to([P, G2, P]), ALU.mult))
                for t in range(G2):
                    dve.scalar_tensor_tensor(state_d[:, t], state_mid[:, t], s[:, 4, t:t + 1], grown[:, t], ALU.mult, ALU.add)
                    last = dve.scalar_tensor_tensor(state_a[:, t], state_a[:, t], s[:, 5, t:t + 1], grown_a[:, t], ALU.mult,
                                                    ALU.add)
                last.then_inc(states.sem, 1)
                me.check()

            def pick_pairs(me, p, r):
                hold(*pairs_a.at(p, r))
                for j in range(2):
                    mask = masks[:, 2 * r + j:2 * r + j + 1].bitcast(I32)
                    for q in range(2):
                        last = dve.copy_predicated(scores_a[:, q], mask.broadcast_to([P, G2, TC]), ps_a[:, q, j])
                    if j == 0:
                        last.then_inc(me.sem, 1)
                        me.k += 1
                        hold(me.sem, p * me.n + me.k)
                last.then_inc(scored_a.sem, 1)

            chunks(nc.vector.Fori, prepare, run)

        @block.tensor
        def _(pe):
            pe.wait_ge(C["loaded"], C["loaded_n"])
            pe_done.seed_by(pe)

            def rows(q):
                return slice(q * HD, (q + 1) * HD)

            def head(h):
                return slice(h * HD, (h + 1) * HD)

            def run(p, i, u, _):
                f = feats[u]
                pe.wait_ge(*kr_ready.at(p))
                pe.wait_ge(*states.at(p, back=1))
                pe.wait_ge(*oy_out.at(p, back=1))
                pe.wait_ge(*x_out.at(p, back=1))
                for h in range(H):
                    t, q = h // 2, h % 2
                    for m in range(2):
                        mm = pe.matmul(ps_d[:, h, 2 * m * TC:(2 * m + 2) * TC], bk[u][rows(q), m, t],
                                       kr[u][rows(q), t].rearrange("p a n -> p (a n)"), start=True, stop=True)
                    if q == 1:
                        mm.then_inc(pairs_d.sem, 1)
                pe.wait_ge(*qk_ready.at(p))
                for t in range(G2):
                    mm = pe.transpose(ps_o[:, t * TC:(t + 1) * TC], kc[u][:, t], ident)
                mm.then_inc(kc_turned.sem, 1)
                for m in range(2):
                    for t in range(G2):
                        mm = pe.transpose(ps_s[:, (2 * m + t) * TC:(2 * m + t + 1) * TC], bk[u][:, m, t], ident)
                mm.then_inc(bk_turned.sem, 1)

                def pairs(r):
                    if r == 0:
                        pe.wait_ge(*halves_ready.at(p))
                    pe.wait_ge(*(scored_a.at(p, r - 1) if r else scored_a.at(p, back=1)))
                    for j in range(2):
                        m = 2 * r + j
                        for t in range(G2):
                            for q in range(2):
                                x = halves[u][rows(q), m, t] if m < NL else None
                                lhs, rhs_ = (x, x) if m < NL else (f[rows(q), K, t], f[rows(q), Q, t])
                                mm = pe.matmul(ps_a[:, q, j, t], lhs, rhs_, start=True, stop=True)
                    mm.then_inc(pairs_a.sem, 1)

                pe.wait_ge(*first_inv.at(p))
                for h in range(H):
                    mm = pe.transpose(ps_x[h // 2][:, h % 2 * TC:(h % 2 + 1) * TC], inv_t(h), ident)
                mm.then_inc(inv_turned.sem, 1)
                for level in range(NL - 1):
                    pe.wait_ge(*off_ready.at(p, level + 1))
                    for g in range(2):
                        if level == 0:
                            pe.wait_ge(*inv_out.at(p))
                        else:
                            pe.wait_ge(*x_out.at(p, 2 * (level - 1) + g))
                        for h in (2 * g, 2 * g + 1):
                            mm = pe.matmul(ps_y[g][:, h % 2 * TC:(h % 2 + 1) * TC], off[:, level + 1, h], inv(h), start=True,
                                           stop=True)
                        mm.then_inc(y_done.sem, 1)
                    if level < 4:
                        pairs(level)
                    for g in range(2):
                        pe.wait_ge(*w_ready.at(p, 2 * level + g))
                        for h in (2 * g, 2 * g + 1):
                            at = slice(h % 2 * TC, (h % 2 + 1) * TC)
                            if level < NL - 2:
                                pe.matmul(ps_x[g][:, 0:2 * TC][:, at], inv_t(h), w[:, h], start=True, stop=True)
                            mm = pe.matmul(ps_x[g][:, 2 * TC:][:, at], w[:, h], inv_t(h), start=True, stop=True)
                        mm.then_inc(x_done.sem, 1)
                pe.wait_ge(*bk_out.at(p))
                pe.wait_ge(*mid_ready.at(p))
                for t in range(G2):
                    at = slice(t * P, (t + 1) * P)
                    pe.matmul(ps_s[:, at], kr[u][:, t, 0], state_mid[:, t], start=True, stop=False)
                    for h in (2 * t, 2 * t + 1):
                        mm = pe.matmul(ps_s[:, head(h)], scores_d[:, h, 2], vd[u][:, head(h)], start=False, stop=h % 2 == 1)
                mm.then_inc(rhs_done.sem, 1)
                pe.wait_ge(*scored_a.at(p, 3))
                pe.wait_ge(*kc_out.at(p))
                for t in range(G2):
                    at = slice(t * TC, (t + 1) * TC)
                    pe.matmul(ps_o[:, at], state_a[:, t], qc[u][:, t], start=True, stop=False)
                    for q in range(2):
                        pe.matmul(ps_o[rows(q), at], va[u][:, head(2 * t + q)], scores_a[:, q, t], start=False, stop=True)
                pe.wait_ge(*rhs_ready.at(p))
                pe.wait_ge(*x_out.at(p, NS - 1))
                for h in range(H):
                    mm = pe.matmul(ps_s[:, G2 * P + h * HD:G2 * P + (h + 1) * HD], inv_t(h), rhs[:, head(h)], start=True,
                                   stop=True)
                mm.then_inc(sa_done.sem, 1)
                pe.wait_ge(*sa_ready.at(p))
                for t in range(G2):
                    at = slice(t * P, (t + 1) * P)
                    pe.matmul(ps_s[:, at], bk_tok[:, 0, t], sa[:, at], start=True, stop=False)
                    pe.matmul(ps_s[:, at], bk_tok[:, 1, t], vd[u][:, at], start=False, stop=True)
                for t in range(G2):
                    at = slice(t * P, (t + 1) * P)
                    mm = pe.matmul(ps_s[:, G2 * P + t * P:G2 * P + (t + 1) * P], kc_tok[:, t], va[u][:, at], start=True, stop=True)
                mm.then_inc(ds_done.sem, 1)
                for t in range(G2):
                    at = slice((G2 + t) * TC, (G2 + t + 1) * TC)
                    pe.matmul(ps_o[:, at], state_mid[:, t], kr[u][:, t, 1], start=True, stop=False)
                    for q in range(2):
                        h = 2 * t + q
                        pe.matmul(ps_o[rows(q), at], sa[:, head(h)], scores_d[:, h, 1], start=False, stop=False)
                        mm = pe.matmul(ps_o[rows(q), at], vd[u][:, head(h)], scores_d[:, h, 3], start=False, stop=True)
                mm.then_inc(pe_done.sem, 1)

            chunks(nc.tensor.Fori, lambda p, i, u: None, run)


def state_space(nc, ctx, D, C):
    with ExitStack() as mem:
        def sb(name, shape, dt=F32):
            return mem.enter_context(nc.sbuf_tensor(name, shape, dt))

        def sig(name, n=1, unit=1, seed=0):
            return Signal(nc.alloc_semaphore(name), n, unit, seed)

        NG, NP, GC = 16, 64, 16
        L = P // GC
        NS = SEQ // L
        HALF = NS // 2
        STEPS = NS.bit_length() - 1
        NBANK = 8
        raw = sb("s5_raw", [P, 3, NG])
        b_in, c_in = sb("b_in", [P, 2, NG, GC]), sb("c_in", [P, 2, NG, GC])
        d_skip = sb("d_skip", [P, NG])
        sign = sb("sign", [P, 2])
        corner = sb("corner", [P, P])
        w_glu = sb("w_glu", [P, G2, G2, P])
        v = [sb(f"s5_v{n}", [P, NG]) for n in range(8)]
        re, im = sb("pow_re", [P, L + 1, NG]), sb("pow_im", [P, L + 1, NG])
        sre, sim = sb("sgn_re", [P, L + 1, NG]), sb("sgn_im", [P, L + 1, NG])
        simb = sb("sgn_imb", [P, L + 1, NG])
        mr, mi = sb("step_re", [P, 2, NG]), sb("step_im", [P, 2, NG])
        coef = sb("coef", [P, 2, NG, 2])
        b_bar = sb("b_bar", [P, 2, NG, GC])
        b_pad = sb("b_pad", [P, NG, 2 * L - 1, GC])
        w_p = sb("w_p", [P, NG, L, GC])
        c_pad = sb("c_pad", [P, NG, 2 * L, GC])
        tmp = sb("s5_tmp", [P, NG, GC])
        w_in = sb("s5_w_in", [P, NG, P])
        taps = sb("taps", [P, NG, P])
        step = [sb(f"step{u}", [P, NG, P]) for u in range(2)]
        u_sub = sb("u_sub", [P, 2, L * NG * GC])
        u_g = sb("u_g", [P, NG, NS])
        h = sb("s5_h", [P, NG, 1 + NS])
        yt = sb("yt", [P, G2, SEQ])
        gate = sb("gate", [P, G2, SEQ])
        y_sub = u_sub[:].rearrange("p h (t c) -> p h t c", t=L)
        sq = u_g[:].rearrange("p g n -> p (g n)").rearrange("p (t n) -> p t n", t=G2)
        inv = sb("s5_inv", [P, SEQ])
        ps = mem.enter_context(nc.psum_tensor("s5_ps", [P, NBANK, TB], F32))
        ident, ones, col = C["ident"], C["ones"], C["col"]

        loaded, u_in = sig("s5_loaded", 7, 16), sig("u_in", 1, 16)
        decay_arg, dt_done, root_arg, powers1 = sig("decay_arg"), sig("dt_done"), sig("angle"), sig("sines")
        weights, c_ready = sig("s5_weights"), sig("c_ready")
        u_turned, u_out = sig("u_turned", NBANK), sig("u_out", NBANK)
        t_done, t_out = sig("taps_done", 4), sig("taps_out", 4)
        wt_done, wt_out = sig("wt_done", 4), sig("wt_out", 4)
        v_done, v_out = sig("v_done", NBANK), sig("v_out", NBANK)
        m_ready, l_done, l_out = sig("m_ready", STEPS), sig("l_done", STEPS * NBANK), sig("l_out", STEPS * NBANK)
        y_done, y_out = sig("y_done5", NBANK), sig("y_out5", NBANK)
        yt_done, yt_out = sig("yt_done", NBANK), sig("yt_out", NBANK)
        glu_done, glu_out = sig("glu_done", NBANK), sig("glu_out", NBANK)
        o_ready, sq_ready = sig("o_ready", NBANK), sig("sq_ready", NBANK)
        n_done, n_out, n_root, yc_ready = sig("n_done", NB), sig("n_out", NB), sig("n_root", NB), sig("yc_ready", NB)
        stored = sig("yc_stored", NB * G2, 16)
        u_grouped = sig("u_grouped")
        own_v, own_a = sig("s5_dve_own").sem, sig("s5_act_own").sem
        block = mem.enter_context(nc.Block())

        @block.sync
        def _(sp):
            for dst, src in ((raw, "s5_raw"), (b_in, "s5_b"), (c_in, "s5_c"), (d_skip, "s5_d"), (sign, "s5_sign"),
                             (corner, "s5_corner"), (w_glu, "s5_glu")):
                sp.dma_start(dst[:], D[src]).then_inc(loaded.sem, 16)
            src = D["cu"].rearrange("c n x -> (c n x)").rearrange("(h s m) -> s h m", h=2, s=HALF)
            sp.dma_start(u_sub[:], src).then_inc(u_in.sem, 16)
            for b in range(NB):
                sp.wait_ge(*yc_ready.at(0, b))
                for t in range(G2):
                    sp.dma_start(D["late"][b * CB:(b + 1) * CB, :, len(LATE) - 1, t].rearrange("c p n -> p c n"),
                                 yt[:, t, b * TB:(b + 1) * TB].rearrange("p (c n) -> p c n", c=CB)).then_inc(stored.sem, 16)
            sp.wait_ge(*stored.at(0))

        @block.scalar
        def _(act):
            me = Own(act, own_a)
            act.wait_ge(*loaded.at(0))
            me.done(act.activation(v[0][:], raw[:, 2], ACT.Exp), dt_done)
            act.wait_ge(*decay_arg.at(0))
            me.done(act.activation(v[1][:], v[1][:], ACT.Exp))
            act.wait_ge(*root_arg.at(0))
            me.done(act.activation(v[3][:], v[2][:], ACT.Sin))
            me.done(act.activation(v[4][:], v[2][:], ACT.Sin, scale=0.5), powers1)
            for n in range(NBANK):
                act.wait_ge(*u_turned.at(0, n))
                act.activation(u_g[:, 2 * n:2 * n + 2].rearrange("p g n -> p (g n)"), ps[:, n], ACT.Copy).then_inc(u_out.sem, 1)
            for n in range(4):
                act.wait_ge(*wt_done.at(0, n))
                act.activation(w_in[:, 4 * n:4 * n + 4].rearrange("p g n -> p (g n)"), ps[:, 4 + n], ACT.Copy).then_inc(wt_out.sem, 1)
            for n in range(NBANK):
                act.wait_ge(*v_done.at(0, n))
                act.activation(h[:, 2 * n:2 * n + 2, 1:], ps[:, n].rearrange("p (g n) -> p g n", g=2), ACT.Copy).then_inc(v_out.sem, 1)
            for n in range(NBANK):
                half, g = n // 4, n % 4 * 4
                act.wait_ge(*y_done.at(0, n))
                act.activation(y_sub[:, half, :, g * GC:(g + 4) * GC].rearrange("p t (g c) -> p g t c", g=4),
                               ps[:, n].rearrange("p (g t c) -> p g t c", g=4, t=L), ACT.Gelu_apprx_tanh).then_inc(y_out.sem, 1)
            for n in range(NBANK):
                t, b = n // NB, n % NB
                act.wait_ge(*glu_done.at(0, n))
                act.activation(gate[:, t, b * TB:(b + 1) * TB], ps[:, n], ACT.Sigmoid, bias=col("s5_b_glu", t)).then_inc(glu_out.sem, 1)
            for b in range(NB):
                for t in range(G2):
                    act.wait_ge(*o_ready.at(0, t * NB + b))
                    act.activation(sq[:, t, b * TB:(b + 1) * TB], yt[:, t, b * TB:(b + 1) * TB], ACT.Square).then_inc(sq_ready.sem, 1)
            for b in range(NB):
                act.wait_ge(*n_out.at(0, b))
                act.activation(inv[:, b * TB:(b + 1) * TB], inv[:, b * TB:(b + 1) * TB], ACT.Sqrt).then_inc(n_root.sem, 1)

        @block.vector
        def _(dve):
            me = Own(dve, own_v)
            tt, ts, stt = dve.tensor_tensor, dve.tensor_scalar, dve.scalar_tensor_tensor
            ADD, SUB, MUL = ALU.add, ALU.subtract, ALU.mult
            for x in (b_pad[:], c_pad[:], h[:, :, 0:1], re[:, 0], im[:, 0]):
                last = dve.memset(x, 0.0)
            me.done(last)
            me.done(dve.memset(re[:, 0], 1.0))
            dve.wait_ge(*loaded.at(0))
            lr, li = raw[:, 0], raw[:, 1]
            dve.wait_ge(*dt_done.at(0))
            me.done(tt(v[1][:], lr, v[0][:], MUL), decay_arg)
            me.done(tt(v[2][:], li, v[0][:], MUL))
            me.done(ts(v[5][:], v[2][:], float(1 / (2 * np.pi)), 12582912.0, MUL, ADD))
            me.done(ts(v[5][:], v[5][:], -12582912.0, None, ADD))
            me.done(stt(v[2][:], v[5][:], -6.28125, v[2][:], MUL, ADD))
            me.done(stt(v[2][:], v[5][:], -float(2 * np.pi - 6.28125), v[2][:], MUL, ADD))
            me.done(ts(v[2][:], v[2][:], 3.1415925, -3.1415925, ALU.min, ALU.max), root_arg)
            dve.wait_ge(*powers1.at(0))
            me.done(tt(v[4][:], v[4][:], v[4][:], MUL))
            me.done(ts(v[4][:], v[4][:], -2.0, 1.0, MUL, ADD))
            me.done(tt(re[:, 1], v[4][:], v[1][:], MUL))
            me.done(tt(im[:, 1], v[3][:], v[1][:], MUL))

            def times(out_re, out_im, x_re, x_im, y_re, y_im):
                tt(v[5][:], x_im, y_im, MUL)
                tt(v[6][:], x_im, y_re, MUL)
                tt(v[7][:], x_re, y_im, MUL)
                me.done(tt(v[4][:], x_re, y_re, MUL))
                tt(out_re, v[4][:], v[5][:], SUB)
                me.done(tt(out_im, v[6][:], v[7][:], ADD))

            for n in range(1, L):
                times(re[:, n + 1], im[:, n + 1], re[:, n], im[:, n], re[:, 1], im[:, 1])
            me.done(ts(v[0][:], re[:, 1], -1.0, None, ADD))
            tt(v[1][:], lr, lr, MUL)
            me.done(tt(v[2][:], li, li, MUL))
            me.done(tt(v[1][:], v[1][:], v[2][:], ADD))
            me.done(dve.reciprocal(v[1][:], v[1][:]))
            me.done(ts(v[3][:], li, -1.0, None, MUL))
            times(v[2][:], v[0][:], v[0][:], im[:, 1], lr, v[3][:])
            me.done(tt(v[2][:], v[2][:], v[1][:], MUL))
            me.done(tt(v[0][:], v[0][:], v[1][:], MUL))
            me.done(ts(v[0][:], v[0][:], sign[:, 0:1], None, MUL))
            ts(sre[:], re[:], sign[:, 1:2], None, MUL)
            ts(simb[:], im[:], sign[:, 0:1], None, MUL)
            me.done(ts(sim[:], im[:], -1.0, None, MUL))

            def wide(x):
                return x.rearrange("p (g c) -> p g c", c=1).broadcast_to([P, NG, GC])

            for n in range(2):
                me.done(tt(tmp[:], b_in[:, 1 - n], wide(v[0][:]), MUL))
                me.done(tt(b_bar[:, n], b_in[:, n], wide(v[2][:]), MUL))
                me.done(tt(b_bar[:, n], b_bar[:, n], tmp[:], SUB if n else ADD))
            me.done(dve.tensor_copy(b_pad[:, :, L - 1], b_bar[:, 0]))
            for n in range(L + 1):
                me.done(tt(tmp[:], c_in[:, 1], wide(sim[:, n]), MUL))
                me.done(tt(c_pad[:, :, L - 1 + n], c_in[:, 0], wide(sre[:, n]), MUL))
                me.done(tt(c_pad[:, :, L - 1 + n], c_pad[:, :, L - 1 + n], tmp[:], ADD), *((c_ready,) if n == L else ()))
            for n in range(L):
                me.done(tt(tmp[:], b_bar[:, 1], wide(simb[:, n]), MUL))
                me.done(tt(w_p[:, :, L - 1 - n], b_bar[:, 0], wide(re[:, n]), MUL))
                me.done(tt(w_p[:, :, L - 1 - n], w_p[:, :, L - 1 - n], tmp[:], ADD), *((weights,) if n == L - 1 else ()))

            def make_step(n):
                s_re, s_im = (re[:, L], im[:, L]) if n == 0 else (mr[:, n % 2], mi[:, n % 2])
                if n:
                    o_re, o_im = (re[:, L], im[:, L]) if n == 1 else (mr[:, (n - 1) % 2], mi[:, (n - 1) % 2])
                    times(s_re, s_im, o_re, o_im, o_re, o_im)
                c = coef[:, n % 2]
                for half in range(2):
                    r = slice(half * NP, (half + 1) * NP)
                    dve.tensor_copy(c[r, :, half], s_re[r])
                    last = ts(c[r, :, 1 - half], s_im[r], sign[r, 1:2], None, MUL)
                me.done(last)
                if n >= 2:
                    dve.wait_ge(*l_done.at(0, (n - 1) * NBANK - 1))
                me.done(tt(step[n % 2][:].rearrange("p g (a m) -> p g a m", a=2),
                           corner[:].rearrange("p (b a m) -> p b a m", a=2, b=1).broadcast_to([P, NG, 2, NP]),
                           c.rearrange("p g (a b) -> p g a b", b=1).broadcast_to([P, NG, 2, NP]), MUL), m_ready, n)

            make_step(0)
            for n in range(4):
                dve.wait_ge(*t_done.at(0, n))
                for g in range(4 * n, 4 * n + 4):
                    last = stt(taps[:, g], ident, d_skip[:, g:g + 1], ps[:, n, g % 4 * P:(g % 4 + 1) * P], MUL, ADD)
                last.then_inc(t_out.sem, 1)
            for n in range(STEPS):
                if n + 1 < STEPS:
                    make_step(n + 1)
                d = 1 << n
                for m in range(NBANK):
                    dve.wait_ge(*l_done.at(0, n * NBANK + m))
                    to = h[:, 2 * m:2 * m + 2, 1 + d:]
                    tt(to, to, ps[:, m].rearrange("p (g n) -> p g n", g=2)[:, :, 0:NS - d], ADD).then_inc(l_out.sem, 1)
            for n in range(NBANK):
                half, t, j = n // 4, n // 2 % 2, n % 2 * 4
                dve.wait_ge(*yt_done.at(0, n))
                to = yt[:, t].rearrange("p (h s l) -> p h l s", h=2, l=L)[:, half, j:j + 4]
                dve.tensor_copy(to, ps[:, n].rearrange("p (l s) -> p l s", l=4)).then_inc(yt_out.sem, 1)
            for n in range(NBANK):
                t, b = n // NB, n % NB
                at = slice(b * TB, (b + 1) * TB)
                dve.wait_ge(*glu_out.at(0, n))
                dve.wait_ge(*glu_done.at(0))
                tt(yt[:, t, at], yt[:, t, at], gate[:, t, at], MUL).then_inc(o_ready.sem, 1)
            for b in range(NB):
                at = slice(b * TB, (b + 1) * TB)
                dve.wait_ge(*n_done.at(0, b))
                ts(inv[:, at], ps[:, b], 1.0 / (G2 * P), EPS, MUL, ADD).then_inc(n_out.sem, 1)
            for b in range(NB):
                at = slice(b * TB, (b + 1) * TB)
                dve.wait_ge(*n_root.at(0, b))
                me.done(dve.reciprocal(inv[:, at], inv[:, at]))
                dve.wait_ge(*sq_ready.at(0, G2 * b + 1))
                for t in range(G2):
                    last = stt(yt[:, t, at], yt[:, t, at], col("s5_norm", t), inv[:, at], MUL, MUL)
                last.then_inc(yc_ready.sem, 1)

        @block.gpsimd
        def _(pool):
            pool.wait_ge(*u_in.at(0))
            for half in range(2):
                last = pool.tensor_copy(gate[:, half].rearrange("p (g t c) -> p g t c", g=NG, t=L),
                                        u_sub[:, half].rearrange("p (t g c) -> p g t c", g=NG, t=L))
            last.then_inc(u_grouped.sem, 1)

        @block.tensor
        def _(pe):
            pe.wait_ge(C["loaded"], C["loaded_n"])
            pe.wait_ge(*u_grouped.at(0))
            u4 = gate[:].rearrange("p h (g m) -> p h g m", g=NG)
            for n in range(NBANK):
                for g in (2 * n, 2 * n + 1):
                    for half in range(2):
                        at = (g % 2 * 2 + half) * P
                        mm = pe.transpose(ps[:, n, at:at + P], u4[:, half, g], ident)
                mm.then_inc(u_turned.sem, 1)
            pe.wait_ge(*loaded.at(0))
            pe.wait_ge(*c_ready.at(0))
            for n in range(4):
                pe.wait_ge(*u_out.at(0, n))
                for g in range(4 * n, 4 * n + 4):
                    for s in range(L):
                        mm = pe.matmul(ps[:, n, g % 4 * P:(g % 4 + 1) * P],
                                       b_pad[:, g, L - 1 - s:2 * L - 1 - s].rearrange("p s c -> p (s c)"),
                                       c_pad[:, g, L - 1 - s:2 * L - 1 - s].rearrange("p s c -> p (s c)"),
                                       start=s == 0, stop=s == L - 1)
                mm.then_inc(t_done.sem, 1)
            pe.wait_ge(*weights.at(0))
            for n in range(4):
                pe.wait_ge(*u_out.at(0, 4 + n))
                for g in range(4 * n, 4 * n + 4):
                    mm = pe.transpose(ps[:, 4 + n, g % 4 * P:(g % 4 + 1) * P], w_p[:, g].rearrange("p s c -> p (s c)"), ident)
                mm.then_inc(wt_done.sem, 1)
            for n in range(NBANK):
                if n < 4:
                    pe.wait_ge(*t_out.at(0, n))
                pe.wait_ge(*wt_out.at(0, max(n - 4, n // 2)))
                for g in (2 * n, 2 * n + 1):
                    mm = pe.matmul(ps[:, n, g % 2 * NS:(g % 2 + 1) * NS], w_in[:, g], u_g[:, g], start=True, stop=True)
                mm.then_inc(v_done.sem, 1)
            for n in range(STEPS):
                pe.wait_ge(*m_ready.at(0, n))
                d = 1 << n
                for m in range(NBANK):
                    pe.wait_ge(*(l_out.at(0, (n - 1) * NBANK + m) if n else v_out.at(0, m)))
                    for g in (2 * m, 2 * m + 1):
                        at = g % 2 * NS
                        mm = pe.matmul(ps[:, m, at:at + NS - d], step[n % 2][:, g], h[:, g, 1:1 + NS - d], start=True, stop=True)
                    mm.then_inc(l_done.sem, 1)
            pe.wait_ge(*t_out.at(0))
            for n in range(NBANK):
                half, g0 = n // 4, n % 4 * 4
                pe.wait_ge(*l_out.at(0, (STEPS - 1) * NBANK + max(n, g0 // 2 + 1)))
                for g in range(g0, g0 + 4):
                    to = ps[:, n, g % 4 * P:(g % 4 + 1) * P]
                    pe.matmul(to, u_g[:, g, half * HALF:(half + 1) * HALF], taps[:, g], start=True, stop=False)
                    mm = pe.matmul(to, h[:, g, half * HALF:(half + 1) * HALF], c_pad[:, g, L:].rearrange("p s c -> p (s c)"),
                                   start=False, stop=True)
                mm.then_inc(y_done.sem, 1)
            for n in range(NBANK):
                half, t, j = n // 4, n // 2 % 2, n % 2 * 4
                pe.wait_ge(*y_out.at(0, max(n, 4 * half + 3)))
                for k in range(4):
                    mm = pe.transpose(ps[:, n, k * P:(k + 1) * P], y_sub[:, half, j + k, t * P:(t + 1) * P], ident)
                mm.then_inc(yt_done.sem, 1)
            for n in range(NBANK):
                t, b = n // NB, n % NB
                pe.wait_ge(*yt_out.at(0))
                for k in range(G2):
                    mm = pe.matmul(ps[:, n], w_glu[:, k, t], yt[:, k, b * TB:(b + 1) * TB], start=k == 0, stop=k == G2 - 1)
                mm.then_inc(glu_done.sem, 1)
            for b in range(NB):
                pe.wait_ge(*glu_out.at(0, b))
                pe.wait_ge(*sq_ready.at(0, G2 * b + 1))
                for k in range(G2):
                    mm = pe.matmul(ps[:, b], ones, sq[:, k, b * TB:(b + 1) * TB], start=k == 0, stop=k == G2 - 1)
                mm.then_inc(n_done.sem, 1)


def attend_memory(nc, ctx, D, C):
    with ExitStack() as mem:
        def sb(name, shape, dt=F32):
            return mem.enter_context(nc.sbuf_tensor(name, shape, dt))

        def sig(name, n=1, unit=1, seed=0):
            return Signal(nc.alloc_semaphore(name), n, unit, seed)

        MT = N_MEM // P
        KVT = 2 * KT
        HDT = XA_HD // P
        D_HALF = D_MODEL // 2
        w_out = sb("w_out_sb", [P, KT, D_MODEL])
        key_w = sb("key_w", [P, KT, XA_HEADS * N_MEM])
        val_w = sb("val_w", [P, XA_HEADS * MT, D_MODEL])
        ident, headones, col, cols = C["ident"], C["headones"], C["col"], C["cols"]

        with ExitStack() as pre:
            def psb(name, shape):
                return pre.enter_context(nc.sbuf_tensor(name, shape, F32))

            NW = 4
            m_t = psb("m_t", [P, MT, D_MODEL])
            m_junk = psb("m_junk", [P, D_MODEL])
            m_sq = psb("m_sq", [P, MT])
            mn = psb("mn", [P, KT, N_MEM])
            kv = psb("kv", [P, KVT, N_MEM])
            ring = psb("xa_ring", [P, NW, D_MODEL])
            ps = pre.enter_context(nc.psum_tensor("m_ps", [P, 8, TB], F32))
            NT = KVT + KT + KT
            m_in, w_in = sig("m_in", 1, 16), [sig(f"xa_w_in{s}", NT // NW, 16) for s in range(NW)]
            w_out_in = sig("w_out_in", 1, 16)
            m_sumsq, m_ms, m_root, m_scaled = sig("m_sumsq"), sig("m_ms"), sig("m_root"), sig("m_scaled")
            m_turned, mn_ready = sig("m_turned", KT), sig("mn_ready", KT)
            kv_done, kv_out = sig("kv_done", KVT), sig("kv_out", KVT)
            kw_done, kw_out = sig("kw_done", 4 * XA_HEADS), sig("kw_out", 4 * XA_HEADS)
            vw_done, vw_out = sig("vw_done", 4 * XA_HEADS), sig("vw_out", 4 * XA_HEADS)
            own_v, own_a = sig("s3m_dve_own").sem, sig("s3m_act_own").sem

            def multiplied(n):
                if n < KVT:
                    return kv_done.at(0, n)
                if n < KVT + KT:
                    return kw_done.at(0, (n - KVT) // HDT * 4 + 3)
                return vw_done.at(0, (n - KVT - KT) // HDT * 4 + 3)

            with nc.Block() as block:
                @block.sync
                def _(sp):
                    sp.dma_start(m_t[:], D["mem"].rearrange("(j p) n -> p j n", p=P)).then_inc(m_in.sem, 16)
                    for n in range(NT):
                        if n >= NW:
                            sp.wait_ge(*multiplied(n - NW))
                        if n < KVT:
                            src = D["wkv"][n]
                        elif n < KVT + KT:
                            src = D["wq_t"][n - KVT]
                        else:
                            src = D["wo"][n - KVT - KT]
                        sp.dma_start(ring[:, n % NW], src).then_inc(w_in[n % NW].sem, 16)
                    sp.dma_start(w_out[:], D["w_out"]).then_inc(w_out_in.sem, 16)
                    sp.wait_ge(*w_out_in.at(0))

                @block.scalar
                def _(act):
                    me = Own(act, own_a)
                    act.wait_ge(*m_in.at(0))
                    for j in range(MT):
                        me.done(act.activation(m_junk[:], m_t[:, j], ACT.Square, accum_out=m_sq[:, j:j + 1]),
                                *((m_sumsq,) if j == MT - 1 else ()))
                    act.wait_ge(*m_ms.at(0))
                    me.done(act.activation(m_sq[:], m_sq[:], ACT.Sqrt), m_root)
                    for n in range(KVT):
                        act.wait_ge(*kv_done.at(0, n))
                        act.activation(kv[:, n], ps[:, n % 4, 0:N_MEM], ACT.Copy).then_inc(kv_out.sem, 1)
                    for n in range(4 * XA_HEADS):
                        act.wait_ge(*vw_done.at(0, n))
                        h, j, half = n // 4, n // 2 % 2, n % 2
                        act.activation(val_w[:, h * MT + j, half * D_HALF:(half + 1) * D_HALF], ps[:, 4 + n % 4],
                                       ACT.Copy).then_inc(vw_out.sem, 1)

                @block.vector
                def _(dve):
                    me = Own(dve, own_v)
                    dve.wait_ge(*m_sumsq.at(0))
                    me.done(dve.tensor_scalar(m_sq[:], m_sq[:], 1.0 / D_MODEL, EPS, ALU.mult, ALU.add), m_ms)
                    dve.wait_ge(*m_root.at(0))
                    me.done(dve.reciprocal(m_sq[:], m_sq[:]))
                    for j in range(MT):
                        last = dve.tensor_scalar(m_t[:, j], m_t[:, j], m_sq[:, j:j + 1], None, ALU.mult)
                    last.then_inc(m_scaled.sem, 1)
                    for k in range(KT):
                        dve.wait_ge(*m_turned.at(0, k))
                        dve.tensor_scalar(mn[:, k], ps[:, k, 0:N_MEM], col("xa_mem_norm", k), None, ALU.mult)\
                           .then_inc(mn_ready.sem, 1)
                    for n in range(4 * XA_HEADS):
                        dve.wait_ge(*kw_done.at(0, n))
                        h, k = n // 4, n % 4 * 2
                        dve.tensor_copy(key_w[:, k:k + 2, h * N_MEM:(h + 1) * N_MEM],
                                        ps[:, n % 4].rearrange("p (k m) -> p k m", k=2)).then_inc(kw_out.sem, 1)

                @block.tensor
                def _(pe):
                    pe.wait_ge(*m_scaled.at(0))
                    for k in range(KT):
                        for j in range(MT):
                            mm = pe.transpose(ps[:, k, j * P:(j + 1) * P], m_t[:, j, k * P:(k + 1) * P], ident)
                        mm.then_inc(m_turned.sem, 1)
                    pe.wait_ge(*mn_ready.at(0))
                    for n in range(KVT):
                        pe.wait_ge(*w_in[n % NW].at(0, n // NW))
                        if n >= 4:
                            pe.wait_ge(*kv_out.at(0, n - 4))
                        for k in range(KT):
                            mm = pe.matmul(ps[:, n % 4, 0:N_MEM], ring[:, n % NW, k * P:(k + 1) * P], mn[:, k], start=k == 0,
                                           stop=k == KT - 1)
                        mm.then_inc(kv_done.sem, 1)
                    pe.wait_ge(*kv_out.at(0))
                    for h in range(XA_HEADS):
                        for d in range(HDT):
                            n = KVT + h * HDT + d
                            pe.wait_ge(*w_in[n % NW].at(0, n // NW))
                        for k in range(KT):
                            n = h * 4 + k // 2
                            if k % 2 == 0 and n >= 4:
                                pe.wait_ge(*kw_out.at(0, n - 4))
                            for d in range(HDT):
                                w = ring[:, (KVT + h * HDT + d) % NW, k * P:(k + 1) * P]
                                mm = pe.matmul(ps[:, n % 4, k % 2 * N_MEM:(k % 2 + 1) * N_MEM], w, kv[:, h * HDT + d],
                                               start=d == 0, stop=d == HDT - 1)
                            if k % 2:
                                mm.then_inc(kw_done.sem, 1)
                    for h in range(XA_HEADS):
                        for d in range(HDT):
                            n = KVT + KT + h * HDT + d
                            pe.wait_ge(*w_in[n % NW].at(0, n // NW))
                        for m in range(4):
                            j, half, n = m // 2, m % 2, h * 4 + m
                            if n >= 4:
                                pe.wait_ge(*vw_out.at(0, n - 4))
                            for d in range(HDT):
                                w = ring[:, (KVT + KT + h * HDT + d) % NW, half * D_HALF:(half + 1) * D_HALF]
                                mm = pe.matmul(ps[:, 4 + n % 4], kv[:, KT + h * HDT + d, j * P:(j + 1) * P], w, start=d == 0,
                                               stop=d == HDT - 1)
                            mm.then_inc(vw_done.sem, 1)

        x_t = [sb(f"s3_x{u}", [P, D_MODEL]) for u in range(2)]
        oy = [sb(f"s3_oy{u}", [P, 2, G2, TC]) for u in range(2)]
        late = [sb(f"s3_late{u}", [P, 3, G2, TC]) for u in range(2)]
        mix = [sb(f"mix{u}", [P, KT, TC]) for u in range(2)]
        sq_o, sq_y = sb("sq_o", [P, G2, TC]), sb("sq_y", [P, G2, TC])
        head_var = sb("head_var", [P, 2, G2, TC])
        hn_tok, h2_tok = sb("hn_tok", [P, D_MODEL]), sb("h2_tok", [P, D_MODEL])
        s3_junk = sb("s3_junk", [P, D_MODEL])
        ms1, ms2 = sb("ms1", [P, 1]), sb("ms2", [P, 1])
        hn_t, h3_t = sb("hn_t", [P, KT, TC]), sb("h3_t", [P, KT, TC])
        top = sb("top", [P, XA_HEADS])
        total = sb("total", [P, XA_HEADS])
        prob = sb("prob", [P, XA_HEADS, N_MEM])
        prob_t = sb("prob_t", [P, XA_HEADS * MT, TC])
        ps_w = mem.enter_context(nc.psum_tensor("ps_w", [P, 2, TB], F32))
        ps_s = mem.enter_context(nc.psum_tensor("ps_score", [P, 2, TB], F32))
        ps_v = mem.enter_context(nc.psum_tensor("ps_v", [P, 2, TB], F32))
        ps_m = mem.enter_context(nc.psum_tensor("ps_m", [P, 2, TB], F32))
        SCALE = XA_HD ** -0.5

        loaded = [sig(f"s3_loaded{u}", 3, 16) for u in range(2)]
        x_loaded = [sig(f"s3_x_loaded{u}", 1, 16) for u in range(2)]
        names = {"fin_sq": 0, "fin1": 0, "centred": 0, "cent_sq": 0, "fin2": 0, "var_ready": 0, "var_root": 0, "mixed": 0,
                 "w_done": 2, "h1_ready": 0, "ss1": 0, "ms1_ready": 0, "root1": 0, "hn_scaled": 0, "turned0": 0, "turned1": 0,
                 "hn_out0": 0, "hn_out1": 0, "score_done": 0, "top_ready": 0, "exp_done": 0, "prob_ready": 0,
                 "p_turned0": 0, "p_turned1": 0, "p_out0": 0, "p_out1": 0, "v_done3": 0, "h2_ready": 0, "ss2": 0,
                 "ms2_ready": 0, "root2": 0, "h2_scaled": 0, "turned2": 0, "turned3": 0, "h3_out0": 0, "h3_out1": 0}
        S = {n: sig("s3_" + n, 1, 1, seed) for n, seed in names.items()}
        h2_stored, h3_stored = sig("h2_stored", 1, 16, 1), sig("h3_stored", 1, 16, 1)
        own = {n: sig("s3_own_" + n).sem for n in ("dve_fin", "dve_soft", "dve_n1", "dve_n2", "act", "sp_hold")}
        block = mem.enter_context(nc.Block())
        AG, DG, BONUS = range(3)

        def tiles(fori, parts, first):
            first()
            for p in range(2):
                parts(p, 0, p % 2, p > 0, True, True)
            with fori(0, NCH // 2 - 2) as i:
                for u in range(2):
                    parts(2 * i + 2 + u, i + 1, u, True, True, True)
            for p in (NCH - 2, NCH - 1):
                parts(p, NCH // 2 - 1, p % 2, True, p < NCH - 1, False)

        @block.sync
        def _(sp):
            for s in (h2_stored, h3_stored):
                s.seed_by(sp)

            def load(p, u):
                at = bass.ds(p, 1)
                sp.dma_start(oy[u][:], D["oy"][at].rearrange("a p k t n -> (a p) k t n")).then_inc(loaded[u].sem, 16)
                sp.dma_start(late[u][:], D["late"][at, :, 0:3].rearrange("a p k t n -> (a p) k t n")).then_inc(loaded[u].sem, 16)
                sp.dma_start(mix[u][:, G2:3 * G2].rearrange("p (k t) n -> p k t n", t=G2),
                             D["late"][at, :, 3:5].rearrange("a p k t n -> (a p) k t n")).then_inc(loaded[u].sem, 16)

            def load_x(p, u):
                sp.dma_start(x_t[u][:], D["x"][bass.ds(p * TC, TC)]).then_inc(x_loaded[u].sem, 16)

            def hold(at):
                sp.wait_ge(*at)
                sp.sem_inc(own["sp_hold"], 1)

            def store_h2(p, u):
                hold(S["h2_scaled"].at(p))
                sp.dma_start(D["h2"][bass.ds(p * TC, TC)], x_t[u][:]).then_inc(h2_stored.sem, 16)

            def parts(p, i, u, has_before, has_next, has_after):
                if has_after:
                    hold(S["w_done"].at(p))
                    load(p + 2, u)
                if has_before:
                    store_h2(p - 1, 1 - u)
                    if has_next:
                        hold(h2_stored.at(p - 1))
                        load_x(p + 1, 1 - u)
                    store_turned(p - 1)

            def store_turned(p):
                hold(S["h3_out1"].at(p))
                sp.dma_start(D["h3t"][:, :, bass.ds(p * TC, TC)].rearrange("k p n -> p k n"), h3_t[:]).then_inc(h3_stored.sem, 16)

            tiles(nc.sync.Fori, parts, lambda: [(load(p, p), load_x(p, p)) for p in range(2)])
            store_h2(NCH - 1, (NCH - 1) % 2)
            store_turned(NCH - 1)
            sp.wait_ge(*h2_stored.at(NCH - 1))
            sp.wait_ge(*h3_stored.at(NCH - 1))

        @block.tensor
        def _(pe):
            S["w_done"].seed_by(pe)

            def fin1(p, u):
                pe.wait_ge(*S["fin_sq"].at(p))
                pe.matmul(ps_m[:, 0, 0:G2 * TC], headones, sq_o[:].rearrange("p t n -> p (t n)"), start=True, stop=True)
                pe.matmul(ps_m[:, 0, G2 * TC:], headones, oy[u][:, 1].rearrange("p t n -> p (t n)"), start=True,
                          stop=True).then_inc(S["fin1"].sem, 1)

            def fin2(p, u):
                pe.wait_ge(*S["cent_sq"].at(p))
                pe.matmul(ps_m[:, 1, 0:G2 * TC], headones, sq_y[:].rearrange("p t n -> p (t n)"), start=True,
                          stop=True).then_inc(S["fin2"].sem, 1)

            def project(p, u):
                pe.wait_ge(*S["mixed"].at(p))
                for half in range(2):
                    for k in range(KT):
                        mm = pe.matmul(ps_w[:, half], mix[u][:, k], w_out[:, k, half * D_HALF:(half + 1) * D_HALF],
                                       start=k == 0, stop=k == KT - 1)
                mm.then_inc(S["w_done"].sem, 1)

            def turn(src, ready, dones, p):
                pe.wait_ge(*ready.at(p))
                for b in range(2):
                    for k in range(4):
                        mm = pe.transpose(ps_m[:, b, k * P:(k + 1) * P], src[:, (4 * b + k) * P:(4 * b + k + 1) * P], ident)
                    mm.then_inc(dones[b].sem, 1)

            def times(ps, lhs, rhs, outs, p, between=None):
                pe.wait_ge(*S[outs + "0"].at(p))
                for half in range(2):
                    for k in range(KT):
                        if half == 0 and k == KT // 2:
                            pe.wait_ge(*S[outs + "1"].at(p))
                        mm = pe.matmul(ps[:, half], lhs[:, k], rhs[:, k, half * TB:(half + 1) * TB], start=k == 0,
                                       stop=k == KT - 1)
                    if half == 0 and between:
                        between()
                return mm

            def parts(p, i, u, has_before, has_next, has_after):
                times(ps_s, hn_t, key_w, "hn_out", p, (lambda: fin2(p + 1, 1 - u)) if has_next else None)\
                    .then_inc(S["score_done"].sem, 1)
                if has_next:
                    pe.wait_ge(*S["var_ready"].at(p + 1))
                if has_before:
                    turn(h2_tok, S["h2_scaled"], (S["turned2"], S["turned3"]), p - 1)
                if has_next:
                    project(p + 1, 1 - u)
                if has_before:
                    pe.wait_ge(*S["h3_out1"].at(p - 1))
                turn(prob[:].rearrange("p h m -> p (h m)"), S["prob_ready"], (S["p_turned0"], S["p_turned1"]), p)
                times(ps_v, prob_t, val_w, "p_out", p, (lambda: fin1(p + 2, u)) if has_after else None)\
                    .then_inc(S["v_done3"].sem, 1)
                if has_next:
                    if has_after:
                        pe.wait_ge(*S["centred"].at(p + 2))
                    turn(hn_tok, S["hn_scaled"], (S["turned0"], S["turned1"]), p + 1)

            def first():
                fin1(0, 0)
                fin2(0, 0)
                pe.wait_ge(*S["var_ready"].at(0))
                fin1(1, 1)
                project(0, 0)
                pe.wait_ge(*S["centred"].at(1))
                turn(hn_tok, S["hn_scaled"], (S["turned0"], S["turned1"]), 0)

            tiles(nc.tensor.Fori, parts, first)
            turn(h2_tok, S["h2_scaled"], (S["turned2"], S["turned3"]), NCH - 1)

        @block.scalar
        def _(act):
            def fin_sq(p, u, i):
                act.wait_ge(*loaded[u].at(i))
                act.activation(sq_o[:], oy[u][:, 0], ACT.Square).then_inc(S["fin_sq"].sem, 1)

            def cent_sq(p, u):
                act.wait_ge(*S["centred"].at(p))
                act.activation(sq_y[:], oy[u][:, 1], ACT.Square).then_inc(S["cent_sq"].sem, 1)

            def var_root(p):
                act.wait_ge(*S["var_ready"].at(p))
                act.activation(head_var[:], head_var[:], ACT.Sqrt).then_inc(S["var_root"].sem, 1)

            def norm(p, u, ready, ms, ss, ms_ready, root):
                act.wait_ge(*S[ready].at(p))
                act.activation(s3_junk[:], x_t[u][:], ACT.Square, accum_out=ms[:]).then_inc(S[ss].sem, 1)
                act.wait_ge(*S[ms_ready].at(p))
                act.activation(ms[:], ms[:], ACT.Sqrt).then_inc(S[root].sem, 1)

            def norm2(p, u):
                norm(p, u, "h2_ready", ms2, "ss2", "ms2_ready", "root2")

            def parts(p, i, u, has_before, has_next, has_after):
                if has_before:
                    norm2(p - 1, 1 - u)
                if has_next:
                    var_root(p + 1)
                act.wait_ge(*S["top_ready"].at(p))
                for h in range(XA_HEADS):
                    s = ps_s[:, h // 2, h % 2 * N_MEM:(h % 2 + 1) * N_MEM]
                    last = act.activation(prob[:, h], s, ACT.Exp, bias=top[:, h:h + 1], scale=SCALE,
                                          accum_out=total[:, h:h + 1])
                last.then_inc(S["exp_done"].sem, 1)
                if has_after:
                    fin_sq(p + 2, u, i + 1)
                for b in range(2):
                    act.wait_ge(*S[f"p_turned{b}"].at(p))
                    act.activation(prob_t[:, 4 * b:4 * b + 4].rearrange("p k n -> p (k n)"), ps_m[:, b], ACT.Copy)\
                       .then_inc(S[f"p_out{b}"].sem, 1)
                if has_next:
                    norm(p + 1, 1 - u, "h1_ready", ms1, "ss1", "ms1_ready", "root1")
                if has_after:
                    cent_sq(p + 2, u)

            def first():
                fin_sq(0, 0, 0)
                cent_sq(0, 0)
                var_root(0)
                fin_sq(1, 1, 0)
                norm(0, 0, "h1_ready", ms1, "ss1", "ms1_ready", "root1")
                cent_sq(1, 1)

            tiles(nc.scalar.Fori, parts, first)
            norm2(NCH - 1, (NCH - 1) % 2)

        @block.vector
        def _(dve):
            def centre(p, u):
                dve.wait_ge(*S["fin1"].at(p))
                dve.tensor_scalar(head_var[:, 0].rearrange("p t n -> p (t n)"), ps_m[:, 0, 0:G2 * TC], 1.0 / HD, EPS, ALU.mult,
                                  ALU.add)
                y = oy[u][:, 1].rearrange("p t n -> p (t n)")
                dve.scalar_tensor_tensor(y, ps_m[:, 0, G2 * TC:], -1.0 / HD, y, ALU.mult, ALU.add).then_inc(S["centred"].sem, 1)

            def finish(p, u):
                me = Own(dve, own["dve_fin"], p, 4)
                dve.wait_ge(*S["fin2"].at(p))
                dve.tensor_scalar(head_var[:, 1].rearrange("p t n -> p (t n)"), ps_m[:, 1, 0:G2 * TC], 1.0 / HD, RW_LN_EPS,
                                  ALU.mult, ALU.add).then_inc(S["var_ready"].sem, 1)
                dve.wait_ge(*S["var_root"].at(p))
                dve.wait_ge(*S["w_done"].at(p, back=2))
                me.done(dve.reciprocal(head_var[:], head_var[:]))
                o, y = mix[u][:, 0:G2], mix[u][:, 3 * G2:]
                dve.tensor_tensor(o, oy[u][:, 0], head_var[:, 0], ALU.mult)
                me.done(dve.tensor_tensor(y, oy[u][:, 1], head_var[:, 1], ALU.mult))
                dve.tensor_tensor(o, o, late[u][:, AG], ALU.mult)
                for t in range(G2):
                    last = dve.tensor_scalar(y[:, t], y[:, t], col("rw_ln_g", t), col("rw_ln_b", t), ALU.mult, ALU.add)
                me.done(last)
                me.done(dve.tensor_tensor(y, y, late[u][:, BONUS], ALU.add))
                me.done(dve.tensor_tensor(y, y, late[u][:, DG], ALU.mult), S["mixed"])
                me.check()

            def residual(p, u, done, ps, ready):
                dve.wait_ge(*S[done].at(p))
                x = x_t[u][:]
                dve.tensor_tensor(x, x, ps[:].rearrange("p a n -> p (a n)"), ALU.add).then_inc(S[ready].sem, 1)

            def scale(p, u, name, ms, ss, ms_ready, root, dst, scaled, free):
                me = Own(dve, own[name], p, 1)
                dve.wait_ge(*S[ss].at(p))
                dve.tensor_scalar(ms[:], ms[:], 1.0 / D_MODEL, EPS, ALU.mult, ALU.add).then_inc(S[ms_ready].sem, 1)
                dve.wait_ge(*S[root].at(p))
                me.done(dve.reciprocal(ms[:], ms[:]))
                if free:
                    dve.wait_ge(*free)
                dve.tensor_scalar(dst[:], x_t[u][:], ms[:, 0:1], None, ALU.mult).then_inc(S[scaled].sem, 1)

            def turned(p, names, gain, dst, outs, free=None):
                if free:
                    dve.wait_ge(*free)
                for b in range(2):
                    dve.wait_ge(*S[names[b]].at(p))
                    g = cols(gain, KT)[:, 4 * b:4 * b + 4].rearrange("p (k n) -> p k n", n=1).broadcast_to([P, 4, TC])
                    dve.tensor_tensor(dst[:, 4 * b:4 * b + 4], ps_m[:, b].rearrange("p (k n) -> p k n", k=4), g,
                                      ALU.mult).then_inc(S[outs[b]].sem, 1)

            def n1(p, u):
                scale(p, u, "dve_n1", ms1, "ss1", "ms1_ready", "root1", hn_tok, "hn_scaled", None)

            def end(p, u):
                residual(p, u, "v_done3", ps_v, "h2_ready")
                scale(p, u, "dve_n2", ms2, "ss2", "ms2_ready", "root2", h2_tok, "h2_scaled", None)

            def parts(p, i, u, has_before, has_next, has_after):
                if has_before:
                    end(p - 1, 1 - u)
                if has_next:
                    finish(p + 1, 1 - u)
                me = Own(dve, own["dve_soft"], p, 2)
                dve.wait_ge(*S["score_done"].at(p))
                me.done(dve.tensor_reduce(top[:], ps_s[:].rearrange("p a (h m) -> p (a h) m", m=N_MEM), AX_X, ALU.max))
                dve.tensor_scalar(top[:], top[:], -SCALE, None, ALU.mult).then_inc(S["top_ready"].sem, 1)
                dve.wait_ge(*S["exp_done"].at(p))
                me.done(dve.reciprocal(total[:], total[:]))
                dve.tensor_tensor(prob[:], prob[:], total[:].rearrange("p (h m) -> p h m", m=1).broadcast_to([P, XA_HEADS, N_MEM]),
                                  ALU.mult).then_inc(S["prob_ready"].sem, 1)
                if has_before:
                    turned(p - 1, ("turned2", "turned3"), "ffn_norm", h3_t, ("h3_out0", "h3_out1"), h3_stored.at(p - 1, back=1))
                if has_next:
                    dve.wait_ge(*x_loaded[1 - u].at(i + u))
                    residual(p + 1, 1 - u, "w_done", ps_w, "h1_ready")
                    n1(p + 1, 1 - u)
                if has_after:
                    centre(p + 2, u)
                if has_next:
                    turned(p + 1, ("turned0", "turned1"), "xa_norm", hn_t, ("hn_out0", "hn_out1"))

            def first():
                centre(0, 0)
                finish(0, 0)
                centre(1, 1)
                dve.wait_ge(*x_loaded[0].at(0))
                residual(0, 0, "w_done", ps_w, "h1_ready")
                n1(0, 0)
                turned(0, ("turned0", "turned1"), "xa_norm", hn_t, ("hn_out0", "hn_out1"))

            tiles(nc.vector.Fori, parts, first)
            end(NCH - 1, (NCH - 1) % 2)
            turned(NCH - 1, ("turned2", "turned3"), "ffn_norm", h3_t, ("h3_out0", "h3_out1"), h3_stored.at(NCH - 1, back=1))


def gated_mlp(nc, ctx, D, C):
    with ExitStack() as mem:
        def sb(name, shape, dt=F32):
            return mem.enter_context(nc.sbuf_tensor(name, shape, dt))

        def sig(name, n=1, unit=1, seed=0):
            return Signal(nc.alloc_semaphore(name), n, unit, seed)

        DH = D_MODEL // 2
        PAIRS = FF_T // 2
        UP, DOWN, HN, ITEMS = 0, FF_T, 2 * FF_T, 2 * FF_T + 2
        hn = [sb(f"ffn_hn_{n}", [P, KT, TB], F32R) for n in ("high", "low")]
        h3 = sb("h3", [P, CB, D_MODEL])
        hidden = [sb(f"hidden_{n}", [P, FF_T, TB], F32R) for n in ("high", "low")]
        raw = sb("ffn_raw", [P, 2, 2, 2 + TB])
        tails = sb("tails", [P, FF_T, 2, 2])
        gate, value = sb("ffn_gate", [P, TB]), sb("ffn_value", [P, TB])
        loads = sb("w_ring_raw", [P, 2, 2 * D_MODEL])
        w = [sb(f"w_ring_{n}", [P, 2, 2 * D_MODEL], F32R) for n in ("high", "low")]
        gain = sb("final_gain", [P, D_MODEL])
        sumsq, rms = sb("ffn_sumsq", [P, CB]), sb("ffn_rms", [P, CB])
        junk = raw[:].rearrange("p a b n -> p (a b n)")[:, 0:D_MODEL]
        ps = mem.enter_context(nc.psum_tensor("ffn_ps", [P, 8, TB], F32))

        loaded = [sig(f"ring_in{u}", ITEMS // 2, 16, 1) for u in range(2)]
        high, split = sig("ring_high", ITEMS, 1, 1), sig("ring_split", ITEMS, 1, 1)
        used = sig("w_down_used", FF_T - 1, 1, 1)
        h2_in, gain_in = sig("ffn_h2_in", 1, 16), sig("gain_in", 1, 16)
        up_done, up_out = sig("up_done", 2 * FF_T, 1, 1), sig("up_out", FF_T, 1, 1)
        conv_gate, gated = sig("conv_gate", FF_T), sig("gated", FF_T)
        product, hidden_high, hidden_ready = sig("product", FF_T), sig("hidden_high", FF_T), sig("hidden_ready", FF_T, 1, 1)
        dn_done, added = sig("dn_done", 2 * CB, 1, 1), sig("added", 2 * CB, 1, 1)
        squared, ms_ready, root_ready, out_ready = sig("squared"), sig("ffn_ms"), sig("ffn_root"), sig("out_ready", CB)
        stored = sig("out_stored", CB, 16, 1)
        own_conv, own_norm, own_recip, own_act, s4_hold, own_hold_pe, own_hold_dve = (sig(n).sem for n in (
            "own_conv", "own_norm", "own_recip", "ffn_own_act", "s4_hold", "s4_hold_pe", "s4_hold_dve"))
        block = mem.enter_context(nc.Block())
        PASSES = ((0, 0), (0, 1), (1, 0))

        def blocks(fori, run):
            with fori(0, NB - 1) as p:
                run(p, True)
            run(NB - 1, False)

        def feature_tiles(fori, run):
            with fori(0, PAIRS - 1) as i:
                for u in range(2):
                    run(2 * i + u, i, u, True)
            for u in range(2):
                run(FF_T - 2 + u, PAIRS - 1, u, False)

        @block.sync
        def _(sp):
            for s in loaded:
                sp.sem_inc(s.sem, HN // 2 * 16)
            stored.seed_by(sp)

            def slot(p, j, u):
                sp.wait_ge(*split.at(p, j - 2))
                sp.sem_inc(s4_hold, 1)
                return loads[:, u]

            def load_up(p, f, u):
                dst = slot(p, UP + f, u).rearrange("p (g n) -> p g n", g=2)
                sp.dma_start(dst, D["w_up"][bass.ds(f, 1)].rearrange("a p g n -> (a p) g n")).then_inc(loaded[u].sem, 16)

            def load_hn(p, u):
                dst = slot(p - 1, HN + u, u).rearrange("p (k n) -> p k n", n=TB)
                src = D["h3t"][u * KT // 2:(u + 1) * KT // 2, :, bass.ds(p * TB, TB)]
                sp.dma_start(dst, src.rearrange("k p n -> p k n")).then_inc(loaded[u].sem, 16)

            for u in range(2):
                sp.dma_start(loads[:, u].rearrange("p (k n) -> p k n", n=TB),
                             D["h3t"][u * KT // 2:(u + 1) * KT // 2, :, 0:TB].rearrange("k p n -> p k n")).then_inc(loaded[u].sem, 16)
            sp.dma_start(gain[:], D["final_gain"]).then_inc(gain_in.sem, 16)
            for u in range(2):
                load_up(0, u, u)

            def run(p, has_next):
                sp.wait_ge(*stored.at(p, back=1))
                sp.sem_inc(s4_hold, 1)
                sp.dma_start(h3[:], D["h2"][bass.ds(p * TB, TB)].rearrange("(t p) n -> p t n", p=P)).then_inc(h2_in.sem, 16)
                with nc.sync.Fori(0, PAIRS - 1) as i:
                    for u in range(2):
                        load_up(p, 2 * i + 2 + u, u)
                for f in range(FF_T):
                    sp.dma_start(slot(p, DOWN + f, f % 2)[:, 0:D_MODEL], D["w_down"][f]).then_inc(loaded[f % 2].sem, 16)
                if has_next:
                    for u in range(2):
                        load_hn(p + 1, u)
                    for u in range(2):
                        load_up(p + 1, u, u)
                for t in range(CB):
                    sp.wait_ge(*out_ready.at(p, t))
                    sp.sem_inc(s4_hold, 1)
                    sp.dma_start(D["out"][bass.ds(p * TB + t * TC, TC)], h3[:, t]).then_inc(stored.sem, 16)

            blocks(nc.sync.Fori, run)
            sp.wait_ge(*stored.at(NB - 1))

        @block.tensor
        def _(pe):
            used.seed_by(pe)
            dn_done.seed_by(pe)
            up_done.seed_by(pe)

            def run(p, has_next):
                def up(f, i, u, more):
                    pe.wait_ge(*split.at(p, UP + f))
                    pe.wait_ge(*up_out.at(p, f - 2))
                    for g in range(2):
                        for k in range(KT):
                            for a, b in PASSES:
                                mm = pe.matmul(ps[:, 2 * u + g], w[a][:, u, g * D_MODEL + k * P:g * D_MODEL + (k + 1) * P],
                                               hn[b][:, k], start=k == a == b == 0, stop=k == KT - 1 and a == 1)
                        mm.then_inc(up_done.sem, 1)

                pe.wait_ge(*split.at(p, -1))
                pe.wait_ge(*added.at(p, back=1))
                pe.sem_inc(own_hold_pe, 1)
                feature_tiles(nc.tensor.Fori, up)
                pe.wait_ge(*up_out.at(p))
                for f in range(FF_T):
                    u = f % 2
                    pe.wait_ge(*split.at(p, DOWN + f))
                    pe.wait_ge(*hidden_ready.at(p, f))
                    for t in range(CB):
                        for c in range(2):
                            for a, b in PASSES:
                                mm = pe.matmul(ps[:, 2 * t + c], hidden[a][:, f, t * TC:(t + 1) * TC],
                                               w[b][:, u, c * DH:(c + 1) * DH], start=f == a == b == 0,
                                               stop=f == FF_T - 1 and a == 1)
                            if f == FF_T - 1:
                                mm.then_inc(dn_done.sem, 1)
                    if f < FF_T - 1:
                        mm.then_inc(used.sem, 1)

            blocks(nc.tensor.Fori, run)

        @block.scalar
        def _(act):
            act.sem_inc(high.sem, HN)
            up_out.seed_by(act)

            def take(p, index, u, dst, n):
                act.wait_ge(*loaded[u].at(p, index))
                act.activation(dst, loads[:, u, 0:n], ACT.Copy).then_inc(high.sem, 1)

            def take_up(p, f, index, u, before):
                act.wait_ge(*before)
                take(p, index, u, w[0][:, u], 2 * D_MODEL)

            def take_down(p, f):
                act.wait_ge(*(used.at(p, f - 2) if f >= 2 else up_done.at(p, 2 * (FF_T + f - 2) + 1)))
                take(p, (DOWN + f) // 2, f % 2, w[0][:, f % 2, 0:D_MODEL], D_MODEL)

            def take_hn(p, u):
                act.wait_ge(*up_done.at(p))
                take(p, HN // 2, u, hn[0][:, u * KT // 2:(u + 1) * KT // 2].rearrange("p k n -> p (k n)"), 2 * D_MODEL)

            def ahead(p, of_next):
                for u in range(2):
                    take_hn(p, u)
                take_up(of_next, 0, 0, 0, used.at(p))
                take_up(of_next, 1, 0, 1, dn_done.at(p))

            def run(p, has_next):
                own = Own(act, own_act, p, CB)

                def tile(f, i, u, more):
                    act.wait_ge(*hidden_ready.at(p, f - 2))
                    act.wait_ge(*up_done.at(p, 2 * f + 1))
                    act.activation(raw[:, u, :, 2:], ps[:, 2 * u:2 * u + 2], ACT.Copy).then_inc(up_out.sem, 1)
                    if more:
                        take_up(p, f + 2, i + 1, u, up_done.at(p, 2 * f + 1))
                    else:
                        take_down(p, f + 2 - FF_T)
                    act.wait_ge(*conv_gate.at(p, f))
                    act.activation(gate[:], gate[:], ACT.Silu).then_inc(gated.sem, 1)
                    act.wait_ge(*product.at(p, f))
                    act.activation(hidden[0][:, bass.ds(f, 1)].rearrange("p a n -> p (a n)"), gate[:],
                                   ACT.Copy).then_inc(hidden_high.sem, 1)

                feature_tiles(nc.scalar.Fori, tile)
                for f in range(2, FF_T):
                    take_down(p, f)
                if has_next:
                    ahead(p, p + 1)
                for t in range(CB):
                    act.wait_ge(*added.at(p, 2 * t + 1))
                    own.done(act.activation(junk, h3[:, t], ACT.Square, accum_out=sumsq[:, t:t + 1]))
                act.sem_inc(squared.sem, 1)
                act.wait_ge(*ms_ready.at(p))
                act.activation(rms[:], rms[:], ACT.Sqrt).then_inc(root_ready.sem, 1)
                own.check()

            ahead(-1, 0)
            blocks(nc.scalar.Fori, run)

        @block.vector
        def _(dve):
            dve.sem_inc(split.sem, HN)
            for s in (hidden_ready, added):
                s.seed_by(dve)
            start = Own(dve, own_norm)
            start.done(dve.memset(tails[:], 0.0))

            def low(p, j, dst, high_part, u, n=2 * D_MODEL):
                dve.wait_ge(*high.at(p, j))
                dve.tensor_tensor(dst, loads[:, u, 0:n], high_part, ALU.subtract).then_inc(split.sem, 1)

            def low_up(p, f, u):
                low(p, UP + f, w[1][:, u], w[0][:, u], u)

            def low_down(p, f):
                low(p, DOWN + f, w[1][:, f % 2, 0:D_MODEL], w[0][:, f % 2, 0:D_MODEL], f % 2, D_MODEL)

            def ahead(p, of_next):
                for u in range(2):
                    dst, high_part = (x[:, u * KT // 2:(u + 1) * KT // 2].rearrange("p k n -> p (k n)") for x in (hn[1], hn[0]))
                    low(p, HN + u, dst, high_part, u)
                low_up(of_next, 0, 0)

            def taps(u, g, f, dst, own, signal=None):
                src, at = raw[:, u, g], C["col_at"]
                own.done(dve.tensor_scalar(dst, src[:, 2:2 + TB], at("ffn_conv_w2", f), at("ffn_conv_b", f), ALU.mult, ALU.add))
                own.done(dve.scalar_tensor_tensor(dst, src[:, 1:1 + TB], at("ffn_conv_w1", f), dst, ALU.mult, ALU.add))
                last = dve.scalar_tensor_tensor(dst, src[:, 0:TB], at("ffn_conv_w0", f), dst, ALU.mult, ALU.add)
                if signal:
                    last.then_inc(signal.sem, 1)
                else:
                    own.done(last)

            def run(p, has_next):
                def tile(f, i, u, more):
                    own = Own(dve, own_conv, p * FF_T + f, 6)
                    dve.wait_ge(*up_out.at(p, f))
                    tail = tails[:, bass.ds(f, 1)].rearrange("p a g n -> p (a g) n")
                    dve.sem_inc(own_hold_dve, 1)
                    own.done(dve.tensor_copy(raw[:, u, :, 0:2], tail))
                    dve.sem_inc(own_hold_dve, 1)
                    dve.tensor_copy(tail, raw[:, u, :, TB:])
                    taps(u, 0, f, gate[:], own, conv_gate)
                    taps(u, 1, f + FF_T, value[:], own)
                    if more:
                        low_up(p, f + 2, u)
                    else:
                        low_down(p, f + 2 - FF_T)
                    dve.wait_ge(*gated.at(p, f))
                    dve.tensor_tensor(gate[:], gate[:], value[:], ALU.mult).then_inc(product.sem, 1)
                    dve.wait_ge(*hidden_high.at(p, f))
                    at = [x[:, bass.ds(f, 1)].rearrange("p a n -> p (a n)") for x in hidden]
                    dve.tensor_tensor(at[1], gate[:], at[0], ALU.subtract).then_inc(hidden_ready.sem, 1)
                    own.check()

                feature_tiles(nc.vector.Fori, tile)
                for f in range(2, FF_T):
                    low_down(p, f)
                if has_next:
                    ahead(p, p + 1)
                dve.wait_ge(*h2_in.at(p))
                for t in range(CB):
                    for c in range(2):
                        dve.wait_ge(*dn_done.at(p, 2 * t + c))
                        h = h3[:, t, c * DH:(c + 1) * DH]
                        dve.tensor_tensor(h, h, ps[:, 2 * t + c], ALU.add).then_inc(added.sem, 1)
                if has_next:
                    low_up(p + 1, 1, 1)
                dve.wait_ge(*squared.at(p))
                dve.tensor_scalar(rms[:], sumsq[:], 1.0 / D_MODEL, EPS, ALU.mult, ALU.add).then_inc(ms_ready.sem, 1)
                dve.wait_ge(*root_ready.at(p))
                own = Own(dve, own_recip, p, 1)
                own.done(dve.reciprocal(rms[:], rms[:]))
                dve.wait_ge(*gain_in.at(0))
                for t in range(CB):
                    dve.scalar_tensor_tensor(h3[:, t], h3[:, t], rms[:, t:t + 1], gain[:], ALU.mult, ALU.mult)\
                       .then_inc(out_ready.sem, 1)

            ahead(-1, 0)
            low_up(0, 1, 1)
            blocks(nc.vector.Fori, run)


def channels(v):
    return np.ascontiguousarray(np.asarray(v).reshape(-1, P).T)


def parameter_columns(i):
    mu = i["rw_mu"][0].reshape(-1, P)
    parts = {
        "mix_norm": channels(i["mix_norm"]), "lb_param": channels(i["lb_param"]), "hg_norm": channels(i["hg_norm"]),
        "rw_mu": np.stack([mu[c - FEATURES[3][1]] for _, c in FEATURES[:Z_TILES]], 1),
        "lru_norm": channels(i["lru_norm"]), "s5_norm": channels(i["s5_norm"]), "s5_b_glu": channels(i["s5_b_glu"]),
        "xa_norm": channels(i["xa_norm"]), "xa_mem_norm": channels(i["xa_mem_norm"]), "ffn_norm": channels(i["ffn_norm"]),
        "ffn_conv_b": channels(i["ffn_conv_b"]),
    }
    for n in ("rw_w0", "rw_a0", "rw_k_k", "rw_k_a", "rw_r_k", "rw_ln_g", "rw_ln_b", "lru_ba", "lru_bx", "lru_lam",
              "lru_conv_b"):
        parts[n] = channels(i[n])
    for tap in range(LRU_TAPS):
        parts[f"lru_conv_w{tap}"] = channels(i["lru_conv_w"][0, tap])
    for tap in range(3):
        parts[f"ffn_conv_w{tap}"] = channels(i["ffn_conv_w"][0, tap])
    at, n = {}, 0
    for name, a in parts.items():
        at[name] = n
        n += a.shape[1]
    return np.ascontiguousarray(np.concatenate(list(parts.values()), 1)), at


def constants():
    t = np.arange(P)
    heads = (t[:, None] // HD == t[None] // HD)
    reset = np.broadcast_to((np.arange(TB) % TC != 0), (P, TB))
    cst = np.concatenate([np.eye(P), heads, np.ones((P, P)), reset], 1).astype(np.float32)
    s, t = t[:, None], t[None]
    masks = [(s // (2 * b) == t // (2 * b)) & (s % (2 * b) < b) & (t % (2 * b) >= b) for b in LEVELS] + [s == t]
    pair_mask = np.stack([s < t, s <= t, s < t, s <= t], 1).astype(np.float32)
    return cst, np.concatenate([np.stack(masks, 1).astype(np.float32), pair_mask], 1)


def lay_out(i):
    a, k = {}, lambda w: w.reshape(KT, P, -1).transpose(1, 0, 2)
    w_in = i["w_in"][0]
    a["x"] = i["x"][0]
    a["w_feat"] = np.stack([k(w_in[:, c * P:(c + 1) * P]) for _, c in FEATURES])
    a["prm"], at = parameter_columns(i)
    a["cst"], a["masks"] = constants()
    lora = np.zeros((P, 6, P), np.float32)
    for m, (name, r0, r1) in enumerate((("rw_w_up", 0, 32), ("rw_a_up", 32, 64), ("rw_g_up", 64, 128))):
        lora[r0:r1, 2 * m:2 * m + 2] = i[name][0].reshape(r1 - r0, 2, P)
    a["lora"] = lora
    lru_w = np.zeros((P, 4, P), np.float32)
    for m, name in enumerate(("lru_wa", "lru_wx")):
        for g in range(4):
            r = g % 2 * HD
            lru_w[r:r + HD, 2 * m + g // 2, r:r + HD] = i[name][0, g]
    a["lru_w"] = lru_w
    stack = np.concatenate
    a["s5_raw"] = np.stack([stack([x.T, x.T]) for x in (i["s5_a_re"][0], i["s5_a_im"][0],
                                                        np.broadcast_to(i["s5_log_dt"][0][:, None], (16, HD)))], 1)
    b_re, b_im = (i[n][0].transpose(1, 0, 2) for n in ("s5_b_re", "s5_b_im"))
    c_re, c_im = (i[n][0].transpose(2, 0, 1) for n in ("s5_c_re", "s5_c_im"))
    for name, x, y in (("s5_b", b_re, b_im), ("s5_c", c_re, c_im)):
        a[name] = np.stack([stack([x, y]), stack([y, x])], 1)
    a["s5_d"] = np.tile(i["s5_d"][0].reshape(16, 16).T, (8, 1))
    half = np.arange(P)[:, None] < HD
    a["s5_sign"] = np.where(half, [[-1, 1]], [[1, -1]]).astype(np.float32)
    a["s5_corner"] = (np.arange(P)[:, None] % HD == np.arange(P)[None] % HD).astype(np.float32)
    a["s5_glu"] = i["s5_w_glu"][0].reshape(2, P, 2, P).transpose(1, 0, 2, 3)
    a["mem"] = i["mem"][0]
    wkv = i["xa_wkv"][0]
    a["wkv"] = np.stack([k(wkv[:, n:n + P]).reshape(P, -1) for n in range(0, 2 * D_MODEL, P)])
    a["wq_t"] = i["xa_wq"][0].T.reshape(KT, P, D_MODEL)
    a["wo"] = i["xa_wo"][0].reshape(KT, P, D_MODEL)
    a["w_out"] = k(i["w_out"][0])
    a["w_up"] = i["ffn_w_up"][0].reshape(KT, P, 2, FF_T, P).transpose(3, 1, 2, 0, 4).reshape(FF_T, P, 2, D_MODEL)
    a["w_down"] = i["ffn_w_down"][0].reshape(FF_T, P, D_MODEL)
    a["final_gain"] = np.broadcast_to(i["final_norm"], (P, D_MODEL))
    return {n: np.ascontiguousarray(v) for n, v in a.items()}, at


SCRATCH = {"scan": (NCH, P, len(SCAN), G2, TC), "late": (NCH, P, len(LATE), G2, TC), "va": (NCH, P, G2 * P), "cu": (NCH, P, G2 * P),
           "vd": (NCH, P, G2 * P), "oy": (NCH, P, 2, G2, TC), "h2": (SEQ, D_MODEL), "h3t": (KT, P, SEQ)}


def build(nc, D):
    with ExitStack() as ctx:
        with ExitStack() as mixers:
            C = load_constants(nc, ctx, mixers, D)
            for stage in (project_and_prepare, scan_chunks, state_space):
                with nc.cleanup_on_exit():
                    stage(nc, ctx, D, C)
        for stage in (attend_memory, gated_mlp):
            with nc.cleanup_on_exit():
                stage(nc, ctx, D, C)


def kernel(**inputs):
    import concourse.bacc as bacc
    from concourse.bass_utils import run_bass_kernel_spmd

    arrays, prm_at = lay_out({name: np.asarray(a) for name, a in inputs.items()})
    nc = bacc.Bacc("TRN2", target_bir_lowering=False, num_devices=1)
    D = {n: nc.dram_tensor("in_" + n, a.shape, F32, kind="ExternalInput").ap() for n, a in arrays.items()}
    D["prm_at"] = prm_at
    for n, shape in SCRATCH.items():
        D[n] = nc.dram_tensor("scratch_" + n, shape, F32, kind="Internal").ap()
    D["out"] = nc.dram_tensor("out", (SEQ, D_MODEL), F32, kind="ExternalOutput").ap()
    build(nc, D)
    r = run_bass_kernel_spmd(nc, [{"in_" + n: a for n, a in arrays.items()}], core_ids=[0])
    return r.results[0]["out"].reshape(1, SEQ, D_MODEL)
```
